# Optimizing a Trainium2 kernel written in Bass

```python
import math
import jax, jax.numpy as jnp
from jax import lax
import numpy as np

D_MODEL = 1024
BATCH = 1
SEQ = 128
DEPTH = 2
DEC_BATCH = 1
DEC_SEQ = 256
PAST_LEN = 128

GRID_W = 64
EPS = 1e-6
CHUNK = 128
Q_BLOCK = 128
ROPE_BASE = 10000.0
N_DIR = 2
BRANCH_W = 512

DA_HEADS = 4
DA_HD = 64
DA_WIDTH = DA_HEADS * 2 * DA_HD
MB_INNER = 512
MB_HD = 64
MB_HEADS = MB_INNER // MB_HD
MB_GROUPS = 2
MB_STATE = 64
MB_CONV = 3
MB_CONV_DIM = MB_INNER + 2 * MB_GROUPS * MB_STATE
ML_HEADS = 4
ML_DK = 64
ML_DV = 128
ML_WIDTH = ML_HEADS * ML_DV
N_EXPERTS = 16
EC_FACTOR = 2
EXPERT_FF = 1024

IN_SIZES = (DA_WIDTH, DA_WIDTH, DA_WIDTH,
            MB_INNER, MB_CONV_DIM, N_DIR * MB_HEADS,
            ML_HEADS * ML_DK, ML_HEADS * ML_DK, ML_WIDTH, ML_WIDTH, N_DIR * 2 * ML_HEADS)
IN_WIDTH = sum(IN_SIZES)

kernel_name = 'hybrid_diff_mamba2_mlstm_ecmoe_dit_step'

F32 = jnp.float32

def rmsnorm(x, g):
    xf = x.astype(F32)
    y = xf * lax.rsqrt(jnp.mean(xf * xf, axis=-1, keepdims=True) + EPS)
    return (y * g.astype(F32)).astype(x.dtype)

def flip(a):
    return jnp.flip(a, axis=1)

def split_columns(p):
    offs, o = [], 0
    for s in IN_SIZES[:-1]:
        o += s
        offs.append(o)
    return jnp.split(p, offs, axis=-1)

def apply_axial_rope(x):
    L = x.shape[1]
    t = jnp.arange(L)
    pos = jnp.stack([t // GRID_W, t % GRID_W], axis=-1).astype(F32)
    nf = DA_HD // 4
    inv = ROPE_BASE ** (-jnp.arange(nf, dtype=F32) / nf)
    ang = pos[:, :, None] * inv
    cos = jnp.cos(ang)[None, :, None, None]
    sin = jnp.sin(ang)[None, :, None, None]
    xr = x.astype(F32).reshape(x.shape[:-1] + (2, 2, nf))
    x1, x2 = xr[..., 0, :], xr[..., 1, :]
    out = jnp.stack([x1 * cos - x2 * sin, x1 * sin + x2 * cos], axis=-2)
    return out.reshape(x.shape).astype(x.dtype)

def diff_attend(q, k, v, lam):
    b, Lq, H, _, d = q.shape
    nb = Lq // Q_BLOCK
    qb = jnp.moveaxis(q.reshape(b, nb, Q_BLOCK, H, 2, d), 1, 0)
    scale = d ** -0.5

    def one_block(qblk):
        s = jnp.einsum('bqhmd,bkhmd->bhmqk', qblk, k).astype(F32) * scale
        p = jax.nn.softmax(s, axis=-1)
        p = (p[:, :, 0] - lam * p[:, :, 1]).astype(v.dtype)
        return jnp.einsum('bhqk,bkhe->bqhe', p, v)

    o = lax.map(one_block, qb)
    return jnp.moveaxis(o, 0, 1).reshape(b, Lq, H, 2 * d)

def depthwise_conv(x, w, bias):
    K = w.shape[0]
    y = lax.conv_general_dilated(x, w[:, None, :].astype(x.dtype), window_strides=(1,),
                                 padding=[((K - 1) // 2, K // 2)],
                                 dimension_numbers=('NWC', 'WIO', 'NWC'),
                                 feature_group_count=x.shape[-1])
    return y + bias.astype(x.dtype)

def ssd_scan(x, dt, A, Bm, Cm, h0):
    b, L, H, P = x.shape
    G, N = Bm.shape[2], Bm.shape[3]
    nc = L // CHUNK
    rep = H // G
    xc = x.astype(F32).reshape(b, nc, CHUNK, H, P)
    Bc = jnp.repeat(Bm.astype(F32), rep, axis=2).reshape(b, nc, CHUNK, H, N)
    Cc = jnp.repeat(Cm.astype(F32), rep, axis=2).reshape(b, nc, CHUNK, H, N)
    dtc = dt.reshape(b, nc, CHUNK, H)
    acum = jnp.cumsum(dtc * A, axis=2)
    causal = jnp.tril(jnp.ones((CHUNK, CHUNK), bool))[None, None, :, :, None]
    seg = acum[:, :, :, None, :] - acum[:, :, None, :, :]
    decay = jnp.exp(jnp.where(causal, seg, -jnp.inf))
    cb = jnp.einsum('bcihn,bcjhn->bcijh', Cc, Bc)
    y_diag = jnp.einsum('bcijh,bcjhp->bcihp', cb * decay * dtc[:, :, None, :, :], xc)
    to_end = jnp.exp(acum[:, :, -1:, :] - acum) * dtc
    states = jnp.einsum('bcjhn,bcjh,bcjhp->bchpn', Bc, to_end, xc)
    chunk_decay = jnp.exp(acum[:, :, -1, :])

    def step(h, inp):
        s, dcy = inp
        return h * dcy[:, :, None, None] + s, h

    h_final, h_start = lax.scan(step, h0.astype(F32),
                                (jnp.moveaxis(states, 1, 0), jnp.moveaxis(chunk_decay, 1, 0)))
    h_start = jnp.moveaxis(h_start, 0, 1)
    y_off = jnp.einsum('bcihn,bchpn->bcihp', Cc, h_start) * jnp.exp(acum)[..., None]
    return (y_diag + y_off).reshape(b, L, H, P), h_final

def mlstm_chunked(q, k, v, log_i, log_f, C0, n0, m0):
    b, L, H, DK = q.shape
    DV = v.shape[-1]
    nc = L // CHUNK
    qc = q.reshape(b, nc, CHUNK, H, DK)
    kc = k.reshape(b, nc, CHUNK, H, DK)
    vc = v.reshape(b, nc, CHUNK, H, DV)
    li = log_i.reshape(b, nc, CHUNK, H)
    bcum = jnp.cumsum(log_f.reshape(b, nc, CHUNK, H), axis=2)
    b_end = bcum[:, :, -1]
    w_end = b_end[:, :, None] - bcum + li

    def step(carry, inp):
        C, n, m = carry
        be, we, kj, vj = inp
        m_new = jnp.maximum(be + m, jnp.max(we, axis=1))
        s_old = jnp.exp(be + m - m_new)
        s_tok = jnp.exp(we - m_new[:, None])
        C_new = s_old[..., None, None] * C + jnp.einsum('bjh,bjhk,bjhv->bhkv', s_tok, kj, vj)
        n_new = s_old[..., None] * n + jnp.einsum('bjh,bjhk->bhk', s_tok, kj)
        return (C_new, n_new, m_new), (C, n, m)

    mv = lambda a: jnp.moveaxis(a, 1, 0)
    (Cf, nf, mf), (Cs, ns, ms) = lax.scan(
        step, (C0.astype(F32), n0.astype(F32), m0.astype(F32)),
        (mv(b_end), mv(w_end), mv(kc), mv(vc)))
    Cs, ns, ms = mv(Cs), mv(ns), mv(ms)
    causal = jnp.tril(jnp.ones((CHUNK, CHUNK), bool))[None, None, :, :, None]
    dmat = jnp.where(causal, bcum[:, :, :, None, :] - bcum[:, :, None, :, :] + li[:, :, None, :, :], -jnp.inf)
    inter = bcum + ms[:, :, None, :]
    m_t = jnp.maximum(inter, jnp.max(dmat, axis=3))
    s_intra = jnp.exp(dmat - m_t[:, :, :, None, :]) * jnp.einsum('bcihd,bcjhd->bcijh', qc, kc)
    s_inter = jnp.exp(inter - m_t)
    num = (s_inter[..., None] * jnp.einsum('bcihd,bchdv->bcihv', qc, Cs)
           + jnp.einsum('bcijh,bcjhv->bcihv', s_intra, vc))
    den = s_inter * jnp.einsum('bcihd,bchd->bcih', qc, ns) + jnp.sum(s_intra, axis=3)
    h = num / jnp.maximum(jnp.abs(den), jnp.exp(-m_t))[..., None]
    return h.reshape(b, L, H, DV), (Cf, nf, mf)

def mamba_branch(z, xbc, dt_raw, P, h0):
    b, L, _ = xbc.shape
    xbc = jax.nn.silu(depthwise_conv(xbc, P['mb_conv_w'], P['mb_conv_b']))
    xs, Bm, Cm = jnp.split(xbc, [MB_INNER, MB_INNER + MB_GROUPS * MB_STATE], axis=-1)
    xs = xs.reshape(b, L, MB_HEADS, MB_HD)
    Bm = Bm.reshape(b, L, MB_GROUPS, MB_STATE)
    Cm = Cm.reshape(b, L, MB_GROUPS, MB_STATE)
    dt = jax.nn.softplus(dt_raw.reshape(b, L, N_DIR, MB_HEADS).astype(F32) + P['mb_dt_bias'].astype(F32))
    A = -jnp.exp(P['mb_a_log'].astype(F32))
    y_f, h_f = ssd_scan(xs, dt[:, :, 0], A[0], Bm, Cm, h0[:, 0])
    y_b, h_b = ssd_scan(flip(xs), flip(dt[:, :, 1]), A[1], flip(Bm), flip(Cm), h0[:, 1])
    y = y_f + flip(y_b) + P['mb_d'].astype(F32)[:, None] * xs.astype(F32)
    y = y.reshape(b, L, MB_INNER).astype(z.dtype)
    y = rmsnorm(y * jax.nn.silu(z), P['mb_norm_g'])
    return y, jnp.stack([h_f, h_b], axis=1)

def mlstm_branch(q, k, v, o, gates, P, C0, n0, m0):
    b, L, _ = q.shape
    q = q.reshape(b, L, ML_HEADS, ML_DK).astype(F32)
    k = k.reshape(b, L, ML_HEADS, ML_DK).astype(F32) * (ML_DK ** -0.5)
    v = v.reshape(b, L, ML_HEADS, ML_DV).astype(F32)
    pre = gates.reshape(b, L, N_DIR, 2, ML_HEADS).astype(F32) + P['ml_gate_b'].astype(F32)
    log_i = pre[:, :, :, 0]
    log_f = jax.nn.log_sigmoid(pre[:, :, :, 1])
    h_f, (Cf, nf, mf) = mlstm_chunked(q, k, v, log_i[:, :, 0], log_f[:, :, 0], C0[:, 0], n0[:, 0], m0[:, 0])
    h_b, (Cb, nb, mb) = mlstm_chunked(flip(q), flip(k), flip(v), flip(log_i[:, :, 1]), flip(log_f[:, :, 1]),
                                      C0[:, 1], n0[:, 1], m0[:, 1])
    h = rmsnorm(h_f + flip(h_b), P['ml_norm_g']) * jax.nn.sigmoid(o.reshape(b, L, ML_HEADS, ML_DV).astype(F32))
    return (h.reshape(b, L, ML_WIDTH).astype(o.dtype),
            jnp.stack([Cf, Cb], axis=1), jnp.stack([nf, nb], axis=1), jnp.stack([mf, mb], axis=1))

def mixer_block(h, l, P, ctx):
    b, L, _ = h.shape
    (da_q, da_k, da_v, mb_z, mb_xbc, mb_dt,
     ml_q, ml_k, ml_v, ml_o, ml_if) = split_columns(h @ P['w_in'])
    q = da_q.reshape(b, L, DA_HEADS, 2, DA_HD)
    k = da_k.reshape(b, L, DA_HEADS, 2, DA_HD)
    v = da_v.reshape(b, L, DA_HEADS, 2 * DA_HD)
    lam_init = 0.8 - 0.6 * math.exp(-0.3 * l)
    lp = P['da_lambda'].astype(F32)
    lam = jnp.exp(jnp.sum(lp[0] * lp[1])) - jnp.exp(jnp.sum(lp[2] * lp[3])) + lam_init
    if ctx is None:
        att = diff_attend(q, k, v, lam)
        ssm0 = jnp.zeros((b, N_DIR, MB_HEADS, MB_HD, MB_STATE), F32)
        C0 = jnp.zeros((b, N_DIR, ML_HEADS, ML_DK, ML_DV), F32)
        n0 = jnp.zeros((b, N_DIR, ML_HEADS, ML_DK), F32)
        m0 = jnp.zeros((b, N_DIR, ML_HEADS), F32)
    else:
        k_ctx, v_ctx, ssm0, C0, n0, m0 = ctx
        k_all = jnp.concatenate([k_ctx.astype(k.dtype), apply_axial_rope(k)], axis=1)
        v_all = jnp.concatenate([v_ctx.astype(v.dtype), v], axis=1)
        att = diff_attend(apply_axial_rope(q), k_all, v_all, lam)
    y_da = (rmsnorm(att, P['da_subln_g']) * (1.0 - lam_init)).reshape(b, L, DA_WIDTH)
    y_mb, ssm_fin = mamba_branch(mb_z, mb_xbc, mb_dt, P, ssm0)
    y_ml, Cfin, nfin, mfin = mlstm_branch(ml_q, ml_k, ml_v, ml_o, ml_if, P, C0, n0, m0)
    gates = jax.nn.sigmoid((h @ P['w_mgate'] + P['b_mgate']).astype(F32)).reshape(b, L, 3, D_MODEL)
    branches = jnp.stack([y_da, y_mb, y_ml], axis=2)
    proj_br = jnp.einsum('blnw,nwd->blnd', branches, P['w_branch'])
    merged = jnp.sum(gates * proj_br, axis=2).astype(h.dtype)
    out = merged @ P['w_out']
    new_ctx = (k, v, ssm_fin, Cfin, nfin, mfin) if ctx is None else None
    return out, new_ctx

def expert_choice_ffn(h, router_w, w_gate, w_up, w_down):
    B_, L, D = h.shape
    T = B_ * L
    xt = h.reshape(T, D)
    aff = jax.nn.softmax((xt @ router_w).astype(F32), axis=-1)
    cap = EC_FACTOR * T // N_EXPERTS
    g, idx = lax.top_k(aff.T, cap)
    xe = xt[idx]
    hid = jax.nn.silu(jnp.einsum('ecd,edf->ecf', xe, w_gate)) * jnp.einsum('ecd,edf->ecf', xe, w_up)
    ye = jnp.einsum('ecf,efd->ecd', hid, w_down).astype(F32) * g[..., None]
    out = jnp.zeros((T, D), F32).at[idx.reshape(-1)].add(ye.reshape(-1, D))
    return out.reshape(B_, L, D).astype(h.dtype)

def trunk_layer(x, mod, l, P, ctx):
    sh1, sc1, g1, sh2, sc2, g2 = jnp.split(mod.astype(x.dtype), 6, axis=-1)
    h = rmsnorm(x, P['norm1_g']) * (1 + sc1) + sh1
    mix, new_ctx = mixer_block(h, l, P, ctx)
    x = x + g1 * mix
    h = rmsnorm(x, P['norm2_g']) * (1 + sc2) + sh2
    x = x + g2 * expert_choice_ffn(h, P['router_w'], P['ex_w_gate'], P['ex_w_up'], P['ex_w_down'])
    return x, new_ctx

def setup_inputs(seed: int = 0) -> dict:
    key = jax.random.key(seed)
    ks = iter(jax.random.split(key, 48))

    def nrm(shape, s):
        return jax.random.normal(next(ks), shape, F32) * s

    x_prompt = nrm((BATCH, SEQ, D_MODEL), 1.0)
    x_sample = nrm((DEC_BATCH, DEC_SEQ, D_MODEL), 1.0)
    cache_k = nrm((DEC_BATCH, DEPTH, PAST_LEN, DA_HEADS, 2, DA_HD), 1.0)
    cache_v = nrm((DEC_BATCH, DEPTH, PAST_LEN, DA_HEADS, 2 * DA_HD), 1.0)
    state_ssm = nrm((DEC_BATCH, DEPTH, N_DIR, MB_HEADS, MB_HD, MB_STATE), 0.5)
    state_mlstm_c = nrm((DEC_BATCH, DEPTH, N_DIR, ML_HEADS, ML_DK, ML_DV), 0.3)
    state_mlstm_n = nrm((DEC_BATCH, DEPTH, N_DIR, ML_HEADS, ML_DK), 0.3)
    state_mlstm_m = nrm((DEC_BATCH, DEPTH, N_DIR, ML_HEADS), 0.5)
    c = nrm((DEC_BATCH, D_MODEL), 1.0)
    c_ctx = nrm((D_MODEL,), 1.0)
    ada_w = nrm((DEPTH, D_MODEL, 6 * D_MODEL), 0.5 * D_MODEL ** -0.5)
    ada_b = nrm((DEPTH, 6 * D_MODEL), 0.02)
    norm1_g = 1.0 + nrm((DEPTH, D_MODEL), 0.05)
    norm2_g = 1.0 + nrm((DEPTH, D_MODEL), 0.05)
    w_in = nrm((DEPTH, D_MODEL, IN_WIDTH), D_MODEL ** -0.5)
    da_lambda = nrm((DEPTH, 4, DA_HD), 0.1)
    da_subln_g = 1.0 + nrm((DEPTH, 2 * DA_HD), 0.05)
    mb_conv_w = nrm((DEPTH, MB_CONV, MB_CONV_DIM), MB_CONV ** -0.5)
    mb_conv_b = nrm((DEPTH, MB_CONV_DIM), 0.02)
    dt0 = jnp.exp(jax.random.uniform(next(ks), (DEPTH, N_DIR, MB_HEADS), F32, math.log(1e-3), math.log(1e-1)))
    mb_dt_bias = dt0 + jnp.log(-jnp.expm1(-dt0))
    mb_a_log = jnp.log(jax.random.uniform(next(ks), (DEPTH, N_DIR, MB_HEADS), F32, 1.0, 16.0))
    mb_d = 1.0 + nrm((DEPTH, MB_HEADS), 0.05)
    mb_norm_g = 1.0 + nrm((DEPTH, MB_INNER), 0.05)
    ml_gate_b = jnp.stack([nrm((DEPTH, N_DIR, ML_HEADS), 0.1),
                           3.0 + nrm((DEPTH, N_DIR, ML_HEADS), 0.1)], axis=2)
    ml_norm_g = 1.0 + nrm((DEPTH, ML_HEADS, ML_DV), 0.05)
    w_branch = nrm((DEPTH, 3, BRANCH_W, D_MODEL), BRANCH_W ** -0.5)
    w_mgate = nrm((DEPTH, D_MODEL, 3 * D_MODEL), D_MODEL ** -0.5)
    b_mgate = nrm((DEPTH, 3 * D_MODEL), 0.02)
    w_out = nrm((DEPTH, D_MODEL, D_MODEL), D_MODEL ** -0.5)
    router_w = nrm((DEPTH, D_MODEL, N_EXPERTS), D_MODEL ** -0.5)
    ex_w_gate = nrm((DEPTH, N_EXPERTS, D_MODEL, EXPERT_FF), D_MODEL ** -0.5)
    ex_w_up = nrm((DEPTH, N_EXPERTS, D_MODEL, EXPERT_FF), D_MODEL ** -0.5)
    ex_w_down = nrm((DEPTH, N_EXPERTS, EXPERT_FF, D_MODEL), EXPERT_FF ** -0.5)
    final_g = 1.0 + nrm((D_MODEL,), 0.05)
    return {'x_prompt': x_prompt, 'x_sample': x_sample,
            'cache_k': cache_k, 'cache_v': cache_v, 'state_ssm': state_ssm,
            'state_mlstm_c': state_mlstm_c, 'state_mlstm_n': state_mlstm_n, 'state_mlstm_m': state_mlstm_m,
            'c': c, 'c_ctx': c_ctx, 'ada_w': ada_w, 'ada_b': ada_b,
            'norm1_g': norm1_g, 'norm2_g': norm2_g, 'w_in': w_in,
            'da_lambda': da_lambda, 'da_subln_g': da_subln_g,
            'mb_conv_w': mb_conv_w, 'mb_conv_b': mb_conv_b, 'mb_dt_bias': mb_dt_bias,
            'mb_a_log': mb_a_log, 'mb_d': mb_d, 'mb_norm_g': mb_norm_g,
            'ml_gate_b': ml_gate_b, 'ml_norm_g': ml_norm_g,
            'w_branch': w_branch, 'w_mgate': w_mgate, 'b_mgate': b_mgate, 'w_out': w_out,
            'router_w': router_w, 'ex_w_gate': ex_w_gate, 'ex_w_up': ex_w_up, 'ex_w_down': ex_w_down,
            'final_g': final_g}

def reference(x_prompt, x_sample, cache_k, cache_v, state_ssm, state_mlstm_c, state_mlstm_n,
              state_mlstm_m, c, c_ctx, ada_w, ada_b, norm1_g, norm2_g, w_in, da_lambda, da_subln_g,
              mb_conv_w, mb_conv_b, mb_dt_bias, mb_a_log, mb_d, mb_norm_g, ml_gate_b, ml_norm_g,
              w_branch, w_mgate, b_mgate, w_out, router_w, ex_w_gate, ex_w_up, ex_w_down, final_g):
    layers = [dict(norm1_g=norm1_g[l], norm2_g=norm2_g[l], w_in=w_in[l], da_lambda=da_lambda[l],
                   da_subln_g=da_subln_g[l], mb_conv_w=mb_conv_w[l], mb_conv_b=mb_conv_b[l],
                   mb_dt_bias=mb_dt_bias[l], mb_a_log=mb_a_log[l], mb_d=mb_d[l], mb_norm_g=mb_norm_g[l],
                   ml_gate_b=ml_gate_b[l], ml_norm_g=ml_norm_g[l], w_branch=w_branch[l],
                   w_mgate=w_mgate[l], b_mgate=b_mgate[l], w_out=w_out[l], router_w=router_w[l],
                   ex_w_gate=ex_w_gate[l], ex_w_up=ex_w_up[l], ex_w_down=ex_w_down[l])
              for l in range(DEPTH)]
    y_p = x_prompt
    ks, vs, ssms, Cs, ns, ms = [], [], [], [], [], []
    for l in range(DEPTH):
        mod = (jax.nn.silu(c_ctx) @ ada_w[l] + ada_b[l])[None, None, :]
        y_p, st = trunk_layer(y_p, mod, l, layers[l], None)
        ks.append(st[0]); vs.append(st[1]); ssms.append(st[2])
        Cs.append(st[3]); ns.append(st[4]); ms.append(st[5])
    y_s = x_sample
    for l in range(DEPTH):
        mod = (jax.nn.silu(c) @ ada_w[l] + ada_b[l])[:, None, :]
        ctx = (cache_k[:, l], cache_v[:, l], state_ssm[:, l],
               state_mlstm_c[:, l], state_mlstm_n[:, l], state_mlstm_m[:, l])
        y_s, _ = trunk_layer(y_s, mod, l, layers[l], ctx)
    y_prompt = rmsnorm(y_p, final_g)
    y_sample = rmsnorm(y_s, final_g)
    new_cache_k = jnp.stack(ks, axis=1)
    new_cache_v = jnp.stack(vs, axis=1)
    new_state_ssm = jnp.stack(ssms, axis=1)
    new_state_mlstm_c = jnp.stack(Cs, axis=1)
    new_state_mlstm_n = jnp.stack(ns, axis=1)
    new_state_mlstm_m = jnp.stack(ms, axis=1)
    return (y_prompt, y_sample, new_cache_k, new_cache_v, new_state_ssm,
            new_state_mlstm_c, new_state_mlstm_n, new_state_mlstm_m)


_drawn_inputs = setup_inputs


def setup_inputs(seed=0):
    import zlib

    import numpy as np

    out = dict(_drawn_inputs(seed))
    spreads = {}
    factors = {'state_mlstm_c': 4.3,
     'state_mlstm_n': 8.0,
     'state_mlstm_m': 8.0,
     'norm2_g': 3.23,
     'da_lambda': 8.0,
     'da_subln_g': 4.838,
     'mb_d': 7.415,
     'mb_norm_g': 4.51,
     'ml_norm_g': 7.916,
     'b_mgate': 8.0}
    for name, (base, spread) in spreads.items():
        noise = np.random.default_rng([zlib.crc32(name.encode()), seed]).standard_normal(out[name].shape)
        drawn = base * np.exp(spread * noise) if base else spread * noise
        out[name] = __import__('jax').numpy.asarray(drawn.astype(out[name].dtype))
    for name, factor in factors.items():
        out[name] = (out[name] * factor).astype(out[name].dtype)
    return out
```

```python
import math
from contextlib import ExitStack

import numpy as np
import concourse.bass as bass
from concourse import mybir

F = mybir.dt.float32
ALU = mybir.AluOpType
ACT = mybir.ActivationFunctionType
AX = mybir.AxisListType

P = 128
D = 1024
KT = D // P
DEPTH = 2
TT = 3
N = TT * P
NS = 2 * P
SEGS = ((0, 0, P), (1, P, N))
EPS = 1e-6
HEADS = 4
RING = 4
CH = 512
EXPERTS = 16
GE = 4
GROUPS = EXPERTS // GE
CAP_S, CAP_C = 32, 16
CAP = CAP_S + CAP_C
NEG = -1.0e30
XW = N + 3

Q0, K0, V0, Z0, X0, DT0, MQ0, MV0, MO0, IF0 = 0, 512, 1024, 1536, 2048, 2816, 2832, 3344, 3856, 4368
WIN = 4384

MIX_CHUNKS = (
    [("ada", c * CH) for c in range(4)]
    + [("q", Q0), ("k", K0), ("v", V0), ("z", Z0), ("x0", X0), ("x1", X0 + CH)]
    + [("ada", c * CH) for c in range(4, 12)]
    + [("gate", 0), ("branch", 0), ("gate", 1), ("branch", 1)]
    + [("mq", MQ0), ("mv", MV0), ("mo", MO0), ("if", IF0)]
    + [("gate", 2), ("branch", 2), ("gate", 3), ("branch", 3)]
    + [("gate", 4), ("branch", 4), ("gate", 5), ("branch", 5)]
    + [("out", 0), ("out", 1)]
)
EXPERT_CHUNKS = ["gate0", "up0", "gate1", "up1", "down0", "down1"]
CHUNKS = len(MIX_CHUNKS) + EXPERTS * len(EXPERT_CHUNKS)
assert len(MIX_CHUNKS) % RING == 0 and (GE * len(EXPERT_CHUNKS)) % RING == 0

STATES = [(0, 0), (0, 1), (1, 0), (2, 1)]
STARTED = [(1, 0), (2, 1), (1, 1), (2, 0)]


def schedule():
    s = [("ada", c) for c in range(4)] + [("norm", 0)]
    s += [("q", h) for h in range(HEADS)] + [("k", h) for h in range(HEADS)] + [("rope",)]
    s += [("v", t) for t in range(TT)]
    dense = [("z", t) for t in range(TT)] + [("x", j) for j in range(6)] + [("dt",)]
    dense += [("ada", c) for c in range(4, 12)]
    n = TT * HEADS
    for i in range(n + 2):
        if i < n:
            s.append(("score", i))
        if dense:
            s.append(dense.pop(0))
        if 0 <= i - 1 < n:
            s.append(("turn", i - 1))
        if dense:
            s.append(dense.pop(0))
        if 0 <= i - 2 < n:
            s.append(("value", i - 2))
            if (i - 2) % HEADS == HEADS - 1:
                s += [("att_y", (i - 2) // HEADS)]
        if i - 4 >= 0 and (i - 4) % HEADS == HEADS - 1:
            s += [("y_turn", 0, (i - 4) // HEADS)]
    s += dense
    s += [("y_turn", 0, 2)]
    s += [("merge", 0, d) for d in range(KT)]
    s += [("conv",), ("acum",)]
    for t in range(TT):
        s += [("xs_turn", t), ("b_turn", t)]
    mq = [("mq", j) for j in range(4)] + [("mv", t) for t in range(TT)] + [("mo", t) for t in range(TT)] + [("if",)]
    s += [("state", 0), ("state", 1), ("state", 2), ("state", 3)]
    for t in range(TT):
        s += [("xd", t), ("decay", t, 0), mq.pop(0), ("decay", t, 1), ("diag", t, 0), mq.pop(0), ("diag", t, 1)]
        if t:
            s += [("off", t, 0), ("off", t, 1)]
        s += [("mb_y", t), mq.pop(0), ("y_turn", 1, t)]
    s += mq
    s += [("merge", 1, d) for d in range(KT)]
    s += [("bcum",)]
    s += [("k_turn", t) for t in range(TT)]
    s += [("urow", t, d) for t in range(TT) for d in range(2)]
    s += [("stab",)]
    s += [("cstate", i) for i in range(4)]
    for t in range(TT):
        s += [("qk", t), ("erow", t, 0), ("erow", t, 1), ("num", t, 0), ("num", t, 1), ("ml_y", t), ("y_turn", 2, t)]
    s += [("merge", 2, d) for d in range(KT)]
    s += [("out", d) for d in range(KT)]
    s += [("norm", 1)]
    s += [("h_turn", t, f) for t in range(TT) for f in range(2)] + [("router",)]
    return s


def group_schedule():
    s = [("rank", j) for j in range(GE)] + [("gather", 0), ("gather", 1), ("gather", 2), ("g_turn",)]
    for j in range(GE):
        s += [("up", j, 0), ("up", j, 1), ("down", j, 0), ("down", j, 1)]
    s += [("scatter", d) for d in range(KT)]
    return s


STEPS = schedule()
GROUP_STEPS = group_schedule()
END_STEPS = [("norm", 2)]

ACT_STEPS = {"score", "att_y", "merge", "conv", "mb_y", "ml_y", "norm", "decay", "erow", "gather", "router", "up",
             "turn", "dt", "if", "stab", "acum", "y_turn", "z", "xs_turn", "b_turn", "h_turn"}
DVE_STEPS = {"ada", "norm", "rope", "v", "turn", "score", "att_y", "merge", "z", "dt", "conv", "acum", "state", "xd",
             "decay", "diag", "mb_y", "if", "bcum", "urow", "cstate", "erow", "num", "ml_y", "out", "router", "rank",
             "up", "scatter"}

BANKS = ("D0", "D1", "T0", "T1", "R0", "R1", "Y0", "Y1")


def banks_of(step, turn):
    kind = step[0]

    def rot(k):
        turn[k] += 1
        return f"{k}{turn[k] % 2}"

    if kind in ("ada", "norm", "q", "k", "v", "z", "x", "dt", "mq", "mv", "mo", "if", "out"):
        return [rot("D")]
    if kind in ("merge", "up"):
        return [rot("D"), rot("D")]
    if kind in ("turn", "y_turn", "xs_turn", "b_turn", "acum", "state", "off", "bcum", "k_turn", "cstate", "qk",
                "h_turn", "router", "g_turn"):
        return [rot("T")]
    if kind == "score":
        return ["R0", "R1"]
    if kind == "decay":
        return ["R0", "R1"]
    if kind in ("urow", "erow"):
        return [f"R{step[2]}"]
    if kind == "rank":
        return [f"R{step[1] % 2}"]
    if kind == "value":
        return [f"Y{step[1] // HEADS % 2}"] if step[1] % HEADS == 0 else []
    if kind == "diag":
        return [f"Y{step[1] % 2}"] if step[2] == 0 else []
    if kind == "num":
        return ["Y0", "Y1", rot("T")] if step[1] else ["Y0", rot("T")]
    if kind == "gather":
        return [f"Y{step[1] % 2}"]
    if kind == "down":
        return [f"Y{step[2]}"]
    if kind == "scatter":
        return [f"R{step[1] % 2}"]
    return []


def bank_uses():
    uses = {b: {"layer": [], "group": [], "end": []} for b in BANKS}
    where = {}
    turn = {"D": 0, "T": 0}
    for part, steps in (("layer", STEPS), ("group", GROUP_STEPS), ("end", END_STEPS)):
        for step in steps:
            for k, b in enumerate(banks_of(step, turn)):
                where[(part, step, k)] = (b, len(uses[b][part]))
                uses[b][part].append((step, k))
    return uses, where


BANK_USES, WHERE = bank_uses()


class Place:

    def __init__(self):
        self.layer, self.group, self.part = 0, 0, "layer"


class Use:

    def __init__(self, hw, place, step, k=0, part=None, group=None):
        part = part or ("layer" if ("layer", step, k) in WHERE and place.part != "end" else place.part)
        name, i = WHERE[(part, step, k)]
        uses = BANK_USES[name]
        per_layer = len(uses["layer"]) + GROUPS * len(uses["group"])
        n = place.layer * per_layer
        if part == "layer":
            i += 0
        elif part == "group":
            i += len(uses["layer"])
            g = place.group if group is None else group
            if isinstance(g, int):
                i += g * len(uses["group"])
            else:
                n = n + g * len(uses["group"])
        else:
            n, i = DEPTH * per_layer, i
        self.t, self.filled, self.drained = hw.banks[name], hw.filled[name], hw.drained[name]
        self.before, self.after = n + i, n + (i + 1)
        self.bank, self.order = name, (part, i)


def drains(after, before=()):
    last = {}
    for u, value, i in [(u, u.after, 1) for u in after] + [(u, u.before, 0) for u in before]:
        place = (u.order[0] != "layer", u.order[1] + i)
        if u.bank not in last or last[u.bank][0] < place:
            last[u.bank] = (place, u.drained, value)
    return [(semaphore, value) for _, semaphore, value in last.values()]


def constant_table():
    i, j = np.meshgrid(np.arange(P), np.arange(P), indexing="ij")
    parts = {
        "ident": (i == j), "tri_f": (i <= j), "tri_b": (i >= j),
        "neg_f": np.where(i <= j, 0.0, NEG), "neg_b": np.where(i >= j, 0.0, NEG),
        "ones": np.ones((P, P)), "before": (j < i), "none": np.zeros((P, P)),
    }
    t = np.arange(NS)
    pos = np.stack([t // 64, t % 64]).astype(np.float32)
    inv = (np.float32(10000.0) ** (-np.arange(16, dtype=np.float32) / np.float32(16))).astype(np.float32)
    ch = np.arange(P) % 64
    ang = pos[ch // 32] * inv[ch % 16][:, None]
    parts["cos"] = np.cos(ang)
    parts["sin"] = np.sin(ang) * np.where(ch % 32 < 16, -1.0, 1.0)[:, None]
    parts["slot_s"] = np.broadcast_to(np.arange(CAP_S), (P, CAP_S))
    parts["slot_c"] = np.broadcast_to(np.where(np.arange(CAP_S) < CAP_C, np.arange(CAP_S), -1), (P, CAP_S))
    parts["eps"] = np.full((P, 1), EPS)
    where, at = {}, 0
    for k, v in parts.items():
        where[k] = (at, at + v.shape[1])
        at += v.shape[1]
    return np.concatenate([np.asarray(v, np.float32) for v in parts.values()], axis=1), where


CONSTANTS, CONST_AT = constant_table()


def offsets(sizes):
    where, at = {}, 0
    for k, n in sizes:
        where[k] = (at, at + n)
        at += n
    return where, at


ROW_SIZES = [("dt_b", 16), ("a_log", 16), ("mb_d", 8), ("gate_b", 16), ("m0", 8), ("lam", 256), ("subln", P),
             ("mb_g", 512), ("ml_g", 512), ("lam_init", 1), ("lam_rest", 1)]
ROW_AT, ROW_N = offsets(ROW_SIZES)
COL_SIZES = [("ada_b", 48), ("n1", KT), ("n2", KT), ("b_gate", 24), ("conv_w", 18), ("conv_b", 6),
             ("router", KT * EXPERTS), ("final", KT)]
COL_AT, COL_N = offsets(COL_SIZES)



def last_uses():
    out = []
    for kind, c in MIX_CHUNKS:
        if kind == "ada":
            out.append((("ada", c // CH), 0))
        elif kind in ("gate", "branch"):
            out.append((("merge", c // 2, c % 2 * 4 + 3), int(kind == "branch")))
        elif kind == "out":
            out.append((("out", c * 4 + 3), 0))
        else:
            out.append(({"q": ("q", 3), "k": ("k", 3), "v": ("v", 2), "z": ("z", 2), "x0": ("x", 3), "x1": ("dt",),
                         "mq": ("mq", 3), "mv": ("mv", 2), "mo": ("mo", 2), "if": ("if",)}[kind], 0))
    return out


LAST_USE = last_uses()
GROUP_LAST_USE = [use for j in range(GE) for use in
                  ((("up", j, 0), 0), (("up", j, 0), 1), (("up", j, 1), 0), (("up", j, 1), 1),
                   (("down", j, 0), 0), (("down", j, 1), 0))]
GROUP_CHUNKS = len(GROUP_LAST_USE)
CHUNK_AT = {}
for _i, (_kind, _c) in enumerate(MIX_CHUNKS):
    CHUNK_AT[(_kind, _c // CH if _kind == "ada" else _c if _kind in ("gate", "branch", "out") else 0)] = _i


class Hardware:
    pass


def build(nc, A):
    ctx = ExitStack()
    with ctx:
        hw = Hardware()
        hw.banks = {b: ctx.enter_context(nc.psum_tensor(f"bank_{b}", [P, 512], F)) for b in BANKS}
        hw.filled = {b: ctx.enter_context(nc.semaphore(f"filled_{b}")) for b in BANKS}
        hw.drained = {b: ctx.enter_context(nc.semaphore(f"drained_{b}")) for b in BANKS}

        def sb(name, *shape):
            return ctx.enter_context(nc.sbuf_tensor(name, [P, *shape], F))

        def sem(name):
            return ctx.enter_context(nc.semaphore(name))

        ring = sb("ring", RING, KT * CH)
        XT, HT, MG = sb("XT", KT, N), sb("HT", KT, N), sb("MG", KT, N)
        CT = sb("CT", CONSTANTS.shape[1])
        ROWS, COLS = sb("ROWS", ROW_N), sb("COLS", COL_N)
        CSIG = sb("CSIG", KT, 2)
        MOD, AMOD = sb("MOD", 6, KT, 2), sb("AMOD", 2, KT, 2)
        RS, SG = sb("RS", N), sb("SG", 2, N)
        LAM = sb("LAM", 8)
        EB = sb("EB", 2, 2, HEADS * P)
        YTILE, YT = sb("YTILE", 2, 512), sb("YT", 4, N)
        TMP = sb("TMP", 512)
        ST4 = sb("ST4", 2, HEADS)

        def const(name):
            a, b = CONST_AT[name]
            return CT[:, a:b]

        def row(name):
            a, b = ROW_AT[name]
            return ROWS[:, a:b]

        def col(name):
            a, b = COL_AT[name]
            return COLS[:, a:b]

        ident, ones, eps = const("ident"), const("ones"), const("eps")
        TRI = (const("tri_f"), const("tri_b"))
        NEGT = (const("neg_f"), const("neg_b"))
        before_at = CONST_AT["ones"][0]

        def views(arena, sizes):
            out, at = [], 0
            for shape in sizes:
                n = math.prod(shape)
                v = arena[:, at:at + n]
                if len(shape) == 2:
                    v = v.rearrange("p (a b) -> p a b", a=shape[0])
                if len(shape) == 3:
                    v = v.rearrange("p (a b c) -> p a b c", a=shape[0], b=shape[1])
                out.append(v)
                at += n
            assert at <= arena.shape[1], (at, arena.shape)
            return out

        arena_a, arena_b = sb("arena_a", 7948), sb("arena_b", 9876)
        CVEC, = views(arena_b, [(KT, 2)])
        QT, KTT, V, VC, PR, PT, NMX, SMX, RCP = views(
            arena_a, [(HEADS, N), (HEADS, 4 * P), (TT, 512), (512,), (2, 2, N), (2, N), (2, 2), (2, 2), (2, 2)])
        ROT = PR.rearrange("p a b c -> p (a b c)")[:, 0:HEADS * NS].rearrange("p (a b) -> p a b", a=HEADS)
        MQ, MK, MKTOK, MV, MO, CS, CC, PRE, LG, UB, MARG, MEXP, HC = views(
            arena_a, [(2, N), (2, N), (TT, 2 * P), (TT, 512), (TT, 512), (2, 2, 129), (2, 2, 129),
                      (48,), (3, 24), (8, 24), (4, 24), (4, 24), (2, 256)])
        UM, PM, MS, MXX, NRR, MNEW, BC, TB = [UB[:, k, :] for k in range(8)]
        LAB, LFF, UU = [LG[:, k, :] for k in range(3)]
        Z, XB, CX, XD, XWT, HS, CB, BTK, DT3, EX3, DTV, EXPA = views(
            arena_b, [(TT, 512), (6, XW), (6, XW), (2, 512), (512,), (2, 256), (TT, 256), (TT, P),
                      (3, 48), (3, 48), (4, 48), (16,)])
        XS = XB.rearrange("p a b -> p (a b)")[:, 0:TT * 512].rearrange("p (a b) -> p a b", a=TT)
        OFF = (0, P + 1, 2 * P + 1)
        HA, DEN, QK, KW = views(arena_b, [(512,), (8,), (512,), (2 * P,)])
        H2, PO, GO, GT, XE, SGE, HID, YES, YEC, RK, AFF, AG, R3 = views(
            arena_b, [(TT, D), (TT, GE * CAP_S), (TT, GE * CAP_S), (TT, P), (KT, GE, CAP), (2, 4 * CAP), (2, KT, CAP),
                      (D,), (D,), (16,), (TT, EXPERTS), (TT, GE), (8,)])

        def tile(t):
            return slice(t * P, (t + 1) * P)

        slot_in = [sem(f"slot_in_{k}") for k in range(RING)]
        consts_in, small_in, cache_in, ssm_in, c0_in = (
            sem(x) for x in ("consts_in", "small_in", "cache_in", "ssm_in", "c0_in"))
        layer_done = sem("layer_done")
        c_sigmoid, c_ready = sem("c_sigmoid"), sem("c_ready")
        squares, rstd_ready, scaled, h_ready = sem("squares"), sem("rstd_ready"), sem("scaled"), sem("h_ready")
        lam_sums, lam_exps = sem("lam_sums"), sem("lam_exps")
        rope_done, maxes, probs_ready = sem("rope_done"), sem("maxes"), sem("probs_ready")
        y_sum, y_rstd, y_ready = sem("y_sum"), sem("y_rstd"), sem("y_ready")
        gate_sigmoid, merged = sem("gate_sigmoid"), sem("merged")
        z_sigmoid, dt_abs, dt_ln, a_exp, dta_ready = (
            sem(x) for x in ("z_sigmoid", "dt_abs", "dt_ln", "a_exp", "dta_ready"))
        conved, conv_sigmoid, conv_done = sem("conved"), sem("conv_sigmoid"), sem("conv_done")
        ac_ready, ac_exp, xd_ready, xw_ready = sem("ac_ready"), sem("ac_exp"), sem("xd_ready"), sem("xw_ready")
        e_exp, m_ready = sem("e_exp"), sem("m_ready")
        lf_abs, lf_ln, lf_ready, u_ready = sem("lf_abs"), sem("lf_ln"), sem("lf_ready"), sem("u_ready")
        stab_ready, stab_exp, kw_ready = sem("stab_ready"), sem("stab_exp"), sem("kw_ready")
        aff_exp, ag_ready, picked, hid_sigmoid = sem("aff_exp"), sem("ag_ready"), sem("picked"), sem("hid_sigmoid")
        k_out, v_out, ssm_out, c_out, m_out, y_out = (sem(x) for x in ("k_out", "v_out", "ssm_out", "c_out", "m_out", "y_out"))
        y_final = sem("y_final")

        def use(place, step, k=0, part=None, group=None):
            return Use(hw, place, step, k, part, group)

        block = ctx.enter_context(nc.Block())

        @block.sync
        def _(sp):
            here = Place()

            def load_mix(l, i):
                kind, c = MIX_CHUNKS[i]
                one = bass.ds(l, 1)
                kt, n = KT, CH
                if kind == "ada":
                    src = A["ada_w"][one, :, c:c + CH]
                elif kind == "gate":
                    src = A["w_mgate"][one, :, c * CH:(c + 1) * CH]
                elif kind == "branch":
                    kt = KT // 2
                    src = A["w_branch"][one, c // 2, :, c % 2 * CH:(c % 2 + 1) * CH]
                elif kind == "out":
                    src = A["w_out"][one, :, c * CH:(c + 1) * CH]
                else:
                    n = {"x1": MQ0 - X0 - CH, "if": 16}.get(kind, CH)
                    src = A["w_in"][one, :, c:c + n]
                sp.dma_start(ring[:, i % RING, 0:kt * n].rearrange("p (k n) -> p k n", k=kt),
                             src.rearrange("a (k p) n -> p (a k) n", p=P),
                             allow_slow_non_contiguous=True).then_inc(slot_in[i % RING], 16)

            def load_expert(l, g, i):
                j, what = i // 6, EXPERT_CHUNKS[i % 6]
                half = int(what[-1])
                src = A["ex_w_" + what[:-1]][bass.ds(l, 1), bass.ds(g * GE + j, 1), :, half * CH:(half + 1) * CH]
                sp.dma_start(ring[:, i % RING, :].rearrange("p (k n) -> p k n", k=KT),
                             src.rearrange("a e (k p) n -> p (a e k) n", p=P)).then_inc(slot_in[i % RING], 16)

            with sp.Fori(0, DEPTH) as l:
                here.layer = l
                for i in range(len(MIX_CHUNKS)):
                    if i < RING:
                        step, k = GROUP_LAST_USE[GROUP_CHUNKS - RING + i]
                        at_1 = Place()
                        at_1.layer = 0
                        last = use(at_1, step, k, "group", GROUPS - 1)
                        sp.wait_ge(last.filled, l * last.after)
                    else:
                        last = use(here, *LAST_USE[i - RING])
                        sp.wait_ge(last.filled, last.after)
                    load_mix(l, i)
                for i in range(RING):
                    last = use(here, *LAST_USE[len(MIX_CHUNKS) - RING + i])
                    sp.wait_ge(last.filled, last.after)
                    load_expert(l, 0, i)
                with sp.Fori(0, GROUPS - 1) as g:
                    for i in range(RING, GROUP_CHUNKS + RING):
                        step, k = GROUP_LAST_USE[i - RING]
                        last = use(here, step, k, "group", g)
                        sp.wait_ge(last.filled, last.after)
                        load_expert(l, g + i // GROUP_CHUNKS, i % GROUP_CHUNKS)
                for i in range(RING, GROUP_CHUNKS):
                    step, k = GROUP_LAST_USE[i - RING]
                    last = use(here, step, k, "group", GROUPS - 1)
                    sp.wait_ge(last.filled, last.after)
                    load_expert(l, GROUPS - 1, i)

        @block.gpsimd
        def _(pool):
            here = Place()
            pool.dma_start(CVEC[:, :, :], A["c_t"]).then_inc(consts_in, 16)
            pool.dma_start(CT[:, :], A["constants"]).then_inc(consts_in, 16)
            pool.dma_start(XT[:, :, :], A["x_t"]).then_inc(consts_in, 16)
            for l in range(DEPTH):
                here.layer = l
                one = slice(l, l + 1)
                if l:
                    pool.wait_ge(layer_done, l)
                pool.dma_start(COLS[:, :], A["cols"][one].rearrange("a p n -> p (a n)")).then_inc(small_in, 16)
                pool.dma_start(ROWS[:, :], A["rows"][one].to_broadcast([P, ROW_N])).then_inc(small_in, 16)
                if l:
                    pool.wait_ge(c_out, l * 16)
                    pool.wait_ge(m_out, l * 16)
                pool.dma_start(KTT[:, :, P:2 * P], A["cache_k_t"][one].rearrange("a p h t -> p (a h) t")).then_inc(cache_in, 16)
                pool.dma_start(VC[:, :], A["cache_v"][one].rearrange("a p n -> p (a n)")).then_inc(cache_in, 16)
                pool.dma_start(HS[:, :, :], A["ssm_t"][one].rearrange("a d p n -> p (a d) n")).then_inc(ssm_in, 16)
                for h in (HEADS - 2, HEADS - 1):
                    u = use(here, ("k", h))
                    pool.wait_ge(u.drained, u.after)
                pool.dma_start(A["k_out"][one].rearrange("a p h t -> p (a h) t"), KTT[:, :, 0:P]).then_inc(k_out, 16)
                u = use(here, ("v", 0))
                pool.wait_ge(u.drained, u.after)
                pool.dma_start(A["v_out"][one].rearrange("a p n -> p (a n)"), V[:, 0, :]).then_inc(v_out, 16)
                u = use(here, ("value", (TT - 1) * HEADS))
                pool.wait_ge(u.drained, u.after)
                pool.wait_ge(k_out, l * 16 + 16)
                pool.wait_ge(v_out, l * 16 + 16)
                pool.dma_start(CS[:, :, :, :], A["c_t0"][one].rearrange("a p d t n -> p (a d) t n")).then_inc(c0_in, 16)
                for i in (0, 1):
                    u = use(here, ("state", i))
                    pool.wait_ge(u.drained, u.after)
                pool.dma_start(A["ssm_out"][one].rearrange("a d p n -> p (a d) n"), HC[:, :, :]).then_inc(ssm_out, 16)
                pool.wait_ge(stab_ready, l + 1)
                pool.dma_start(A["m_out"][one], MNEW[0:1, 0:8]).then_inc(m_out, 16)
                for i in (0, 1):
                    u = use(here, ("cstate", i))
                    pool.wait_ge(u.drained, u.after)
                pool.dma_start(A["c_out"][one].rearrange("a p d t n -> p (a d) t n"), CC[:, :, :, :]).then_inc(c_out, 16)
            pool.wait_ge(y_final, KT)
            pool.dma_start(A["y_out"], HT[:, :, :]).then_inc(y_out, 16)
            pool.wait_ge(y_out, 16)
            for s in (k_out, v_out, ssm_out, c_out, m_out):
                pool.wait_ge(s, DEPTH * 16)

        @block.tensor
        def _(pe):
            here = Place()
            mm, turn = nc.tensor.matmul, nc.tensor.transpose
            row_fence = nc.tensor.drain

            def chunk(l, name, n=CH, kt=KT):
                i = CHUNK_AT[name]
                pe.wait_ge(slot_in[i % RING], 16 * (l * (CHUNKS // RING)) + 16 * (i // RING + 1))
                return ring[:, i % RING, 0:kt * n].rearrange("p (k n) -> p k n", k=kt)

            def expert_chunk(l, g, i):
                n = l * (CHUNKS // RING) + g * (GROUP_CHUNKS // RING)
                pe.wait_ge(slot_in[i % RING], n * 16 + 16 * (len(MIX_CHUNKS) // RING + i // RING + 1))
                return ring[:, i % RING, :].rearrange("p (k n) -> p k n", k=KT)

            def to_channels(u, w, c, src=HT):
                for kt in range(KT):
                    last = mm(u.t[:, 0:N], w[:, kt, c * P:(c + 1) * P], src[:, kt, :], start=kt == 0, stop=kt == KT - 1)
                last.then_inc(u.filled, 1)

            def to_tokens(u, w, t):
                for kt in range(KT):
                    last = mm(u.t[:, :], HT[:, kt, tile(t)], w[:, kt, 0:CH], start=kt == 0, stop=kt == KT - 1)
                last.then_inc(u.filled, 1)

            def spread(u, cols):
                for k, c in enumerate(cols):
                    last = turn(u.t[:, tile(k)], c.to_broadcast([P, P]), ident)
                last.then_inc(u.filled, 1)

            def norm(l, i, name):
                u = use(here, ("norm", name))
                pe.wait_ge(u.drained, u.before)
                for kt in range(KT):
                    pe.wait_ge(squares, l * (2 * KT) + (i * KT + kt + 1))
                    last = mm(u.t[:, 0:N], ones, HT[:, kt, :], start=kt == 0, stop=kt == KT - 1)
                last.then_inc(u.filled, 1)

            def mixer_step(l, step):
                kind = step[0]
                if kind == "ada":
                    c = step[1]
                    u = use(here, step)
                    w = chunk(l, ("ada", c))
                    pe.wait_ge(c_ready, 1)
                    pe.wait_ge(u.drained, u.before)
                    for j in range(4):
                        for kt in range(KT):
                            last = mm(u.t[:, 2 * j:2 * j + 2], w[:, kt, j * P:(j + 1) * P], CSIG[:, kt, :],
                                      start=kt == 0, stop=kt == KT - 1)
                    last.then_inc(u.filled, 1)
                elif kind == "norm":
                    norm(l, step[1], step[1])
                elif kind in ("q", "k", "mq"):
                    u = use(here, step)
                    w = chunk(l, (kind, 0))
                    pe.wait_ge(h_ready, l * 2 + 1)
                    pe.wait_ge(u.drained, u.before)
                    to_channels(u, w, step[1])
                elif kind in ("v", "z", "mv", "mo"):
                    u = use(here, step)
                    w = chunk(l, (kind, 0))
                    pe.wait_ge(u.drained, u.before)
                    to_tokens(u, w, step[1])
                elif kind == "x":
                    j = step[1]
                    u = use(here, step)
                    w = chunk(l, ("x0", 0)) if j < 4 else chunk(l, ("x1", 0), MQ0 - X0 - CH)
                    pe.wait_ge(u.drained, u.before)
                    to_channels(u, w, j % 4)
                elif kind in ("dt", "if"):
                    u = use(here, step)
                    w = chunk(l, ("x1", 0), MQ0 - X0 - CH)[:, :, 256:272] if kind == "dt" else chunk(l, ("if", 0), 16)
                    pe.wait_ge(u.drained, u.before)
                    for t in range(TT):
                        for kt in range(KT):
                            last = mm(u.t[:, t * 16:(t + 1) * 16], HT[:, kt, tile(t)], w[:, kt, :],
                                      start=kt == 0, stop=kt == KT - 1)
                    last.then_inc(u.filled, 1)
                elif kind == "score":
                    t, h = divmod(step[1], HEADS)
                    keys = slice(P, 4 * P) if t else slice(0, P)
                    if step[1] == 0:
                        pe.wait_ge(rope_done, l + 1)
                        pe.wait_ge(cache_in, l * 32 + 32)
                    for m in range(2):
                        u = use(here, step, m)
                        pe.wait_ge(u.drained, u.before)
                        half = slice(64 * m, 64 * m + 64)
                        mm(u.t[:, 0:keys.stop - keys.start], QT[half, h, tile(t)], KTT[half, h, keys],
                           start=True, stop=True).then_inc(u.filled, 1)
                elif kind == "turn":
                    i = step[1]
                    u = use(here, step)
                    pe.wait_ge(probs_ready, l * (TT * HEADS) + (i + 1))
                    pe.wait_ge(u.drained, u.before)
                    for b in range(3 if i // HEADS else 1):
                        last = turn(u.t[:, tile(b)], PR[:, i % 2, 0, tile(b)], ident)
                    last.then_inc(u.filled, 1)
                elif kind == "value":
                    i = step[1]
                    t, h = divmod(i, HEADS)
                    u = use(here, ("value", t * HEADS))
                    if h == 0:
                        pe.wait_ge(u.drained, u.before)
                    if i == 0:
                        for semaphore, value in drains([use(here, ("v", s)) for s in range(TT)]):
                            pe.wait_ge(semaphore, value)
                    p = use(here, ("turn", i))
                    pe.wait_ge(p.drained, p.after)
                    head = slice(h * P, (h + 1) * P)
                    vs = [VC[:, head], V[:, 1, head], V[:, 2, head]] if t else [V[:, 0, head]]
                    for b, v in enumerate(vs):
                        last = mm(u.t[:, head], PT[:, i % 2, tile(b)], v, start=b == 0, stop=b == len(vs) - 1)
                    if h == HEADS - 1:
                        last.then_inc(u.filled, 1)
                elif kind == "y_turn":
                    n, t = step[1:]
                    u = use(here, step)
                    if n == 0:
                        y = use(here, ("value", t * HEADS))
                        pe.wait_ge(y.drained, y.after)
                    else:
                        pe.wait_ge(y_ready, l * 6 + ((n - 1) * TT + t + 1))
                    pe.wait_ge(u.drained, u.before)
                    for j in range(4):
                        last = turn(u.t[:, tile(j)], YTILE[:, (n * TT + t) % 2, tile(j)], ident)
                    last.then_inc(u.filled, 1)
                elif kind == "merge":
                    n, d = step[1:]
                    gate, proj = use(here, step, 0), use(here, step, 1)
                    w = chunk(l, ("gate", 2 * n + d // 4))
                    pe.wait_ge(gate.drained, gate.before)
                    to_channels(gate, w, d % 4)
                    w = chunk(l, ("branch", 2 * n + d // 4), kt=4)
                    if d == 0:
                        for semaphore, value in drains([use(here, ("y_turn", n, t)) for t in range(TT)]):
                            pe.wait_ge(semaphore, value)
                    pe.wait_ge(proj.drained, proj.before)
                    for kt in range(4):
                        last = mm(proj.t[:, 0:N], w[:, kt, (d % 4) * P:(d % 4 + 1) * P], YT[:, kt, :],
                                  start=kt == 0, stop=kt == 3)
                    last.then_inc(proj.filled, 1)
                elif kind in ("acum", "bcum"):
                    u = use(here, step)
                    w, src = (8, DTV[:, 3, :]) if kind == "acum" else (4, LFF)
                    pe.wait_ge(*((dta_ready, l + 1) if kind == "acum" else (lf_ready, l + 1)))
                    pe.wait_ge(u.drained, u.before)
                    for x in range(2 * TT):
                        mm(u.t[:, x * w:(x + 1) * w], TRI[x % 2], src[:, x * w:(x + 1) * w], start=True, stop=True)
                    mm(u.t[:, 6 * w:12 * w], ones, src, start=True, stop=True).then_inc(u.filled, 1)
                elif kind == "xs_turn":
                    t = step[1]
                    u = use(here, step)
                    pe.wait_ge(conv_done, l * 6 + 6)
                    pe.wait_ge(u.drained, u.before)
                    for j in range(4):
                        last = turn(u.t[:, tile(j)], CX[:, j, OFF[t]:OFF[t] + P], ident)
                    last.then_inc(u.filled, 1)
                elif kind == "b_turn":
                    t = step[1]
                    u = use(here, step)
                    pe.wait_ge(u.drained, u.before)
                    at = slice(OFF[t], OFF[t] + P)
                    turn(u.t[:, 0:P], CX[:, 4, at], ident)
                    for g in range(2):
                        half = slice(64 * g, 64 * g + 64)
                        if g:
                            row_fence()
                        last = mm(u.t[:, tile(1 + g)], CX[half, 4, at], CX[half, 5, at], start=True, stop=True)
                    last.then_inc(u.filled, 1)
                elif kind == "state":
                    t, _ = STATES[step[1]]
                    u = use(here, step)
                    pe.wait_ge(xw_ready, l * 4 + (step[1] + 1))
                    turned = [use(here, ("b_turn", s)) for s in range(TT)] if step[1] == 0 else []
                    for semaphore, value in drains(turned, [u]):
                        pe.wait_ge(semaphore, value)
                    for g in range(2):
                        last = mm(u.t[64 * g:64 * g + 64, 0:256], BTK[:, t, 64 * g:64 * g + 64],
                                  XWT[:, g * 256:(g + 1) * 256], start=True, stop=True)
                    last.then_inc(u.filled, 1)
                elif kind == "decay":
                    t, g = step[1:]
                    pe.wait_ge(ac_ready, l + 1)
                    for d in range(2):
                        u = use(here, step, d)
                        pe.wait_ge(u.drained, u.before)
                        c = t * 16 + d * 8 + g * 4
                        spread(u, [DT3[:, 0, c + h:c + h + 1] for h in range(4)])
                elif kind == "diag":
                    t, g = step[1:]
                    u = use(here, ("diag", t, 0))
                    if g == 0:
                        pe.wait_ge(u.drained, u.before)
                        pe.wait_ge(xd_ready, l * TT + (t + 1))
                    pe.wait_ge(m_ready, l * 18 + ((t * 2 + g) * 2 + 2))
                    for h in range(4):
                        head = slice((g * 4 + h) * 64, (g * 4 + h) * 64 + 64)
                        for d in range(2):
                            last = mm(u.t[:, head], EB[:, g, d, tile(h)], XD[:, d, head], start=d == 0, stop=d == 1)
                    if g == 1:
                        last.then_inc(u.filled, 1)
                elif kind == "off":
                    t, d = step[1:]
                    u = use(here, step)
                    if (t, d) in ((1, 0), (2, 1)):
                        pe.wait_ge(ssm_in, l * 16 + 16)
                        state, closed = HS, []
                    else:
                        state, closed = HC, [use(here, ("state", 2 + d))]
                    for semaphore, value in drains(closed, [u]):
                        pe.wait_ge(semaphore, value)
                    for g in range(2):
                        half = slice(64 * g, 64 * g + 64)
                        if g:
                            row_fence()
                        last = mm(u.t[:, g * 256:(g + 1) * 256], CX[half, 5, OFF[t]:OFF[t] + P], state[half, d, :],
                                  start=True, stop=True)
                    last.then_inc(u.filled, 1)
                elif kind == "k_turn":
                    t = step[1]
                    u = use(here, step)
                    keys = [use(here, ("mq", j)) for j in (2, 3)] if t == 0 else []
                    for semaphore, value in drains(keys, [u]):
                        pe.wait_ge(semaphore, value)
                    for j in range(2):
                        last = turn(u.t[:, tile(j)], MK[:, j, tile(t)], ident)
                    last.then_inc(u.filled, 1)
                elif kind in ("urow", "erow"):
                    t, d = step[1:]
                    u = use(here, step)
                    pe.wait_ge(*((u_ready, l + 1) if kind == "urow" else (stab_ready, l + 1)))
                    pe.wait_ge(u.drained, u.before)
                    src = UU if kind == "urow" else NRR
                    c = t * 8 + d * 4
                    spread(u, [src[:, c + h:c + h + 1] for h in range(4)])
                elif kind == "cstate":
                    i = step[1]
                    t, d = STATES[i]
                    u = use(here, step)
                    pe.wait_ge(kw_ready, l * 4 + (i + 1))
                    values = [use(here, ("mv", s)) for s in range(TT)] if i == 0 else []
                    for semaphore, value in drains(values, [u]):
                        pe.wait_ge(semaphore, value)
                    for h in range(HEADS):
                        half, at = slice(64 * (h % 2), 64 * (h % 2) + 64), (h // 2) * 130
                        k = KW[:, h * 64:(h + 1) * 64]
                        mm(u.t[half, at:at + P], k, MV[:, t, tile(h)], start=True, stop=True)
                        last = mm(u.t[half, at + P:at + P + 1], k, ones[:, 0:1], start=True, stop=True)
                    last.then_inc(u.filled, 1)
                elif kind == "qk":
                    t = step[1]
                    u = use(here, step)
                    pe.wait_ge(u.drained, u.before)
                    for h in (0, 2, 1, 3):
                        half = slice(64 * (h % 2), 64 * (h % 2) + 64)
                        if h == 1:
                            row_fence()
                        last = mm(u.t[:, tile(h)], MK[half, h // 2, tile(t)], MQ[half, h // 2, tile(t)],
                                  start=True, stop=True)
                    last.then_inc(u.filled, 1)
                elif kind == "num":
                    t, d = step[1:]
                    num, den = use(here, step, 0), use(here, step, 2 if t else 1)
                    pe.wait_ge(m_ready, l * 18 + (12 + t * 2 + d + 1))
                    pe.wait_ge(num.drained, num.before)
                    for h in range(HEADS):
                        last = mm(num.t[:, tile(h)], EB[:, t % 2, d, tile(h)], MV[:, t, tile(h)], start=True, stop=True)
                    last.then_inc(num.filled, 1)
                    if t:
                        inter = use(here, step, 1)
                        if (t, d) in ((1, 0), (2, 1)):
                            pe.wait_ge(c0_in, l * 16 + 16)
                            state = CS
                        else:
                            s = use(here, ("cstate", 2 + d))
                            pe.wait_ge(s.drained, s.after)
                            state = CC
                        pe.wait_ge(inter.drained, inter.before)
                        for h in (0, 2, 1, 3):
                            half = slice(64 * (h % 2), 64 * (h % 2) + 64)
                            if h == 1:
                                row_fence()
                            last = mm(inter.t[:, tile(h)], MQ[half, h // 2, tile(t)], state[half, d, h // 2, 0:P],
                                      start=True, stop=True)
                        last.then_inc(inter.filled, 1)
                    pe.wait_ge(den.drained, den.before)
                    for h in range(HEADS):
                        last = mm(den.t[:, h:h + 1], EB[:, t % 2, d, tile(h)], ones[:, 0:1], start=True, stop=True)
                    if t:
                        for h in (0, 2, 1, 3):
                            half = slice(64 * (h % 2), 64 * (h % 2) + 64)
                            if h < 2:
                                row_fence()
                            last = mm(den.t[:, 4 + h:5 + h], MQ[half, h // 2, tile(t)], state[half, d, h // 2, P:P + 1],
                                      start=True, stop=True)
                    last.then_inc(den.filled, 1)
                elif kind == "out":
                    d = step[1]
                    u = use(here, step)
                    w = chunk(l, ("out", d // 4))
                    pe.wait_ge(merged, l * 16 + 16)
                    pe.wait_ge(u.drained, u.before)
                    to_channels(u, w, d % 4, MG)
                elif kind == "h_turn":
                    t, f = step[1:]
                    u = use(here, step)
                    pe.wait_ge(h_ready, l * 2 + 2)
                    pe.wait_ge(u.drained, u.before)
                    for j in range(4):
                        last = turn(u.t[:, tile(j)], HT[:, f * 4 + j, tile(t)], ident)
                    last.then_inc(u.filled, 1)
                elif kind == "router":
                    u = use(here, step)
                    rw = col("router").rearrange("p (k e) -> p k e", k=KT)
                    pe.wait_ge(u.drained, u.before)
                    for t in range(TT):
                        for kt in range(KT):
                            last = mm(u.t[:, t * EXPERTS:(t + 1) * EXPERTS], HT[:, kt, tile(t)], rw[:, kt, :],
                                      start=kt == 0, stop=kt == KT - 1)
                    last.then_inc(u.filled, 1)

            def group_step(l, g, step):
                kind = step[0]
                if kind == "rank":
                    u = use(here, step)
                    pe.wait_ge(ag_ready, l * GROUPS + g + 1)
                    pe.wait_ge(u.drained, u.before)
                    spread(u, [AG[:, t, step[1]:step[1] + 1] for t in range(TT)])
                elif kind == "gather":
                    a = step[1]
                    u = use(here, step)
                    pe.wait_ge(picked, l * (GROUPS * GE) + g * GE + GE)
                    turned = [use(here, ("h_turn", t, f)) for t in range(TT) for f in range(2)] if a == 0 else []
                    for semaphore, value in drains(turned, [u]):
                        pe.wait_ge(semaphore, value)
                    if a < 2:
                        for k in range(4):
                            for t in (1, 2):
                                last = mm(u.t[:, tile(k)], H2[:, t, tile(a * 4 + k)], PO[:, t, :],
                                          start=t == 1, stop=t == 2)
                    else:
                        slots = PO[:, 0, :].rearrange("p (e c) -> p e c", e=GE)[:, :, 0:CAP_C]
                        for k in range(KT):
                            last = mm(u.t[:, k * 64:(k + 1) * 64], H2[:, 0, tile(k)], slots, start=True, stop=True)
                    last.then_inc(u.filled, 1)
                elif kind == "g_turn":
                    u = use(here, step)
                    pe.wait_ge(u.drained, u.before)
                    for t in range(TT):
                        last = turn(u.t[:, tile(t)], GO[:, t, :], ident)
                    last.then_inc(u.filled, 1)
                elif kind == "up":
                    j, half = step[1:]
                    if j == 0 and half == 0:
                        for semaphore, value in drains([use(here, ("gather", a)) for a in range(3)]):
                            pe.wait_ge(semaphore, value)
                    for k in range(2):
                        u = use(here, step, k)
                        w = expert_chunk(l, g, j * 6 + half * 2 + k)
                        pe.wait_ge(u.drained, u.before)
                        for f in range(4):
                            for kt in range(KT):
                                last = mm(u.t[:, f * CAP:(f + 1) * CAP], w[:, kt, tile(f)], XE[:, kt, j, :],
                                          start=kt == 0, stop=kt == KT - 1)
                        last.then_inc(u.filled, 1)
                elif kind == "down":
                    j, half = step[1:]
                    u = use(here, step)
                    w = expert_chunk(l, g, j * 6 + 4 + half)
                    for semaphore, value in drains([use(here, ("up", j, x), 1) for x in range(2)], [u]):
                        pe.wait_ge(semaphore, value)
                    for f in range(KT):
                        last = mm(u.t[0:CAP, :], HID[:, j % 2, f, :], w[:, f, :], start=f == 0, stop=f == KT - 1)
                    last.then_inc(u.filled, 1)
                elif kind == "scatter":
                    d = step[1]
                    u = use(here, step)
                    if d == 0:
                        for half in range(2):
                            y = use(here, ("down", GE - 1, half))
                            pe.wait_ge(y.drained, y.after)
                        x = use(here, ("g_turn",))
                        pe.wait_ge(x.drained, x.after)
                    pe.wait_ge(u.drained, u.before)
                    mm(u.t[:, 0:P], YEC[:, tile(d)], GT[:, 0, :], start=True, stop=True)
                    mm(u.t[:, P:N], YES[:, tile(d)], GT[:, 1:3, :], start=True, stop=True).then_inc(u.filled, 1)

            pe.wait_ge(consts_in, 48)
            with pe.Fori(0, DEPTH) as l:
                here.layer, here.part = l, "layer"
                for step in STEPS:
                    mixer_step(l, step)
                with pe.Fori(0, GROUPS) as g:
                    here.group, here.part = g, "group"
                    for step in GROUP_STEPS:
                        group_step(l, g, step)
            here.part = "end"
            norm(DEPTH, 0, 2)

        @block.scalar
        def _(act):
            here = Place()
            fn = nc.scalar.activation
            fence = nc.scalar.drain

            def copy(out, in_, scale=1.0):
                return fn(out, in_, ACT.Copy, scale=scale)

            def norm(l, i, name, shift):
                if name == 1:
                    for d in (KT - 2, KT - 1):
                        x = use(here, ("out", d))
                        act.wait_ge(x.drained, x.after)
                else:
                    act.wait_ge(layer_done, l)
                for kt in range(KT):
                    fn(HT[:, kt, :], XT[:, kt, :], ACT.Square).then_inc(squares, 1)
                u = use(here, ("norm", name))
                act.wait_ge(u.filled, u.after)
                fn(RS[:, :], u.t[:, 0:N], ACT.Ln, bias=eps, scale=1.0 / D).then_inc(u.drained, 1)
                fence()
                fn(RS[:, :], RS[:, :], ACT.Exp, scale=-0.5).then_inc(rstd_ready, 1)
                if shift is None:
                    return
                for kt in range(KT):
                    for v, a, b in SEGS:
                        act.wait_ge(scaled, l * (4 * KT) + (i * 2 * KT + kt * 2 + v + 1))
                        last = fn(HT[:, kt, a:b], HT[:, kt, a:b], ACT.Identity, bias=MOD[:, shift, kt, v:v + 1])
                last.then_inc(h_ready, 1)

            def rstd(sums, width):
                fence()
                fn(sums, sums, ACT.Ln, bias=eps, scale=1.0 / width)
                fence()
                return fn(sums, sums, ACT.Exp, scale=-0.5)

            def tile_free(l, n, t):
                i = n * TT + t
                if i >= 2:
                    x = use(here, ("y_turn", (i - 2) // TT, (i - 2) % TT))
                    act.wait_ge(x.filled, x.after)

            def mixer_step(l, step):
                kind = step[0]
                if kind == "norm":
                    norm(l, step[1], step[1], 0 if step[1] == 0 else 3)
                elif kind == "q":
                    u = use(here, step)
                    if step[1] == 0:
                        act.wait_ge(c_out, l * 16)
                        act.wait_ge(m_out, l * 16)
                    act.wait_ge(u.filled, u.after)
                    copy(QT[:, step[1], :], u.t[:, 0:N], 0.125).then_inc(u.drained, 1)
                elif kind == "k":
                    u = use(here, step)
                    act.wait_ge(u.filled, u.after)
                    copy(KTT[:, step[1], 0:P], u.t[:, 0:P])
                    copy(KTT[:, step[1], 2 * P:4 * P], u.t[:, P:N]).then_inc(u.drained, 1)
                elif kind == "v":
                    u = use(here, step)
                    act.wait_ge(u.filled, u.after)
                    copy(V[:, step[1], :], u.t[:, :]).then_inc(u.drained, 1)
                    if step[1] == 0:
                        act.wait_ge(lam_sums, l + 1)
                        fn(LAM[:, 2:4], LAM[:, 0:2], ACT.Exp).then_inc(lam_exps, 1)
                elif kind == "score":
                    i = step[1]
                    nk = N if i // HEADS else P
                    for m in range(2):
                        u = use(here, step, m)
                        act.wait_ge(maxes, l * (2 * TT * HEADS) + (2 * i + m + 1))
                        fn(PR[:, i % 2, m, 0:nk], u.t[:, 0:nk], ACT.Exp, bias=NMX[:, i % 2, m:m + 1],
                           accum_out=SMX[:, i % 2, m:m + 1]).then_inc(u.drained, 1)
                elif kind == "turn":
                    i = step[1]
                    u = use(here, step)
                    nk = N if i // HEADS else P
                    act.wait_ge(u.filled, u.after)
                    copy(PT[:, i % 2, 0:nk], u.t[:, 0:nk]).then_inc(u.drained, 1)
                elif kind == "att_y":
                    t = step[1]
                    u = use(here, ("value", t * HEADS))
                    tile_free(l, 0, t)
                    act.wait_ge(u.filled, u.after)
                    for h in range(HEADS):
                        fn(YTILE[:, t % 2, tile(h)], u.t[:, tile(h)], ACT.Square, accum_out=ST4[:, 0, h:h + 1])
                    rstd(ST4[:, 0, :], P).then_inc(y_rstd, 1)
                elif kind == "y_turn":
                    n, t = step[1:]
                    if n and t == 0:
                        for d in (KT - 2, KT - 1):
                            x = use(here, ("merge", n - 1, d), 1)
                            act.wait_ge(x.filled, x.after)
                    u = use(here, step)
                    act.wait_ge(u.filled, u.after)
                    copy(YT[:, :, tile(t)], u.t[:, :].rearrange("p (j c) -> p j c", j=4)).then_inc(u.drained, 1)
                elif kind == "merge":
                    n, d = step[1:]
                    u = use(here, step, 0)
                    act.wait_ge(u.filled, u.after)
                    if d >= 2:
                        x = use(here, ("merge", n, d - 2), 1)
                    elif n:
                        x = use(here, ("merge", n - 1, KT - 2 + d), 1)
                    else:
                        x = None
                    if x is not None:
                        act.wait_ge(x.drained, x.after)
                    fn(SG[:, d % 2, :], u.t[:, 0:N], ACT.Sigmoid, bias=col("b_gate")[:, n * KT + d:n * KT + d + 1]
                       ).then_inc(u.drained, 1)
                elif kind == "z":
                    u = use(here, step)
                    act.wait_ge(u.filled, u.after)
                    fn(Z[:, step[1], :], u.t[:, :], ACT.Sigmoid).then_inc(z_sigmoid, 1)
                elif kind == "x":
                    j = step[1]
                    u = use(here, step)
                    act.wait_ge(u.filled, u.after)
                    copy(XB[:, j, 1:P + 1], u.t[:, 0:P])
                    copy(XB[:, j, P + 2:XW - 1], u.t[:, P:N]).then_inc(u.drained, 1)
                elif kind == "dt":
                    fn(EXPA[:, :], row("a_log"), ACT.Exp).then_inc(a_exp, 1)
                    act.wait_ge(dt_abs, l + 1)
                    fn(DTV[:, 1, :], DTV[:, 1, :], ACT.Exp, scale=-1.0)
                    fence()
                    fn(DTV[:, 1, :], DTV[:, 1, :], ACT.Ln, bias=1.0).then_inc(dt_ln, 1)
                elif kind == "conv":
                    for j in range(6):
                        act.wait_ge(conved, l * 6 + (j + 1))
                        fn(XB[:, j, 0:XW - 2], CX[:, j, 0:XW - 2], ACT.Sigmoid).then_inc(conv_sigmoid, 1)
                elif kind == "acum":
                    act.wait_ge(ac_ready, l + 1)
                    fn(EX3[:, :, :], DT3[:, :, :], ACT.Exp).then_inc(ac_exp, 1)
                elif kind == "xs_turn":
                    t = step[1]
                    u = use(here, step)
                    act.wait_ge(u.filled, u.after)
                    copy(XS[:, t, :], u.t[:, :]).then_inc(u.drained, 1)
                elif kind == "b_turn":
                    t = step[1]
                    u = use(here, step)
                    act.wait_ge(u.filled, u.after)
                    copy(BTK[:, t, :], u.t[:, 0:P])
                    copy(CB[:, t, :], u.t[:, P:N]).then_inc(u.drained, 1)
                elif kind == "decay":
                    t, g = step[1:]
                    for d in range(2):
                        u = use(here, step, d)
                        act.wait_ge(u.drained, u.after)
                        fn(EB[:, g, d, :], EB[:, g, d, :], ACT.Exp).then_inc(e_exp, 1)
                elif kind in ("mb_y", "ml_y"):
                    t = step[1]
                    n, parts = (1, 1) if kind == "mb_y" else (2, HEADS)
                    i = n * TT + t
                    tile_free(l, n, t)
                    act.wait_ge(y_sum, l * 6 + (i - TT + 1))
                    w = 512 // parts
                    for h in range(parts):
                        fn(YTILE[:, i % 2, h * w:(h + 1) * w], TMP[:, h * w:(h + 1) * w], ACT.Square,
                           accum_out=ST4[:, 0, h:h + 1])
                    rstd(ST4[:, 0, 0:parts], w).then_inc(y_rstd, 1)
                elif kind == "mq":
                    j = step[1]
                    u = use(here, step)
                    if j == 0:
                        act.wait_ge(k_out, l * 16 + 16)
                        act.wait_ge(v_out, l * 16 + 16)
                    act.wait_ge(u.filled, u.after)
                    if j < 2:
                        copy(MQ[:, j, :], u.t[:, 0:N]).then_inc(u.drained, 1)
                    else:
                        copy(MK[:, j - 2, :], u.t[:, 0:N], 0.125).then_inc(u.drained, 1)
                elif kind == "mv":
                    u = use(here, step)
                    act.wait_ge(u.filled, u.after)
                    copy(MV[:, step[1], :], u.t[:, :]).then_inc(u.drained, 1)
                elif kind == "mo":
                    u = use(here, step)
                    act.wait_ge(u.filled, u.after)
                    fn(MO[:, step[1], :], u.t[:, :], ACT.Sigmoid).then_inc(u.drained, 1)
                elif kind == "if":
                    act.wait_ge(lf_abs, l + 1)
                    fn(LAB, LAB, ACT.Exp, scale=-1.0)
                    fence()
                    fn(LAB, LAB, ACT.Ln, bias=1.0).then_inc(lf_ln, 1)
                elif kind == "k_turn":
                    t = step[1]
                    u = use(here, step)
                    act.wait_ge(u.filled, u.after)
                    copy(MKTOK[:, t, :], u.t[:, 0:2 * P]).then_inc(u.drained, 1)
                elif kind == "stab":
                    act.wait_ge(stab_ready, l + 1)
                    fn(MEXP[:, :, :], MARG[:, :, :], ACT.Exp).then_inc(stab_exp, 1)
                elif kind == "qk":
                    t = step[1]
                    u = use(here, step)
                    act.wait_ge(u.filled, u.after)
                    if t:
                        act.wait_ge(m_ready, l * 18 + (12 + 2 * t))
                    copy(QK, u.t[:, :]).then_inc(u.drained, 1)
                elif kind == "erow":
                    t, d = step[1:]
                    u = use(here, step)
                    act.wait_ge(u.drained, u.after)
                    fn(EB[:, t % 2, d, :], EB[:, t % 2, d, :], ACT.Exp, scale=-1.0).then_inc(e_exp, 1)
                elif kind == "h_turn":
                    t, f = step[1:]
                    u = use(here, step)
                    if t == 0 and f == 0:
                        act.wait_ge(ssm_out, l * 16 + 16)
                    act.wait_ge(u.filled, u.after)
                    copy(H2[:, t, f * 512:(f + 1) * 512], u.t[:, :]).then_inc(u.drained, 1)
                elif kind == "router":
                    u = use(here, step)
                    act.wait_ge(u.drained, u.after)
                    fn(AFF[:, :, :], AFF[:, :, :], ACT.Exp).then_inc(aff_exp, 1)

            def group_step(l, g, step):
                kind = step[0]
                if kind == "gather":
                    a = step[1]
                    u = use(here, step)
                    act.wait_ge(u.filled, u.after)
                    if a < 2:
                        for k in range(4):
                            last = copy(XE[:, a * 4 + k, :, 0:CAP_S],
                                        u.t[:, tile(k)].rearrange("p (e c) -> p e c", e=GE))
                    else:
                        last = copy(XE[:, :, :, CAP_S:CAP].rearrange("p k e c -> p (k e) c"),
                                    u.t[:, :].rearrange("p (x c) -> p x c", c=CAP_C))
                    last.then_inc(u.drained, 1)
                elif kind == "g_turn":
                    u = use(here, step)
                    act.wait_ge(u.filled, u.after)
                    copy(GT[:, :, :], u.t[:, 0:N].rearrange("p (t c) -> p t c", t=TT)).then_inc(u.drained, 1)
                elif kind == "up":
                    j, half = step[1:]
                    u = use(here, step, 0)
                    act.wait_ge(u.filled, u.after)
                    fn(SGE[:, half, :], u.t[:, 0:4 * CAP], ACT.Sigmoid).then_inc(hid_sigmoid, 1)
                elif kind == "down":
                    j, half = step[1:]
                    u = use(here, step)
                    act.wait_ge(u.filled, u.after)
                    at = slice(half * 512, half * 512 + 512)
                    copy(YES[32 * j:32 * j + CAP_S, at], u.t[0:CAP_S, :])
                    copy(YEC[32 * j:32 * j + CAP_C, at], u.t[CAP_S:CAP, :]).then_inc(u.drained, 1)

            act.wait_ge(consts_in, 48)
            fn(CSIG[:, :, :], CVEC[:, :, :], ACT.Sigmoid).then_inc(c_sigmoid, 1)
            with act.Fori(0, DEPTH) as l:
                here.layer, here.part = l, "layer"
                act.wait_ge(small_in, l * 32 + 32)
                for step in STEPS:
                    mixer_step(l, step)
                    if step[0] in ACT_STEPS:
                        fence()
                with act.Fori(0, GROUPS) as g:
                    here.group, here.part = g, "group"
                    for step in GROUP_STEPS:
                        group_step(l, g, step)
                        if step[0] in ACT_STEPS:
                            fence()
            here.part = "end"
            norm(DEPTH, 0, 2, None)

        @block.vector
        def _(dve):
            here = Place()
            ve = nc.vector
            tt, ts, stt = ve.tensor_tensor, ve.tensor_scalar, ve.scalar_tensor_tensor
            fence = ve.drain

            def over(ap, n):
                return ap.unsqueeze(2).to_broadcast([ap.shape[0], ap.shape[1], n])

            def norm(l, i, name, scale):
                dve.wait_ge(rstd_ready, l * 2 + (i + 1))
                for kt in range(KT):
                    if scale is None:
                        stt(HT[:, kt, :], XT[:, kt, :], col("final")[:, kt:kt + 1], RS[:, :], ALU.mult,
                            ALU.mult).then_inc(y_final, 1)
                        continue
                    for v, a, b in SEGS:
                        stt(HT[:, kt, a:b], XT[:, kt, a:b], AMOD[:, scale, kt, v:v + 1], RS[:, a:b], ALU.mult,
                            ALU.mult).then_inc(scaled, 1)

            def rotate(x, rot):
                cos = const("cos").unsqueeze(1).to_broadcast([P, HEADS, NS])
                sin = const("sin").unsqueeze(1).to_broadcast([P, HEADS, NS])
                ve.stream_shuffle(rot, x, [(k + 16) % 32 for k in range(32)])
                fence()
                tt(x, x, cos, ALU.mult)
                tt(rot, rot, sin, ALU.mult)
                fence()
                return tt(x, x, rot, ALU.add)

            def mixer_step(l, step):
                kind = step[0]
                if kind == "ada":
                    c = step[1]
                    u = use(here, step)
                    dve.wait_ge(u.filled, u.after)
                    half = c % 2 * 4
                    tt(MOD[:, c // 2, half:half + 4, :], u.t[:, 0:8].rearrange("p (j v) -> p j v", v=2),
                       over(col("ada_b")[:, c * 4:c * 4 + 4], 2), ALU.add).then_inc(u.drained, 1)
                    if c in (3, 9):
                        i = c // 6
                        fence()
                        stt(AMOD[:, i, :, :], MOD[:, c // 2, :, :], 1.0, over(col("n2" if i else "n1"), 2), ALU.add, ALU.mult)
                        fence()
                elif kind == "norm":
                    norm(l, step[1], step[1], step[1])
                elif kind == "rope":
                    for name in ("q", "k"):
                        for h in (HEADS - 2, HEADS - 1):
                            x = use(here, (name, h))
                            dve.wait_ge(x.drained, x.after)
                    lam = row("lam").rearrange("p (a b) -> p a b", a=4)
                    tt(TMP[:, 0:128].rearrange("p (a b) -> p a b", a=2), lam[:, 0:4:2, :], lam[:, 1:4:2, :], ALU.mult)
                    fence()
                    ve.tensor_reduce(LAM[:, 0:2], TMP[:, 0:128].rearrange("p (a b) -> p a b", a=2), AX.X,
                                     ALU.add).then_inc(lam_sums, 1)
                    ts(row("subln"), row("subln"), row("lam_rest"), None, ALU.mult)
                    rotate(QT[:, :, P:N], ROT)
                    fence()
                    rotate(KTT[:, :, 2 * P:4 * P], ROT).then_inc(rope_done, 1)
                elif kind == "v" and step[1] == TT - 1:
                    dve.wait_ge(lam_exps, l + 1)
                    tt(LAM[:, 4:5], LAM[:, 3:4], LAM[:, 2:3], ALU.subtract)
                    fence()
                    ts(LAM[:, 5:6], LAM[:, 4:5], row("lam_init"), None, ALU.subtract)
                elif kind == "score":
                    i = step[1]
                    nk = N if i // HEADS else P
                    for m in range(2):
                        u = use(here, step, m)
                        dve.wait_ge(u.filled, u.after)
                        ve.tensor_reduce(NMX[:, i % 2, m:m + 1], u.t[:, 0:nk], AX.X, ALU.max,
                                         negate=True).then_inc(maxes, 1)
                elif kind == "turn":
                    i = step[1]
                    nk = N if i // HEADS else P
                    for m in range(2):
                        s = use(here, ("score", i), m)
                        dve.wait_ge(s.drained, s.after)
                    ve.reciprocal(RCP[:, i % 2, :], SMX[:, i % 2, :])
                    fence()
                    ts(RCP[:, i % 2, 1:2], RCP[:, i % 2, 1:2], LAM[:, 5:6], None, ALU.mult)
                    ts(PR[:, i % 2, 0, 0:nk], PR[:, i % 2, 0, 0:nk], RCP[:, i % 2, 0:1], None, ALU.mult)
                    fence()
                    stt(PR[:, i % 2, 0, 0:nk], PR[:, i % 2, 1, 0:nk], RCP[:, i % 2, 1:2], PR[:, i % 2, 0, 0:nk],
                        ALU.mult, ALU.add).then_inc(probs_ready, 1)
                elif kind == "att_y":
                    t = step[1]
                    u = use(here, ("value", t * HEADS))
                    dve.wait_ge(y_rstd, l * 9 + (t + 1))
                    for h in range(HEADS):
                        last = stt(YTILE[:, t % 2, tile(h)], u.t[:, tile(h)], ST4[:, 0, h:h + 1], row("subln"),
                                   ALU.mult, ALU.mult)
                    last.then_inc(u.drained, 1)
                elif kind == "merge":
                    n, d = step[1:]
                    gate, u = use(here, step, 0), use(here, step, 1)
                    dve.wait_ge(gate.drained, gate.after)
                    dve.wait_ge(u.filled, u.after)
                    if n == 0:
                        tt(MG[:, d, :], SG[:, d % 2, :], u.t[:, 0:N], ALU.mult).then_inc(u.drained, 1)
                    else:
                        tt(TMP[:, 0:N], SG[:, d % 2, :], u.t[:, 0:N], ALU.mult).then_inc(u.drained, 1)
                        fence()
                        tt(MG[:, d, :], MG[:, d, :], TMP[:, 0:N], ALU.add).then_inc(merged, 1)
                elif kind == "z":
                    t = step[1]
                    u = use(here, step)
                    dve.wait_ge(z_sigmoid, l * TT + (t + 1))
                    tt(Z[:, t, :], Z[:, t, :], u.t[:, :], ALU.mult).then_inc(u.drained, 1)
                elif kind == "dt":
                    u = use(here, step)
                    dve.wait_ge(u.filled, u.after)
                    tt(DTV[:, 0, :].rearrange("p (t c) -> p t c", t=TT), u.t[:, 0:48].rearrange("p (t c) -> p t c", t=TT),
                       row("dt_b").unsqueeze(1).to_broadcast([P, TT, 16]), ALU.add).then_inc(u.drained, 1)
                    fence()
                    stt(DTV[:, 1, :], DTV[:, 0, :], -1.0, DTV[:, 0, :], ALU.mult, ALU.max).then_inc(dt_abs, 1)
                elif kind == "conv":
                    dve.wait_ge(dt_ln, l + 1)
                    stt(DTV[:, 2, :], DTV[:, 0, :], 0.0, DTV[:, 1, :], ALU.max, ALU.add)
                    fence()
                    dve.wait_ge(a_exp, l + 1)
                    stt(DTV[:, 3, :].rearrange("p (t c) -> p t c", t=TT), DTV[:, 2, :].rearrange("p (t c) -> p t c", t=TT),
                        -1.0, EXPA.unsqueeze(1).to_broadcast([P, TT, 16]), ALU.mult, ALU.mult).then_inc(dta_ready, 1)
                    for x in (4, 5):
                        v = use(here, ("x", x))
                        dve.wait_ge(v.drained, v.after)
                    for c in (0, P + 1, XW - 1):
                        ve.memset(XB[:, :, c:c + 1], 0.0)
                    fence()
                    w = col("conv_w").rearrange("p (k j) -> p k j", k=3)
                    n = XW - 2
                    for j in range(6):
                        ts(CX[:, j, 0:n], XB[:, j, 1:1 + n], w[:, 1, j:j + 1], col("conv_b")[:, j:j + 1], ALU.mult, ALU.add)
                    fence()
                    for j in range(6):
                        stt(CX[:, j, 0:n], XB[:, j, 0:n], w[:, 0, j:j + 1], CX[:, j, 0:n], ALU.mult, ALU.add)
                    fence()
                    for j in range(6):
                        stt(CX[:, j, 0:n], XB[:, j, 2:2 + n], w[:, 2, j:j + 1], CX[:, j, 0:n], ALU.mult,
                            ALU.add).then_inc(conved, 1)
                    fence()
                    for j in range(6):
                        dve.wait_ge(conv_sigmoid, l * 6 + (j + 1))
                        tt(CX[:, j, 0:n], CX[:, j, 0:n], XB[:, j, 0:n], ALU.mult).then_inc(conv_done, 1)
                elif kind == "acum":
                    u = use(here, step)
                    dve.wait_ge(u.filled, u.after)
                    ve.tensor_copy(DT3[:, 0, :], u.t[:, 0:48])
                    ve.tensor_copy(DT3[:, 2, :], u.t[:, 48:96]).then_inc(u.drained, 1)
                    fence()
                    tt(DT3[:, 1, :], DT3[:, 2, :], DT3[:, 0, :], ALU.subtract).then_inc(ac_ready, 1)
                    dve.wait_ge(ac_exp, l + 1)
                    tt(DTV[:, 1, :], DTV[:, 2, :], EX3[:, 1, :], ALU.mult)
                    fence()
                elif kind == "state":
                    i = step[1]
                    t, d = STATES[i]
                    x = use(here, ("xs_turn", t))
                    dve.wait_ge(x.drained, x.after)
                    c = t * 16 + d * 8
                    tt(XWT.rearrange("p (h c) -> p h c", h=8), XS[:, t, :].rearrange("p (h c) -> p h c", h=8),
                       over(DTV[:, 1, c:c + 8], 64), ALU.mult).then_inc(xw_ready, 1)
                    u = use(here, step)
                    if i >= 2:
                        dve.wait_ge(ssm_out, l * 16 + 16)
                        dve.wait_ge(ssm_in, l * 16 + 16)
                        for g in range(2):
                            half = slice(64 * g, 64 * g + 64)
                            tt(HC[half, d, :].rearrange("p (h c) -> p h c", h=4),
                               HS[half, d, :].rearrange("p (h c) -> p h c", h=4),
                               over(EX3[half, 2, c + 4 * g:c + 4 * g + 4], 64), ALU.mult)
                        fence()
                        dve.wait_ge(u.filled, u.after)
                        tt(HC[:, d, :], HC[:, d, :], u.t[:, 0:256], ALU.add).then_inc(u.drained, 1)
                    else:
                        dve.wait_ge(u.filled, u.after)
                        ve.tensor_copy(HC[:, d, :], u.t[:, 0:256]).then_inc(u.drained, 1)
                elif kind == "xd":
                    t = step[1]
                    for d in range(2):
                        last = tt(XD[:, d, :].rearrange("p (h c) -> p h c", h=8), XS[:, t, :].rearrange("p (h c) -> p h c", h=8),
                                  over(DTV[:, 2, t * 16 + d * 8:t * 16 + d * 8 + 8], 64), ALU.mult)
                    last.then_inc(xd_ready, 1)
                elif kind == "decay":
                    t, g = step[1:]
                    for d in range(2):
                        u = use(here, step, d)
                        dve.wait_ge(u.filled, u.after)
                        for h in range(4):
                            c = t * 16 + d * 8 + g * 4 + h
                            last = stt(EB[:, g, d, tile(h)], u.t[:, tile(h)], DT3[:, 0, c:c + 1], NEGT[d],
                                       ALU.subtract, ALU.add)
                        last.then_inc(u.drained, 1)
                elif kind == "diag":
                    t, g = step[1:]
                    for d in range(2):
                        dve.wait_ge(e_exp, l * 18 + ((t * 2 + g) * 2 + d + 1))
                        e = EB[:, g, d, :].rearrange("p (h c) -> p h c", h=4)
                        tt(e, e, CB[:, t, tile(g)].unsqueeze(1).to_broadcast([P, 4, P]), ALU.mult).then_inc(m_ready, 1)
                elif kind == "mb_y":
                    t = step[1]
                    u = use(here, ("diag", t, 0))
                    tt(TMP[:, :].rearrange("p (h c) -> p h c", h=8), XS[:, t, :].rearrange("p (h c) -> p h c", h=8),
                       over(row("mb_d"), 64), ALU.mult)
                    fence()
                    dve.wait_ge(u.filled, u.after)
                    tt(TMP[:, :], TMP[:, :], u.t[:, :], ALU.add).then_inc(u.drained, 1)
                    for d in range(2 if t else 0):
                        o = use(here, ("off", t, d))
                        dve.wait_ge(o.filled, o.after)
                        tt(XWT.rearrange("p (h c) -> p h c", h=8), o.t[:, :].rearrange("p (h c) -> p h c", h=8),
                           over(EX3[:, 0, t * 16 + d * 8:t * 16 + d * 8 + 8], 64), ALU.mult).then_inc(o.drained, 1)
                        fence()
                        tt(TMP[:, :], TMP[:, :], XWT, ALU.add)
                        fence()
                    fence()
                    tt(TMP[:, :], TMP[:, :], Z[:, t, :], ALU.mult).then_inc(y_sum, 1)
                    dve.wait_ge(y_rstd, l * 9 + (TT + t + 1))
                    stt(YTILE[:, (TT + t) % 2, :], TMP[:, :], ST4[:, 0, 0:1], row("mb_g"), ALU.mult,
                        ALU.mult).then_inc(y_ready, 1)
                    fence()
                elif kind == "if":
                    u = use(here, step)
                    dve.wait_ge(u.filled, u.after)
                    tt(PRE.rearrange("p (t c) -> p t c", t=TT), u.t[:, 0:48].rearrange("p (t c) -> p t c", t=TT),
                       row("gate_b").unsqueeze(1).to_broadcast([P, TT, 16]), ALU.add).then_inc(u.drained, 1)
                    fence()
                    f = PRE.rearrange("p (x k h) -> p k x h", k=2, h=4)[:, 1, :, :]
                    stt(LAB.rearrange("p (x h) -> p x h", h=4), f, -1.0, f, ALU.mult, ALU.max).then_inc(lf_abs, 1)
                elif kind == "bcum":
                    f = PRE.rearrange("p (x k h) -> p k x h", k=2, h=4)[:, 1, :, :]
                    i_ = PRE.rearrange("p (x k h) -> p k x h", k=2, h=4)[:, 0, :, :]
                    dve.wait_ge(lf_ln, l + 1)
                    stt(LFF.rearrange("p (x h) -> p x h", h=4), f, 0.0, LAB.rearrange("p (x h) -> p x h", h=4), ALU.min,
                        ALU.subtract).then_inc(lf_ready, 1)
                    u = use(here, step)
                    dve.wait_ge(u.filled, u.after)
                    ve.tensor_copy(BC, u.t[:, 0:24])
                    ve.tensor_copy(TB, u.t[:, 24:48]).then_inc(u.drained, 1)
                    fence()
                    tt(UU.rearrange("p (x h) -> p x h", h=4), i_, BC.rearrange("p (x h) -> p x h", h=4),
                       ALU.subtract).then_inc(u_ready, 1)
                elif kind == "urow":
                    t, d = step[1:]
                    u = use(here, step)
                    c = t * 8 + d * 4
                    dve.wait_ge(u.filled, u.after)
                    rows = u.t[:, :].rearrange("p (h c) -> p h c", h=4)
                    ve.tensor_reduce(UM[:, c:c + 4], rows, AX.X, ALU.max)
                    tmp = TMP[:, :].rearrange("p (h c) -> p h c", h=4)
                    fence()
                    tt(tmp, rows, NEGT[1 - d].unsqueeze(1).to_broadcast([P, 4, P]), ALU.add).then_inc(u.drained, 1)
                    fence()
                    ve.tensor_reduce(PM[:, c:c + 4], tmp, AX.X, ALU.max)
                elif kind == "stab":
                    m0 = row("m0")
                    ve.memset(MS[:, 0:8], 0.0)
                    ve.tensor_copy(MS[:, 8:12], m0[:, 0:4])
                    ve.tensor_copy(MS[:, 20:24], m0[:, 4:8])
                    fence()
                    tt(MXX[:, 8:12], MS[:, 8:12], UM[:, 8:12], ALU.max)
                    tt(MXX[:, 20:24], MS[:, 20:24], UM[:, 20:24], ALU.max)
                    fence()
                    tt(MS[:, 16:20], TB[:, 8:12], MXX[:, 8:12], ALU.add)
                    tt(MS[:, 12:16], TB[:, 20:24], MXX[:, 20:24], ALU.add)
                    fence()
                    tt(MXX, MS, UM, ALU.max)
                    tt(NRR, MS, PM, ALU.max)
                    fence()
                    tt(MARG[:, 0, :], MS, NRR, ALU.subtract)
                    tt(MARG[:, 1, :], MS, MXX, ALU.subtract)
                    tt(MARG[:, 2, :], UU, MXX, ALU.subtract)
                    stt(MARG[:, 3, :], BC, -1.0, NRR, ALU.mult, ALU.subtract)
                    tt(MNEW, TB, MXX, ALU.add).then_inc(stab_ready, 1)
                    dve.wait_ge(stab_exp, l + 1)
                elif kind == "cstate":
                    i = step[1]
                    t, d = STATES[i]
                    c = t * 8 + d * 4
                    x = use(here, ("k_turn", t))
                    dve.wait_ge(x.drained, x.after)
                    tt(KW.rearrange("p (h c) -> p h c", h=4), MKTOK[:, t, :].rearrange("p (h c) -> p h c", h=4),
                       over(MEXP[:, 2, c:c + 4], 64), ALU.mult).then_inc(kw_ready, 1)
                    u = use(here, step)
                    new = u.t[:, 0:260].rearrange("p (a b) -> p a b", a=2)[:, :, 0:P + 1]
                    if i < 2:
                        dve.wait_ge(u.filled, u.after)
                        ve.tensor_copy(CC[:, d, :, :], new).then_inc(u.drained, 1)
                    else:
                        dve.wait_ge(c_out, l * 16 + 16)
                        dve.wait_ge(c0_in, l * 16 + 16)
                        dve.wait_ge(u.filled, u.after)
                        for h in range(HEADS):
                            half = slice(64 * (h % 2), 64 * (h % 2) + 64)
                            last = stt(CC[half, d, h // 2, :], CS[half, d, h // 2, :], MEXP[half, 1, c + h:c + h + 1],
                                       new[half, h // 2, :], ALU.mult, ALU.add)
                        last.then_inc(u.drained, 1)
                elif kind == "erow":
                    t, d = step[1:]
                    u = use(here, step)
                    dve.wait_ge(u.filled, u.after)
                    for h in range(4):
                        c = t * 8 + d * 4 + h
                        last = stt(EB[:, t % 2, d, tile(h)], u.t[:, tile(h)], UU[:, c:c + 1], NEGT[d],
                                   ALU.subtract, ALU.subtract)
                    last.then_inc(u.drained, 1)
                    if d == 1:
                        q = use(here, ("qk", t))
                        dve.wait_ge(q.drained, q.after)
                        for x in range(2):
                            dve.wait_ge(e_exp, l * 18 + (12 + t * 2 + x + 1))
                            tt(EB[:, t % 2, x, :], EB[:, t % 2, x, :], QK, ALU.mult).then_inc(m_ready, 1)
                elif kind == "num":
                    t, d = step[1:]
                    c = t * 8 + d * 4
                    num, den = use(here, step, 0), use(here, step, 2 if t else 1)
                    sint = MEXP[:, 0, c:c + 4]
                    ha = HA.rearrange("p (h c) -> p h c", h=4)
                    dve.wait_ge(num.filled, num.after)
                    if t:
                        inter = use(here, step, 1)
                        dve.wait_ge(inter.filled, inter.after)
                        tt(ha, inter.t[:, :].rearrange("p (h c) -> p h c", h=4), over(sint, P), ALU.mult).then_inc(inter.drained, 1)
                        fence()
                        tt(HA, HA, num.t[:, :], ALU.add).then_inc(num.drained, 1)
                        dve.wait_ge(den.filled, den.after)
                        tt(DEN[:, 0:4], den.t[:, 4:8], sint, ALU.mult)
                        fence()
                        tt(DEN[:, 0:4], DEN[:, 0:4], den.t[:, 0:4], ALU.add).then_inc(den.drained, 1)
                    else:
                        ve.tensor_copy(HA, num.t[:, :]).then_inc(num.drained, 1)
                        dve.wait_ge(den.filled, den.after)
                        ve.tensor_copy(DEN[:, 0:4], den.t[:, 0:4]).then_inc(den.drained, 1)
                    fence()
                    stt(DEN[:, 4:8], DEN[:, 0:4], -1.0, DEN[:, 0:4], ALU.mult, ALU.max)
                    fence()
                    tt(DEN[:, 4:8], DEN[:, 4:8], MEXP[:, 3, c:c + 4], ALU.max)
                    fence()
                    ve.reciprocal(DEN[:, 0:4], DEN[:, 4:8])
                    fence()
                    tmp = TMP[:, :].rearrange("p (h c) -> p h c", h=4)
                    if d == 0:
                        tt(tmp, ha, over(DEN[:, 0:4], P), ALU.mult)
                    else:
                        tt(ha, ha, over(DEN[:, 0:4], P), ALU.mult)
                        fence()
                        tt(TMP[:, :], TMP[:, :], HA, ALU.add).then_inc(y_sum, 1)
                    fence()
                elif kind == "ml_y":
                    t = step[1]
                    dve.wait_ge(y_rstd, l * 9 + (2 * TT + t + 1))
                    for h in range(HEADS):
                        stt(TMP[:, tile(h)], TMP[:, tile(h)], ST4[:, 0, h:h + 1], row("ml_g")[:, tile(h)], ALU.mult, ALU.mult)
                    fence()
                    tt(YTILE[:, (2 * TT + t) % 2, :], TMP[:, :], MO[:, t, :], ALU.mult).then_inc(y_ready, 1)
                    fence()
                elif kind == "out":
                    d = step[1]
                    u = use(here, step)
                    dve.wait_ge(u.filled, u.after)
                    for v, a, b in SEGS:
                        last = stt(XT[:, d, a:b], u.t[:, a:b], MOD[:, 2, d, v:v + 1], XT[:, d, a:b], ALU.mult, ALU.add)
                    last.then_inc(u.drained, 1)
                elif kind == "router":
                    u = use(here, step)
                    dve.wait_ge(u.filled, u.after)
                    logits = u.t[:, 0:TT * EXPERTS].rearrange("p (t e) -> p t e", t=TT)
                    ve.tensor_reduce(R3[:, 0:3], logits, AX.X, ALU.max)
                    fence()
                    tt(AFF[:, :, :], logits, over(R3[:, 0:3], EXPERTS), ALU.subtract).then_inc(u.drained, 1)
                    ve.memset(MG[:, :, :], 0.0)
                    ve.memset(YEC[:, :], 0.0)
                    dve.wait_ge(aff_exp, l + 1)
                    ve.tensor_reduce(R3[:, 3:6], AFF[:, :, :], AX.X, ALU.add)
                    fence()
                    ve.reciprocal(R3[:, 0:3], R3[:, 3:6])
                    fence()
                    tt(AFF[:, :, :], AFF[:, :, :], over(R3[:, 0:3], EXPERTS), ALU.mult)
                    fence()

            def group_step(l, g, step):
                kind = step[0]
                if kind == "rank":
                    j = step[1]
                    if j == 0:
                        ve.tensor_copy(AG[:, :, :], AFF[:, :, bass.ds(g * GE, GE)]).then_inc(ag_ready, 1)
                        fence()
                    u = use(here, step)
                    dve.wait_ge(u.filled, u.after)
                    for t in range(TT):
                        own = AG[:, t, j:j + 1]
                        a, b = (P, N) if t else (0, P)
                        first = before_at + {0: 1, 1: 1, 2: 0}[t] * P
                        mask = CT[:, first:first + b - a]
                        rank = RK[:, t:t + 1]
                        stt(TMP[:, 0:b - a], u.t[:, a:b], own, mask, ALU.is_equal, ALU.mult)
                        fence()
                        last = stt(TMP[:, 256:256 + b - a], u.t[:, a:b], own, TMP[:, 0:b - a], ALU.is_gt, ALU.add, accum_out=rank)
                        if t == TT - 1:
                            last.then_inc(u.drained, 1)
                        fence()
                        slot = const("slot_s" if t else "slot_c")
                        at = slice(j * CAP_S, (j + 1) * CAP_S)
                        ts(PO[:, t, at], slot, rank, None, ALU.is_equal)
                        last = ts(GO[:, t, at], slot, rank, own, ALU.is_equal, ALU.mult)
                        if t == TT - 1:
                            last.then_inc(picked, 1)
                elif kind == "gather" and step[1] == 0:
                    pass
                elif kind == "up":
                    j, half = step[1:]
                    gate, up = use(here, step, 0), use(here, step, 1)
                    dve.wait_ge(hid_sigmoid, l * (GROUPS * GE * 2) + g * (GE * 2) + (j * 2 + half + 1))
                    tt(SGE[:, half, :], SGE[:, half, :], gate.t[:, 0:4 * CAP], ALU.mult).then_inc(gate.drained, 1)
                    fence()
                    dve.wait_ge(up.filled, up.after)
                    tt(HID[:, j % 2, half * 4:half * 4 + 4, :], SGE[:, half, :].rearrange("p (f c) -> p f c", f=4),
                       up.t[:, 0:4 * CAP].rearrange("p (f c) -> p f c", f=4), ALU.mult).then_inc(up.drained, 1)
                elif kind == "scatter":
                    d = step[1]
                    u = use(here, step)
                    dve.wait_ge(u.filled, u.after)
                    tt(MG[:, d, :], MG[:, d, :], u.t[:, 0:N], ALU.add).then_inc(u.drained, 1)

            dve.wait_ge(c_sigmoid, 1)
            tt(CSIG[:, :, :], CSIG[:, :, :], CVEC[:, :, :], ALU.mult).then_inc(c_ready, 1)
            with dve.Fori(0, DEPTH) as l:
                here.layer, here.part = l, "layer"
                dve.wait_ge(small_in, l * 32 + 32)
                for step in STEPS:
                    mixer_step(l, step)
                    if step[0] in DVE_STEPS:
                        fence()
                with dve.Fori(0, GROUPS) as g:
                    here.group, here.part = g, "group"
                    for step in GROUP_STEPS:
                        group_step(l, g, step)
                        if step[0] in DVE_STEPS:
                            fence()
                for kt in range(KT):
                    for v, a, b in SEGS:
                        last = stt(XT[:, kt, a:b], MG[:, kt, a:b], MOD[:, 5, kt, v:v + 1], XT[:, kt, a:b], ALU.mult, ALU.add)
                fence()
                ve.tensor_copy(R3[:, 0:1], R3[:, 0:1]).then_inc(layer_done, 1)
            here.part = "end"
            norm(DEPTH, 0, 2, None)


_WEIGHTS = ["ada_w", "w_in", "w_branch", "w_mgate", "w_out", "ex_w_gate", "ex_w_up", "ex_w_down"]
_OUTS = {
    "k_out": (DEPTH, P, HEADS, P), "v_out": (DEPTH, P, 512), "ssm_out": (DEPTH, 2, P, 256),
    "c_out": (DEPTH, P, 2, 2, P + 1), "m_out": (DEPTH, 8), "y_out": (P, KT, N),
}


def _columns(a, parts):
    return np.ascontiguousarray(a.reshape(parts, P).T)


def kernel(**inputs):
    import numpy as _np
    import concourse.bacc as _bacc
    from concourse.bass_utils import run_bass_kernel_spmd as _run

    a = {k: _np.asarray(v) for k, v in inputs.items()}
    arrays = {k: _np.ascontiguousarray(a[k]) for k in _WEIGHTS}
    arrays["constants"] = CONSTANTS
    x = _np.concatenate([a["x_prompt"][0], a["x_sample"][0]], axis=0)
    arrays["x_t"] = _np.ascontiguousarray(x.reshape(N, KT, P).transpose(2, 1, 0))
    arrays["c_t"] = _np.stack([_columns(a["c_ctx"], KT), _columns(a["c"][0], KT)], axis=2)
    rows, cols = [], []
    for l in range(DEPTH):
        lam_init = 0.8 - 0.6 * math.exp(-0.3 * l)
        rows.append(_np.concatenate([
            a["mb_dt_bias"][l].reshape(-1), a["mb_a_log"][l].reshape(-1), a["mb_d"][l], a["ml_gate_b"][l].reshape(-1),
            a["state_mlstm_m"][0, l].reshape(-1), a["da_lambda"][l].reshape(-1), a["da_subln_g"][l],
            a["mb_norm_g"][l], a["ml_norm_g"][l].reshape(-1),
            _np.array([lam_init, 1.0 - lam_init], _np.float32)]))
        cols.append(_np.concatenate([
            _columns(a["ada_b"][l], 48), _columns(a["norm1_g"][l], KT), _columns(a["norm2_g"][l], KT),
            _columns(a["b_mgate"][l], 24), _columns(a["mb_conv_w"][l].reshape(-1), 18), _columns(a["mb_conv_b"][l], 6),
            a["router_w"][l].reshape(KT, P, EXPERTS).transpose(1, 0, 2).reshape(P, KT * EXPERTS),
            _columns(a["final_g"], KT)], axis=1))
    arrays["rows"], arrays["cols"] = _np.stack(rows), _np.stack(cols)
    arrays["cache_k_t"] = _np.ascontiguousarray(
        a["cache_k"][0].reshape(DEPTH, P, HEADS, 2 * 64).transpose(0, 3, 2, 1))
    arrays["cache_v"] = _np.ascontiguousarray(a["cache_v"][0].reshape(DEPTH, P, 512))
    arrays["ssm_t"] = _np.ascontiguousarray(
        a["state_ssm"][0].reshape(DEPTH, 2, 2, 4, 64, 64).transpose(0, 1, 2, 5, 3, 4).reshape(DEPTH, 2, P, 256))
    cn = _np.concatenate([a["state_mlstm_c"][0], a["state_mlstm_n"][0][..., None]], axis=-1)
    arrays["c_t0"] = _np.ascontiguousarray(
        cn.reshape(DEPTH, 2, 2, 2, 64, P + 1).transpose(0, 3, 4, 1, 2, 5).reshape(DEPTH, P, 2, 2, P + 1))

    nc = _bacc.Bacc("TRN2", target_bir_lowering=False, num_devices=1)
    aps = {k: nc.dram_tensor(k, v.shape, F, kind="ExternalInput").ap() for k, v in arrays.items()}
    aps.update({k: nc.dram_tensor(k, s, F, kind="ExternalOutput").ap() for k, s in _OUTS.items()})
    build(nc, aps)
    r = _run(nc, [arrays], core_ids=[0]).results[0]

    y = r["y_out"].transpose(2, 1, 0).reshape(N, D)
    k = r["k_out"].transpose(0, 3, 2, 1).reshape(1, DEPTH, P, HEADS, 2, 64)
    v = r["v_out"].reshape(1, DEPTH, P, HEADS, 2 * 64)
    ssm = r["ssm_out"].reshape(DEPTH, 2, 2, 64, 4, 64).transpose(0, 1, 2, 4, 5, 3).reshape(1, DEPTH, 2, 8, 64, 64)
    c = r["c_out"].reshape(DEPTH, 2, 64, 2, 2, P + 1).transpose(0, 3, 4, 1, 2, 5).reshape(1, DEPTH, 2, HEADS, 64, P + 1)
    m = r["m_out"].reshape(1, DEPTH, 2, HEADS)
    return (y[None, :P], y[None, P:], k, v, ssm, c[..., :P], c[..., P], m)
```

```python
import math
from contextlib import ExitStack

import numpy as np
import concourse.bass as bass
from concourse import mybir

F = mybir.dt.float32
ALU = mybir.AluOpType
ACT = mybir.ActivationFunctionType
AX = mybir.AxisListType

P = 128
D = 1024
KT = D // P
DEPTH = 2
TT = 3
N = TT * P
NS = 2 * P
SEGS = ((0, 0, P), (1, P, N))
EPS = 1e-6
HEADS = 4
RING = 4
MIX_RING = 3
CH = 512
EXPERTS = 16
GE = 4
GROUPS = EXPERTS // GE
CAP_S, CAP_C = 32, 16
SLOTS = 64
NEG = -1.0e30
XW = N + 3

Q0, K0, V0, Z0, X0, DT0, MQ0, MV0, MO0, IF0 = 0, 512, 1024, 1536, 2048, 2816, 2832, 3344, 3856, 4368
WIN = 4384

MIX_CHUNKS = (
    [("ada", c * CH) for c in range(4)]
    + [("q", Q0), ("k", K0), ("v", V0), ("z", Z0), ("x0", X0), ("x1", X0 + CH)]
    + [("ada", c * CH) for c in range(4, 12)]
    + [("gate", 0), ("gate", 1), ("branch", 0), ("branch", 1)]
    + [("mq", MQ0), ("if", IF0), ("gate", 2), ("gate", 3), ("mv", MV0), ("mo", MO0)]
    + [("branch", 2), ("branch", 3), ("gate", 4), ("gate", 5), ("branch", 4), ("branch", 5)]
    + [("out", 0), ("out", 1)]
)
EXPERT_CHUNKS = ["gate0", "up0", "gate1", "up1", "down0", "down1"]
CHUNKS = len(MIX_CHUNKS) + EXPERTS * len(EXPERT_CHUNKS)
assert len(MIX_CHUNKS) % MIX_RING == 0 and (GE * len(EXPERT_CHUNKS)) % RING == 0

STATES = [(0, 0), (0, 1), (1, 0), (2, 1)]
STARTED = [(1, 0), (2, 1), (1, 1), (2, 0)]


def schedule():
    s = []
    for c in range(4):
        s += [("ada", c)] + ([("ada_turn", c - 1)] if c else [])
    s += [("ada_turn", 3), ("norm", 0)]
    s += [("q", h) for h in range(HEADS)] + [("k", h) for h in range(HEADS)] + [("rope",)]
    s += [("v", t) for t in range(TT)]
    dense = [[("z", t)] for t in range(TT)] + [[("x", j)] for j in range(6)] + [[("dt",)]]
    dense += [[("ada", c)] + ([("ada_turn", c - 1)] if c > 4 else []) for c in range(4, 12)]
    dense[-1].append(("ada_turn", 11))
    dense += [[("gate", 0, d)] for d in range(KT)]

    def take(k=1):
        for _ in range(k):
            if dense:
                s.extend(dense.pop(0))

    n = TT * HEADS
    for i in range(n + 2):
        if i < n:
            s.append(("score", i))
        if len(dense) > 2:
            take()
        if 0 <= i - 1 < n:
            s.append(("turn", i - 1))
        if len(dense) > 2:
            take()
        if 0 <= i - 2 < n:
            s.append(("value", i - 2))
            if (i - 2) % HEADS == HEADS - 1:
                s += [("att_y", (i - 2) // HEADS)]
        if i - 4 >= 0 and (i - 4) % HEADS == HEADS - 1:
            s += [("y_turn", 0, (i - 4) // HEADS)]
    take(len(dense))
    s += [("y_turn", 0, 2)]
    for d in range(KT):
        s += [("merge", 0, d)] + ([("conv", d - 1)] if d >= 1 else [])
    s += [("z_sig",)]
    dense += [[("mq", j)] for j in range(4)] + [[("if",)]] + [[("gate", 1, d)] for d in range(KT)]
    dense += [[("mv", t)] for t in range(TT)] + [[("mo", t)] for t in range(TT)]
    s += [("acum",)]
    for t in range(TT):
        s += [("xs_turn", t), ("b_turn", t)]
    for i in range(4):
        s += [("state", i)]
        take()
    take()
    small = [[("bcum",)], [("urow", 0, 0)], [("urow", 0, 1)], [("urow", 1, 0)], [("urow", 1, 1)], [("urow", 2, 0)],
             [("urow", 2, 1)], [("stab",)]]
    for t in range(TT):
        s += [("xd", t), ("decay", t, 0)]
        take()
        s += [("decay", t, 1)]
        take()
        s += small.pop(0)
        s += [("diag", t, 0)]
        take()
        s += [("diag", t, 1)]
        if t:
            s += [("off", t, 0), ("off", t, 1)]
        s += [("mb_y", t)]
        if t == TT - 1:
            s += small.pop(0)
        else:
            s += small.pop(0)
            take()
            s += small.pop(0)
        take(2 if t == TT - 1 else 1)
        s += [("y_turn", 1, t)]
    take(len(dense))
    for d in range(KT):
        s += [("merge", 1, d)]
        if small and d % 2:
            s += small.pop(0)
    for x in small:
        s += x
    s += [("mo_sig",)]
    dense += [[("gate", 2, d)] for d in range(KT)]
    s += [("k_turn", t) for t in range(TT)]
    take()
    for i in range(4):
        s += [("cstate", i)]
        if i % 2:
            take()
    for t in range(TT):
        s += [("qk", t), ("erow", t, 0), ("erow", t, 1)]
        take()
        s += [("num", t, 0), ("num", t, 1), ("ml_y", t)]
        take(2 if t == TT - 1 else 1)
        s += [("y_turn", 2, t)]
    take(len(dense))
    s += [("merge", 2, d) for d in range(KT)]
    s += [("out", d) for d in range(KT)]
    s += [("norm", 1)]
    s += [("h_turn", t, f) for t in range(TT) for f in range(2)] + [("router",)]
    s += [("rank", j) for j in range(GE)]
    return s


def group_schedule():
    s = [("gather", a) for a in range(4)] + [("g_turn",)]
    for j in range(GE):
        s += [("up", j, 0), ("up", j, 1), ("hid_turn", j), ("next_rank", j), ("down", j, 0), ("down", j, 1)]
    s += [("scatter", d) for d in range(KT)]
    return s


STEPS = schedule()
GROUP_STEPS = group_schedule()
END_STEPS = [("norm", 2)]

ACT_STEPS = {"score", "att_y", "merge", "conv", "mb_y", "ml_y", "norm", "decay", "erow", "gather", "router", "up",
             "turn", "dt", "if", "stab", "acum", "y_turn", "z", "z_sig", "mo_sig", "gate", "xs_turn", "b_turn", "h_turn"}
DVE_STEPS = {"ada", "ada_turn", "norm", "rope", "v", "turn", "score", "att_y", "merge", "z_sig", "dt", "conv", "acum", "state", "xd",
             "decay", "diag", "mb_y", "if", "bcum", "urow", "cstate", "erow", "num", "ml_y", "out", "router", "rank", "next_rank",
             "up", "scatter"}

BANKS = ("D0", "D1", "T0", "T1", "R0", "R1", "Y0", "Y1")


def banks_of(step, turn):
    kind = step[0]

    def rot(k):
        turn[k] += 1
        return f"{k}{turn[k] % 2}"

    if kind in ("ada", "norm", "q", "k", "v", "z", "x", "dt", "mq", "mv", "mo", "if", "out",
                "gate", "merge"):
        return [rot("D")]
    if kind == "up":
        return [rot("D"), rot("D")]
    if kind in ("turn", "y_turn", "xs_turn", "b_turn", "acum", "state", "off", "bcum", "k_turn", "cstate", "qk",
                "h_turn", "router", "g_turn", "ada_turn", "hid_turn"):
        return [rot("T")]
    if kind == "score":
        return ["R0", "R1"]
    if kind == "decay":
        return ["R0", "R1"]
    if kind in ("urow", "erow"):
        return [f"R{step[2]}"]
    if kind in ("rank", "next_rank"):
        return [f"R{step[1] % 2}"]
    if kind == "value":
        return [f"Y{step[1] // HEADS % 2}"] if step[1] % HEADS == 0 else []
    if kind == "diag":
        return [f"Y{step[1] % 2}"] if step[2] == 0 else []
    if kind == "num":
        return ["Y0", "Y1"] + ([rot("T"), rot("T")] if step[1] else [])
    if kind == "gather":
        return [f"Y{step[1] % 2}"]
    if kind == "down":
        return [f"Y{step[2]}"]
    if kind == "scatter":
        return [f"R{step[1] % 2}"]
    return []


def bank_uses():
    uses = {b: {"layer": [], "group": [], "end": []} for b in BANKS}
    where = {}
    turn = {"D": 0, "T": 0}
    for part, steps in (("layer", STEPS), ("group", GROUP_STEPS), ("end", END_STEPS)):
        for step in steps:
            for k, b in enumerate(banks_of(step, turn)):
                where[(part, step, k)] = (b, len(uses[b][part]))
                uses[b][part].append((step, k))
    return uses, where


BANK_USES, WHERE = bank_uses()


class Place:

    def __init__(self):
        self.layer, self.group, self.part = 0, 0, "layer"


class Use:

    def __init__(self, hw, place, step, k=0, part=None, group=None):
        part = part or ("layer" if ("layer", step, k) in WHERE and place.part != "end" else place.part)
        name, i = WHERE[(part, step, k)]
        uses = BANK_USES[name]
        per_layer = len(uses["layer"]) + GROUPS * len(uses["group"])
        n = place.layer * per_layer
        if part == "layer":
            i += 0
        elif part == "group":
            i += len(uses["layer"])
            g = place.group if group is None else group
            if isinstance(g, int):
                i += g * len(uses["group"])
            else:
                n = n + g * len(uses["group"])
        else:
            n, i = DEPTH * per_layer, i
        self.t, self.filled, self.drained = hw.banks[name], hw.filled[name], hw.drained[name]
        self.before, self.after = n + (i + 1), n + (i + 2)
        self.bank, self.order = name, (part, i)


def drains(after, before=()):
    last = {}
    for u, value, i in [(u, u.after, 1) for u in after] + [(u, u.before, 0) for u in before]:
        place = (u.order[0] != "layer", u.order[1] + i)
        if u.bank not in last or last[u.bank][0] < place:
            last[u.bank] = (place, u.drained, value)
    return [(semaphore, value) for _, semaphore, value in last.values()]


def constant_table():
    i, j = np.meshgrid(np.arange(P), np.arange(P), indexing="ij")
    parts = {
        "ident": (i == j), "tri_f": (i <= j), "tri_b": (i >= j),
        "neg_f": np.where(i <= j, 0.0, NEG), "neg_b": np.where(i >= j, 0.0, NEG),
        "ones": np.ones((P, P)), "before": (j < i), "none": np.zeros((P, P)),
    }
    t = np.arange(NS)
    pos = np.stack([t // 64, t % 64]).astype(np.float32)
    inv = (np.float32(10000.0) ** (-np.arange(16, dtype=np.float32) / np.float32(16))).astype(np.float32)
    ch = np.arange(P) % 64
    ang = pos[ch // 32] * inv[ch % 16][:, None]
    parts["cos"] = np.cos(ang)
    parts["sin"] = np.sin(ang) * np.where(ch % 32 < 16, -1.0, 1.0)[:, None]
    parts["slot_s"] = np.broadcast_to(np.arange(CAP_S), (P, CAP_S))
    parts["slot_c"] = np.broadcast_to(np.where(np.arange(CAP_S) < CAP_C, np.arange(CAP_S), -1), (P, CAP_S))
    parts["eps"] = np.full((P, 1), EPS)
    where, at = {}, 0
    for k, v in parts.items():
        where[k] = (at, at + v.shape[1])
        at += v.shape[1]
    return np.concatenate([np.asarray(v, np.float32) for v in parts.values()], axis=1), where


CONSTANTS, CONST_AT = constant_table()


def offsets(sizes):
    where, at = {}, 0
    for k, n in sizes:
        where[k] = (at, at + n)
        at += n
    return where, at


ROW_SIZES = [("dt_b", 16), ("a_log", 16), ("mb_d", 8), ("gate_b", 16), ("m0", 8), ("lam", 256), ("subln", P),
             ("mb_g", 512), ("ml_g", 512), ("lam_init", 1), ("lam_rest", 1)]
ROW_AT, ROW_N = offsets(ROW_SIZES)
COL_SIZES = [("ada_b", 48), ("n1", KT), ("n2", KT), ("b_gate", 24), ("conv_w", 18), ("conv_b", 6),
             ("router", KT * EXPERTS), ("final", KT)]
COL_AT, COL_N = offsets(COL_SIZES)



def last_uses():
    out = []
    for kind, c in MIX_CHUNKS:
        if kind == "ada":
            out.append((("ada", c // CH), 0))
        elif kind in ("gate", "branch"):
            out.append((("gate" if kind == "gate" else "merge", c // 2, c % 2 * 4 + 3), 0))
        elif kind == "out":
            out.append((("out", c * 4 + 3), 0))
        else:
            out.append(({"q": ("q", 3), "k": ("k", 3), "v": ("v", 2), "z": ("z", 2), "x0": ("x", 3), "x1": ("dt",),
                         "mq": ("mq", 3), "mv": ("mv", 2), "mo": ("mo", 2), "if": ("if",)}[kind], 0))
    return out


LAST_USE = last_uses()
GROUP_LAST_USE = [use for j in range(GE) for use in
                  ((("up", j, 0), 0), (("up", j, 0), 1), (("up", j, 1), 0), (("up", j, 1), 1),
                   (("down", j, 0), 0), (("down", j, 1), 0))]
GROUP_CHUNKS = len(GROUP_LAST_USE)
CHUNK_AT = {}
for _i, (_kind, _c) in enumerate(MIX_CHUNKS):
    CHUNK_AT[(_kind, _c // CH if _kind == "ada" else _c if _kind in ("gate", "branch", "out") else 0)] = _i


def mix_loads(slot):
    return len(MIX_CHUNKS) // MIX_RING if slot < MIX_RING else 0


def slot_loads(slot):
    return mix_loads(slot) + GROUPS * GROUP_CHUNKS // RING


class Hardware:
    pass


def build(nc, A):
    ctx = ExitStack()
    with ctx:
        hw = Hardware()
        hw.banks = {b: ctx.enter_context(nc.psum_tensor(f"bank_{b}", [P, 512], F)) for b in BANKS}
        hw.filled = {b: ctx.enter_context(nc.semaphore(f"filled_{b}")) for b in BANKS}
        hw.drained = {b: ctx.enter_context(nc.semaphore(f"drained_{b}")) for b in BANKS}

        def sb(name, *shape):
            return ctx.enter_context(nc.sbuf_tensor(name, [P, *shape], F))

        def sem(name):
            return ctx.enter_context(nc.semaphore(name))

        ring = sb("ring", RING, KT * CH)
        XT, HT, MG = sb("XT", KT, N), sb("HT", KT, N), sb("MG", KT, N)
        CT = sb("CT", CONSTANTS.shape[1])
        ROWS, COLS = sb("ROWS", ROW_N), sb("COLS", COL_N)
        CSIG = sb("CSIG", KT, 32)
        MOD, AMOD = sb("MOD", 6, KT, 2), sb("AMOD", 2, KT, 2)
        RS = sb("RS", N)
        GB = ring[:, RING - 1, 0:KT * N].rearrange("p (k n) -> p k n", k=KT)
        LAM = sb("LAM", 2 * KT)
        EB = sb("EB", 2, 2, HEADS * P)
        YTILE, YT = sb("YTILE", 2, 512), sb("YT", 4, N)
        TMP = sb("TMP", 512)
        ST4 = sb("ST4", 2, HEADS)

        def const(name):
            a, b = CONST_AT[name]
            return CT[:, a:b]

        def row(name):
            a, b = ROW_AT[name]
            return ROWS[:, a:b]

        def col(name):
            a, b = COL_AT[name]
            return COLS[:, a:b]

        ident, ones, eps = const("ident"), const("ones"), const("eps")
        TRI = (const("tri_f"), const("tri_b"))
        NEGT = (const("neg_f"), const("neg_b"))
        before_at = CONST_AT["ones"][0]

        def views(arena, sizes):
            out, at = [], 0
            for shape in sizes:
                n = math.prod(shape)
                v = arena[:, at:at + n]
                if len(shape) == 2:
                    v = v.rearrange("p (a b) -> p a b", a=shape[0])
                if len(shape) == 3:
                    v = v.rearrange("p (a b c) -> p a b c", a=shape[0], b=shape[1])
                out.append(v)
                at += n
            assert at <= arena.shape[1], (at, arena.shape)
            return out

        arena_a, arena_b = sb("arena_a", 7948), sb("arena_b", 9876)
        CVEC, = views(arena_b, [(KT, 2)])
        QT, KTT, V, VC, PR, PT, NMX, SMX, RCP = views(
            arena_a, [(HEADS, N), (HEADS, 4 * P), (TT, 512), (512,), (2, 2, N), (2, N), (2, 2), (2, 2), (2, 2)])
        ROT = PR.rearrange("p a b c -> p (a b c)")[:, 0:HEADS * NS].rearrange("p (a b) -> p a b", a=HEADS)
        MQ, MK, MKTOK, MV, MO, CS, CC, PRE, LG, UB, MARG, MEXP, HC = views(
            arena_a, [(2, N), (2, N), (TT, 2 * P), (TT, HEADS, 129), (TT, 512), (2, 2, 129), (2, 2, 129),
                      (48,), (3, 24), (8, 24), (4, 24), (4, 24), (2, 256)])
        UM, PM, MS, MXX, NRR, MNEW, BC, TB = [UB[:, k, :] for k in range(8)]
        LAB, LFF, UU = [LG[:, k, :] for k in range(3)]
        Z, XB, CX, XD, XWT, HS, CB, BTK, DT3, EX3, DTV, EXPA = views(
            arena_b, [(TT, 512), (6, XW), (6, XW), (2, 512), (512,), (2, 256), (TT, 256), (TT, P),
                      (3, 48), (3, 48), (4, 48), (16,)])
        XS = XB.rearrange("p a b -> p (a b)")[:, 0:TT * 512].rearrange("p (a b) -> p a b", a=TT)
        OFF = (0, P + 1, 2 * P + 1)
        HA, DEN, QK, KW = views(arena_b, [(HEADS * 130,), (8,), (512,), (2 * P,)])
        H2, PO, GO, GT, XE, YES, YEC, RK, AFF, AG, R3 = views(
            arena_b, [(TT, D), (TT, GE * CAP_S), (TT, GE * CAP_S), (TT, P), (KT, GE, SLOTS),
                      (D,), (D,), (16,), (TT, EXPERTS + GE), (TT, GE), (8,)])
        SGE, HH, HIDT = views(EB[:, :, :, :].rearrange("p a b c -> p (a b c)"), [(2, 256), (2, 256), (2, KT, SLOTS)])

        def tile(t):
            return slice(t * P, (t + 1) * P)

        slot_in = [sem(f"slot_in_{k}") for k in range(RING)]
        consts_in, small_in, cache_in, ssm_in, c0_in = (
            sem(x) for x in ("consts_in", "small_in", "cache_in", "ssm_in", "c0_in"))
        layer_done, arena_free = sem("layer_done"), sem("arena_free")
        c_sigmoid, c_ready = sem("c_sigmoid"), sem("c_ready")
        squares, rstd_ready, scaled, h_ready = sem("squares"), sem("rstd_ready"), sem("scaled"), sem("h_ready")
        lam_sums, lam_exps = sem("lam_sums"), sem("lam_exps")
        rope_done, maxes, probs_ready = sem("rope_done"), sem("maxes"), sem("probs_ready")
        y_sum, y_rstd, y_ready = sem("y_sum"), sem("y_rstd"), sem("y_ready")
        gate_sigmoid, o_sigmoid, merged = sem("gate_sigmoid"), sem("o_sigmoid"), sem("merged")
        z_sigmoid, dt_abs, dt_ln, a_exp, dta_ready = (
            sem(x) for x in ("z_sigmoid", "dt_abs", "dt_ln", "a_exp", "dta_ready"))
        conved, conv_sigmoid, conv_done = sem("conved"), sem("conv_sigmoid"), sem("conv_done")
        ac_ready, ac_exp, xd_ready, xw_ready = sem("ac_ready"), sem("ac_exp"), sem("xd_ready"), sem("xw_ready")
        e_exp, m_ready = sem("e_exp"), sem("m_ready")
        lf_abs, lf_ln, lf_ready, u_ready = sem("lf_abs"), sem("lf_ln"), sem("lf_ready"), sem("u_ready")
        stab_ready, stab_exp, kw_ready = sem("stab_ready"), sem("stab_exp"), sem("kw_ready")
        aff_exp, ag_ready, picked, hid_sigmoid = sem("aff_exp"), sem("ag_ready"), sem("picked"), sem("hid_sigmoid")
        k_out, v_out, ssm_out, c_out, m_out, y_out = (sem(x) for x in ("k_out", "v_out", "ssm_out", "c_out", "m_out", "y_out"))
        y_final = sem("y_final")

        def use(place, step, k=0, part=None, group=None):
            return Use(hw, place, step, k, part, group)

        block = ctx.enter_context(nc.Block())

        @block.sync
        def _(sp):
            here = Place()

            def load_mix(l, i):
                kind, c = MIX_CHUNKS[i]
                one = bass.ds(l, 1)
                kt, n = KT, CH
                if kind == "ada":
                    src = A["ada_w"][one, :, c:c + CH]
                elif kind == "gate":
                    src = A["w_mgate"][one, :, c * CH:(c + 1) * CH]
                elif kind == "branch":
                    kt = KT // 2
                    src = A["w_branch"][one, c // 2, :, c % 2 * CH:(c % 2 + 1) * CH]
                elif kind == "out":
                    src = A["w_out"][one, :, c * CH:(c + 1) * CH]
                else:
                    n = {"x1": MQ0 - X0 - CH, "if": 16}.get(kind, CH)
                    src = A["w_in"][one, :, c:c + n]
                sp.dma_start(ring[:, i % MIX_RING, 0:kt * n].rearrange("p (k n) -> p k n", k=kt),
                             src.rearrange("a (k p) n -> p (a k) n", p=P),
                             allow_slow_non_contiguous=True).then_inc(slot_in[i % MIX_RING], 16)

            def load_expert(l, g, i):
                j, what = i // 6, EXPERT_CHUNKS[i % 6]
                half = int(what[-1])
                src = A["ex_w_" + what[:-1]][bass.ds(l, 1), bass.ds(g * GE + j, 1), :, half * CH:(half + 1) * CH]
                sp.dma_start(ring[:, i % RING, :].rearrange("p (k n) -> p k n", k=KT),
                             src.rearrange("a e (k p) n -> p (a e k) n", p=P)).then_inc(slot_in[i % RING], 16)

            with sp.Fori(0, DEPTH) as l:
                here.layer = l
                for i in range(len(MIX_CHUNKS)):
                    if i < MIX_RING:
                        step, k = GROUP_LAST_USE[GROUP_CHUNKS - RING + i]
                        at_1 = Place()
                        at_1.layer = 0
                        last = use(at_1, step, k, "group", GROUPS - 1)
                        sp.wait_ge(last.filled, l * (last.after - 1) + 1)
                    else:
                        last = use(here, *LAST_USE[i - MIX_RING])
                        sp.wait_ge(last.filled, last.after)
                    load_mix(l, i)
                for i in range(RING):
                    if i < MIX_RING:
                        last = use(here, *LAST_USE[len(MIX_CHUNKS) - MIX_RING + i])
                        sp.wait_ge(last.filled, last.after)
                    else:
                        last = use(here, ("merge", 2, KT - 1))
                        sp.wait_ge(last.drained, last.after)
                    load_expert(l, 0, i)
                with sp.Fori(0, GROUPS - 1) as g:
                    for i in range(RING, GROUP_CHUNKS + RING):
                        step, k = GROUP_LAST_USE[i - RING]
                        last = use(here, step, k, "group", g)
                        sp.wait_ge(last.filled, last.after)
                        load_expert(l, g + i // GROUP_CHUNKS, i % GROUP_CHUNKS)
                for i in range(RING, GROUP_CHUNKS):
                    step, k = GROUP_LAST_USE[i - RING]
                    last = use(here, step, k, "group", GROUPS - 1)
                    sp.wait_ge(last.filled, last.after)
                    load_expert(l, GROUPS - 1, i)

        @block.gpsimd
        def _(pool):
            here = Place()
            for b in BANKS:
                pool.sem_inc(hw.filled[b], 1)
                pool.sem_inc(hw.drained[b], 1)
            pool.sem_inc(layer_done, 1)
            pool.dma_start(CVEC[:, :, :], A["c_t"]).then_inc(consts_in, 16)
            pool.dma_start(CT[:, :], A["constants"]).then_inc(consts_in, 16)
            pool.dma_start(XT[:, :, :], A["x_t"]).then_inc(consts_in, 16)
            for l in range(DEPTH):
                here.layer = l
                one = slice(l, l + 1)
                if l:
                    pool.wait_ge(layer_done, l + 1)
                pool.dma_start(COLS[:, :], A["cols"][one].rearrange("a p n -> p (a n)")).then_inc(small_in, 16)
                pool.dma_start(ROWS[:, :], A["rows"][one].to_broadcast([P, ROW_N])).then_inc(small_in, 16)
                if l:
                    pool.wait_ge(c_out, l * 16)
                    pool.wait_ge(m_out, l * 16)
                pool.sem_inc(arena_free, 1)
                pool.dma_start(KTT[:, :, P:2 * P], A["cache_k_t"][one].rearrange("a p h t -> p (a h) t")).then_inc(cache_in, 16)
                pool.dma_start(VC[:, :], A["cache_v"][one].rearrange("a p n -> p (a n)")).then_inc(cache_in, 16)
                pool.dma_start(HS[:, :, :], A["ssm_t"][one].rearrange("a d p n -> p (a d) n")).then_inc(ssm_in, 16)
                for h in (HEADS - 2, HEADS - 1):
                    u = use(here, ("k", h))
                    pool.wait_ge(u.drained, u.after)
                pool.dma_start(A["k_out"][one].rearrange("a p h t -> p (a h) t"), KTT[:, :, 0:P]).then_inc(k_out, 16)
                u = use(here, ("v", 0))
                pool.wait_ge(u.drained, u.after)
                pool.dma_start(A["v_out"][one].rearrange("a p n -> p (a n)"), V[:, 0, :]).then_inc(v_out, 16)
                u = use(here, ("value", (TT - 1) * HEADS))
                pool.wait_ge(u.drained, u.after)
                pool.wait_ge(k_out, l * 16 + 16)
                pool.wait_ge(v_out, l * 16 + 16)
                pool.dma_start(CS[:, :, :, :], A["c_t0"][one].rearrange("a p d t n -> p (a d) t n")).then_inc(c0_in, 16)
                for i in (0, 1):
                    u = use(here, ("state", i))
                    pool.wait_ge(u.drained, u.after)
                pool.dma_start(A["ssm_out"][one].rearrange("a d p n -> p (a d) n"), HC[:, :, :]).then_inc(ssm_out, 16)
                pool.wait_ge(stab_ready, l + 1)
                pool.dma_start(A["m_out"][one], MNEW[0:1, 0:8]).then_inc(m_out, 16)
                for i in (0, 1):
                    u = use(here, ("cstate", i))
                    pool.wait_ge(u.drained, u.after)
                pool.dma_start(A["c_out"][one].rearrange("a p d t n -> p (a d) t n"), CC[:, :, :, :]).then_inc(c_out, 16)
            pool.wait_ge(y_final, KT)
            pool.dma_start(A["y_out"], HT[:, :, :]).then_inc(y_out, 16)
            pool.wait_ge(y_out, 16)
            for s in (k_out, v_out, ssm_out, c_out, m_out):
                pool.wait_ge(s, DEPTH * 16)

        @block.tensor
        def _(pe):
            here = Place()
            mm, turn = nc.tensor.matmul, nc.tensor.transpose
            row_fence = nc.tensor.drain

            def chunk(l, name, n=CH, kt=KT):
                i = CHUNK_AT[name]
                pe.wait_ge(slot_in[i % MIX_RING], 16 * (l * slot_loads(i % MIX_RING)) + 16 * (i // MIX_RING + 1))
                return ring[:, i % MIX_RING, 0:kt * n].rearrange("p (k n) -> p k n", k=kt)

            def expert_chunk(l, g, i):
                n = l * slot_loads(i % RING) + g * (GROUP_CHUNKS // RING)
                pe.wait_ge(slot_in[i % RING], n * 16 + 16 * (mix_loads(i % RING) + i // RING + 1))
                return ring[:, i % RING, :].rearrange("p (k n) -> p k n", k=KT)

            def to_channels(u, w, c, src=HT):
                for kt in range(KT):
                    last = mm(u.t[:, 0:N], w[:, kt, c * P:(c + 1) * P], src[:, kt, :], start=kt == 0, stop=kt == KT - 1)
                last.then_inc(u.filled, 1)

            def to_tokens(u, w, t):
                for kt in range(KT):
                    last = mm(u.t[:, :], HT[:, kt, tile(t)], w[:, kt, 0:CH], start=kt == 0, stop=kt == KT - 1)
                last.then_inc(u.filled, 1)

            def spread(u, cols):
                for k, c in enumerate(cols):
                    last = turn(u.t[:, tile(k)], c.to_broadcast([P, P]), ident)
                last.then_inc(u.filled, 1)

            def norm(l, i, name):
                u = use(here, ("norm", name))
                pe.wait_ge(u.drained, u.before)
                for kt in range(KT):
                    pe.wait_ge(squares, l * (2 * KT) + (i * KT + kt + 1))
                    last = mm(u.t[:, 0:N], ones, HT[:, kt, :], start=kt == 0, stop=kt == KT - 1)
                last.then_inc(u.filled, 1)

            def mixer_step(l, step):
                kind = step[0]
                if kind == "ada":
                    c = step[1]
                    u = use(here, step)
                    w = chunk(l, ("ada", c))
                    pe.wait_ge(c_ready, 1)
                    pe.wait_ge(u.drained, u.before)
                    for kt in range(KT):
                        for j in range(4):
                            last = mm(u.t[32 * j:32 * j + 32, 0:P], CSIG[:, kt, :], w[:, kt, tile(j)],
                                      start=kt == 0, stop=kt == KT - 1)
                    last.then_inc(u.filled, 1)
                elif kind == "ada_turn":
                    c = step[1]
                    u, a = use(here, step), use(here, ("ada", c))
                    pe.wait_ge(a.drained, a.after)
                    pe.wait_ge(u.drained, u.before)
                    turn(u.t[:, 0:P], EB[:, 0, 0, tile(c % 2)], ident).then_inc(u.filled, 1)
                elif kind == "norm":
                    norm(l, step[1], step[1])
                elif kind in ("q", "k", "mq"):
                    u = use(here, step)
                    w = chunk(l, (kind, 0))
                    pe.wait_ge(h_ready, l * 2 + 1)
                    pe.wait_ge(u.drained, u.before)
                    to_channels(u, w, step[1])
                elif kind in ("v", "z", "mv", "mo"):
                    u = use(here, step)
                    w = chunk(l, (kind, 0))
                    pe.wait_ge(u.drained, u.before)
                    to_tokens(u, w, step[1])
                elif kind == "x":
                    j = step[1]
                    u = use(here, step)
                    w = chunk(l, ("x0", 0)) if j < 4 else chunk(l, ("x1", 0), MQ0 - X0 - CH)
                    pe.wait_ge(u.drained, u.before)
                    to_channels(u, w, j % 4)
                elif kind in ("dt", "if"):
                    u = use(here, step)
                    w = chunk(l, ("x1", 0), MQ0 - X0 - CH)[:, :, 256:272] if kind == "dt" else chunk(l, ("if", 0), 16)
                    pe.wait_ge(u.drained, u.before)
                    for t in range(TT):
                        for kt in range(KT):
                            last = mm(u.t[:, t * 16:(t + 1) * 16], HT[:, kt, tile(t)], w[:, kt, :],
                                      start=kt == 0, stop=kt == KT - 1)
                    last.then_inc(u.filled, 1)
                elif kind == "score":
                    t, h = divmod(step[1], HEADS)
                    keys = slice(P, 4 * P) if t else slice(0, P)
                    if step[1] == 0:
                        pe.wait_ge(rope_done, l + 1)
                        pe.wait_ge(cache_in, l * 32 + 32)
                    for m in range(2):
                        u = use(here, step, m)
                        pe.wait_ge(u.drained, u.before)
                        half = slice(64 * m, 64 * m + 64)
                        mm(u.t[:, 0:keys.stop - keys.start], QT[half, h, tile(t)], KTT[half, h, keys],
                           start=True, stop=True).then_inc(u.filled, 1)
                elif kind == "turn":
                    i = step[1]
                    u = use(here, step)
                    pe.wait_ge(probs_ready, l * (TT * HEADS) + (i + 1))
                    pe.wait_ge(u.drained, u.before)
                    for b in range(3 if i // HEADS else 1):
                        last = turn(u.t[:, tile(b)], PR[:, i % 2, 0, tile(b)], ident)
                    last.then_inc(u.filled, 1)
                elif kind == "value":
                    i = step[1]
                    t, h = divmod(i, HEADS)
                    u = use(here, ("value", t * HEADS))
                    if h == 0:
                        pe.wait_ge(u.drained, u.before)
                    if i == 0:
                        for semaphore, value in drains([use(here, ("v", s)) for s in range(TT)]):
                            pe.wait_ge(semaphore, value)
                    p = use(here, ("turn", i))
                    pe.wait_ge(p.drained, p.after)
                    head = slice(h * P, (h + 1) * P)
                    vs = [VC[:, head], V[:, 1, head], V[:, 2, head]] if t else [V[:, 0, head]]
                    for b, v in enumerate(vs):
                        last = mm(u.t[:, head], PT[:, i % 2, tile(b)], v, start=b == 0, stop=b == len(vs) - 1)
                    if h == HEADS - 1:
                        last.then_inc(u.filled, 1)
                elif kind == "y_turn":
                    n, t = step[1:]
                    u = use(here, step)
                    if n == 0:
                        y = use(here, ("value", t * HEADS))
                        pe.wait_ge(y.drained, y.after)
                    else:
                        pe.wait_ge(y_ready, l * 6 + ((n - 1) * TT + t + 1))
                    pe.wait_ge(u.drained, u.before)
                    for j in range(4):
                        last = turn(u.t[:, tile(j)], YTILE[:, (n * TT + t) % 2, tile(j)], ident)
                    last.then_inc(u.filled, 1)
                elif kind == "merge":
                    n, d = step[1:]
                    proj = use(here, step)
                    w = chunk(l, ("branch", 2 * n + d // 4), kt=4)
                    if d == 0:
                        for semaphore, value in drains([use(here, ("y_turn", n, t)) for t in range(TT)]):
                            pe.wait_ge(semaphore, value)
                    pe.wait_ge(proj.drained, proj.before)
                    for kt in range(4):
                        last = mm(proj.t[:, 0:N], w[:, kt, (d % 4) * P:(d % 4 + 1) * P], YT[:, kt, :],
                                  start=kt == 0, stop=kt == 3)
                    last.then_inc(proj.filled, 1)
                elif kind == "gate":
                    n, d = step[1:]
                    u = use(here, step)
                    w = chunk(l, ("gate", 2 * n + d // 4))
                    pe.wait_ge(u.drained, u.before)
                    to_channels(u, w, d % 4)
                elif kind in ("acum", "bcum"):
                    u = use(here, step)
                    w, src = (8, DTV[:, 3, :]) if kind == "acum" else (4, LFF)
                    pe.wait_ge(*((dta_ready, l + 1) if kind == "acum" else (lf_ready, l + 1)))
                    pe.wait_ge(u.drained, u.before)
                    for x in range(2 * TT):
                        mm(u.t[:, x * w:(x + 1) * w], TRI[x % 2], src[:, x * w:(x + 1) * w], start=True, stop=True)
                    mm(u.t[:, 6 * w:12 * w], ones, src, start=True, stop=True).then_inc(u.filled, 1)
                elif kind == "xs_turn":
                    t = step[1]
                    u = use(here, step)
                    pe.wait_ge(conv_done, l * 6 + 6)
                    pe.wait_ge(u.drained, u.before)
                    for j in range(4):
                        last = turn(u.t[:, tile(j)], CX[:, j, OFF[t]:OFF[t] + P], ident)
                    last.then_inc(u.filled, 1)
                elif kind == "b_turn":
                    t = step[1]
                    u = use(here, step)
                    pe.wait_ge(u.drained, u.before)
                    at = slice(OFF[t], OFF[t] + P)
                    turn(u.t[:, 0:P], CX[:, 4, at], ident)
                    for g in range(2):
                        half = slice(64 * g, 64 * g + 64)
                        if g:
                            row_fence()
                        last = mm(u.t[:, tile(1 + g)], CX[half, 4, at], CX[half, 5, at], start=True, stop=True)
                    last.then_inc(u.filled, 1)
                elif kind == "state":
                    t, _ = STATES[step[1]]
                    u = use(here, step)
                    pe.wait_ge(xw_ready, l * 4 + (step[1] + 1))
                    turned = [use(here, ("b_turn", s)) for s in range(TT)] if step[1] == 0 else []
                    for semaphore, value in drains(turned, [u]):
                        pe.wait_ge(semaphore, value)
                    for g in range(2):
                        last = mm(u.t[64 * g:64 * g + 64, 0:256], BTK[:, t, 64 * g:64 * g + 64],
                                  XWT[:, g * 256:(g + 1) * 256], start=True, stop=True)
                    last.then_inc(u.filled, 1)
                elif kind == "decay":
                    t, g = step[1:]
                    pe.wait_ge(ac_ready, l + 1)
                    for d in range(2):
                        u = use(here, step, d)
                        pe.wait_ge(u.drained, u.before)
                        c = t * 16 + d * 8 + g * 4
                        spread(u, [DT3[:, 0, c + h:c + h + 1] for h in range(4)])
                elif kind == "diag":
                    t, g = step[1:]
                    u = use(here, ("diag", t, 0))
                    if g == 0:
                        pe.wait_ge(u.drained, u.before)
                        pe.wait_ge(xd_ready, l * TT + (t + 1))
                    pe.wait_ge(m_ready, l * 18 + ((t * 2 + g) * 2 + 2))
                    for h in range(4):
                        head = slice((g * 4 + h) * 64, (g * 4 + h) * 64 + 64)
                        for d in range(2):
                            last = mm(u.t[:, head], EB[:, g, d, tile(h)], XD[:, d, head], start=d == 0, stop=d == 1)
                    if g == 1:
                        last.then_inc(u.filled, 1)
                elif kind == "off":
                    t, d = step[1:]
                    u = use(here, step)
                    if (t, d) in ((1, 0), (2, 1)):
                        pe.wait_ge(ssm_in, l * 16 + 16)
                        state, closed = HS, []
                    else:
                        state, closed = HC, [use(here, ("state", 2 + d))]
                    for semaphore, value in drains(closed, [u]):
                        pe.wait_ge(semaphore, value)
                    for g in range(2):
                        half = slice(64 * g, 64 * g + 64)
                        if g:
                            row_fence()
                        last = mm(u.t[:, g * 256:(g + 1) * 256], CX[half, 5, OFF[t]:OFF[t] + P], state[half, d, :],
                                  start=True, stop=True)
                    last.then_inc(u.filled, 1)
                elif kind == "k_turn":
                    t = step[1]
                    u = use(here, step)
                    keys = [use(here, ("mq", j)) for j in (2, 3)] if t == 0 else []
                    for semaphore, value in drains(keys, [u]):
                        pe.wait_ge(semaphore, value)
                    for j in range(2):
                        last = turn(u.t[:, tile(j)], MK[:, j, tile(t)], ident)
                    last.then_inc(u.filled, 1)
                elif kind in ("urow", "erow"):
                    t, d = step[1:]
                    u = use(here, step)
                    pe.wait_ge(*((u_ready, l + 1) if kind == "urow" else (stab_ready, l + 1)))
                    pe.wait_ge(u.drained, u.before)
                    src = UU if kind == "urow" else NRR
                    c = t * 8 + d * 4
                    spread(u, [src[:, c + h:c + h + 1] for h in range(4)])
                elif kind == "cstate":
                    i = step[1]
                    t, d = STATES[i]
                    u = use(here, step)
                    pe.wait_ge(kw_ready, l * 4 + (i + 1))
                    values = [use(here, ("mv", s)) for s in range(TT)] if i == 0 else []
                    for semaphore, value in drains(values, [u]):
                        pe.wait_ge(semaphore, value)
                    for h in range(HEADS):
                        half, at = slice(64 * (h % 2), 64 * (h % 2) + 64), (h // 2) * 130
                        k = KW[:, h * 64:(h + 1) * 64]
                        last = mm(u.t[half, at:at + P + 1], k, MV[:, t, h, :], start=True, stop=True)
                    last.then_inc(u.filled, 1)
                elif kind == "qk":
                    t = step[1]
                    u = use(here, step)
                    pe.wait_ge(u.drained, u.before)
                    for h in (0, 2, 1, 3):
                        half = slice(64 * (h % 2), 64 * (h % 2) + 64)
                        if h == 1:
                            row_fence()
                        last = mm(u.t[:, tile(h)], MK[half, h // 2, tile(t)], MQ[half, h // 2, tile(t)],
                                  start=True, stop=True)
                    last.then_inc(u.filled, 1)
                elif kind == "num":
                    t, d = step[1:]
                    pe.wait_ge(m_ready, l * 18 + (12 + t * 2 + d + 1))
                    for k in range(2):
                        u = use(here, step, k)
                        pe.wait_ge(u.drained, u.before)
                        for h in (2 * k, 2 * k + 1):
                            at = h % 2 * 256
                            last = mm(u.t[:, at:at + P + 1], EB[:, t % 2, d, tile(h)], MV[:, t, h, :], start=True, stop=True)
                        last.then_inc(u.filled, 1)
                    if t:
                        banks = [use(here, step, 2), use(here, step, 3)]
                        if (t, d) in ((1, 0), (2, 1)):
                            pe.wait_ge(c0_in, l * 16 + 16)
                            state, closed = CS, []
                        else:
                            state, closed = CC, [use(here, ("cstate", 2 + d))]
                        for semaphore, value in drains(closed, banks):
                            pe.wait_ge(semaphore, value)
                        for k in range(2):
                            half = slice(64 * k, 64 * k + 64)
                            for pair in range(2):
                                last = mm(banks[k].t[:, pair * 256:pair * 256 + P + 1], MQ[half, pair, tile(t)],
                                          state[half, d, pair, :], start=True, stop=True)
                            last.then_inc(banks[k].filled, 1)
                elif kind == "out":
                    d = step[1]
                    u = use(here, step)
                    w = chunk(l, ("out", d // 4))
                    pe.wait_ge(merged, l * 16 + 16)
                    pe.wait_ge(u.drained, u.before)
                    to_channels(u, w, d % 4, MG)
                elif kind == "h_turn":
                    t, f = step[1:]
                    u = use(here, step)
                    pe.wait_ge(h_ready, l * 2 + 2)
                    pe.wait_ge(u.drained, u.before)
                    for j in range(4):
                        last = turn(u.t[:, tile(j)], HT[:, f * 4 + j, tile(t)], ident)
                    last.then_inc(u.filled, 1)
                elif kind == "rank":
                    rank(use(here, step), step[1], l * (GROUPS + 1) + 1)
                elif kind == "router":
                    u = use(here, step)
                    rw = col("router").rearrange("p (k e) -> p k e", k=KT)
                    pe.wait_ge(u.drained, u.before)
                    for t in range(TT):
                        for kt in range(KT):
                            last = mm(u.t[:, t * EXPERTS:(t + 1) * EXPERTS], HT[:, kt, tile(t)], rw[:, kt, :],
                                      start=kt == 0, stop=kt == KT - 1)
                    last.then_inc(u.filled, 1)

            def rank(u, j, turns):
                pe.wait_ge(ag_ready, turns)
                pe.wait_ge(u.drained, u.before)
                spread(u, [AG[:, t, j:j + 1] for t in range(TT)])

            def group_step(l, g, step):
                kind = step[0]
                if kind == "next_rank":
                    rank(use(here, step), step[1], l * (GROUPS + 1) + g + 2)
                elif kind == "gather":
                    a = step[1]
                    u = use(here, step)
                    pe.wait_ge(picked, l * ((GROUPS + 1) * GE) + g * GE + GE)
                    turned = [use(here, ("h_turn", t, f)) for t in range(TT) for f in range(2)] if a == 0 else []
                    for semaphore, value in drains(turned, [u]):
                        pe.wait_ge(semaphore, value)
                    for k in range(4):
                        for t in (1, 2) if a < 2 else (0,):
                            last = mm(u.t[:, tile(k)], H2[:, t, tile(a % 2 * 4 + k)], PO[:, t, :],
                                      start=t < 2, stop=t != 1)
                    last.then_inc(u.filled, 1)
                elif kind == "g_turn":
                    u = use(here, step)
                    pe.wait_ge(u.drained, u.before)
                    for t in range(TT):
                        last = turn(u.t[:, tile(t)], GO[:, t, :], ident)
                    last.then_inc(u.filled, 1)
                elif kind == "up":
                    j, half = step[1:]
                    if j == 0 and half == 0:
                        for semaphore, value in drains([use(here, ("gather", a)) for a in range(4)]):
                            pe.wait_ge(semaphore, value)
                    for k in range(2):
                        u = use(here, step, k)
                        w = expert_chunk(l, g, j * 6 + half * 2 + k)
                        pe.wait_ge(u.drained, u.before)
                        for kt in range(KT):
                            for c in range(2):
                                last = mm(u.t[64 * c:64 * c + 64, 0:256], XE[:, kt, j, :], w[:, kt, c * 256:(c + 1) * 256],
                                          start=kt == 0, stop=kt == KT - 1)
                        last.then_inc(u.filled, 1)
                elif kind == "hid_turn":
                    j = step[1]
                    u = use(here, step)
                    for semaphore, value in drains([use(here, ("up", j, x), 1) for x in range(2)]):
                        pe.wait_ge(semaphore, value)
                    pe.wait_ge(u.drained, u.before)
                    for x in range(4):
                        last = turn(u.t[:, tile(x)], HH[:, x // 2, tile(x % 2)], ident)
                    last.then_inc(u.filled, 1)
                elif kind == "down":
                    j, half = step[1:]
                    u = use(here, step)
                    w = expert_chunk(l, g, j * 6 + 4 + half)
                    hid = use(here, ("hid_turn", j))
                    pe.wait_ge(hid.drained, hid.after)
                    pe.wait_ge(u.drained, u.before)
                    for f in range(KT):
                        row = f // 4 * 4 + f % 2 * 2 + f // 2 % 2
                        for c in range(2):
                            last = mm(u.t[64 * c:64 * c + 64, 0:256], HIDT[:, j % 2, f, :], w[:, row, c * 256:(c + 1) * 256],
                                      start=f == 0, stop=f == KT - 1)
                    last.then_inc(u.filled, 1)
                elif kind == "scatter":
                    d = step[1]
                    u = use(here, step)
                    if d == 0:
                        for half in range(2):
                            y = use(here, ("down", GE - 1, half))
                            pe.wait_ge(y.drained, y.after)
                        x = use(here, ("g_turn",))
                        pe.wait_ge(x.drained, x.after)
                    pe.wait_ge(u.drained, u.before)
                    mm(u.t[:, 0:P], YEC[:, tile(d)], GT[:, 0, :], start=True, stop=True)
                    mm(u.t[:, P:N], YES[:, tile(d)], GT[:, 1:3, :], start=True, stop=True).then_inc(u.filled, 1)

            pe.wait_ge(consts_in, 48)
            with pe.Fori(0, DEPTH) as l:
                here.layer, here.part = l, "layer"
                for step in STEPS:
                    mixer_step(l, step)
                with pe.Fori(0, GROUPS) as g:
                    here.group, here.part = g, "group"
                    for step in GROUP_STEPS:
                        group_step(l, g, step)
            here.part = "end"
            norm(DEPTH, 0, 2)

        @block.scalar
        def _(act):
            here = Place()
            fn = nc.scalar.activation
            fence = nc.scalar.drain

            def copy(out, in_, scale=1.0):
                return fn(out, in_, ACT.Copy, scale=scale)

            def norm(l, i, name, shift):
                if name != 1:
                    act.wait_ge(layer_done, l + 1)
                for kt in range(KT):
                    if name == 1:
                        x = use(here, ("out", kt))
                        act.wait_ge(x.drained, x.after)
                    fn(HT[:, kt, :], XT[:, kt, :], ACT.Square).then_inc(squares, 1)
                u = use(here, ("norm", name))
                act.wait_ge(u.filled, u.after)
                fn(RS[:, :], u.t[:, 0:N], ACT.Ln, bias=eps, scale=1.0 / D).then_inc(u.drained, 1)
                fence()
                fn(RS[:, :], RS[:, :], ACT.Exp, scale=-0.5).then_inc(rstd_ready, 1)
                if shift is None:
                    return
                for kt in range(KT):
                    for v, a, b in SEGS:
                        act.wait_ge(scaled, l * (4 * KT) + (i * 2 * KT + kt * 2 + v + 1))
                        last = fn(HT[:, kt, a:b], HT[:, kt, a:b], ACT.Identity, bias=MOD[:, shift, kt, v:v + 1])
                last.then_inc(h_ready, 1)

            def rstd(sums, width):
                fence()
                fn(sums, sums, ACT.Ln, bias=eps, scale=1.0 / width)
                fence()
                return fn(sums, sums, ACT.Exp, scale=-0.5)

            def tile_free(l, n, t):
                i = n * TT + t
                if i >= 2:
                    x = use(here, ("y_turn", (i - 2) // TT, (i - 2) % TT))
                    act.wait_ge(x.filled, x.after)

            def mixer_step(l, step):
                kind = step[0]
                if kind == "norm":
                    norm(l, step[1], step[1], 0 if step[1] == 0 else 3)
                elif kind == "q":
                    u = use(here, step)
                    if step[1] == 0:
                        act.wait_ge(arena_free, l + 1)
                    act.wait_ge(u.filled, u.after)
                    copy(QT[:, step[1], :], u.t[:, 0:N], 0.125).then_inc(u.drained, 1)
                elif kind == "k":
                    u = use(here, step)
                    act.wait_ge(u.filled, u.after)
                    copy(KTT[:, step[1], 0:P], u.t[:, 0:P])
                    copy(KTT[:, step[1], 2 * P:4 * P], u.t[:, P:N]).then_inc(u.drained, 1)
                elif kind == "v":
                    u = use(here, step)
                    act.wait_ge(u.filled, u.after)
                    copy(V[:, step[1], :], u.t[:, :]).then_inc(u.drained, 1)
                    if step[1] == 0:
                        act.wait_ge(lam_sums, l + 1)
                        fn(LAM[:, 2:4], LAM[:, 0:2], ACT.Exp).then_inc(lam_exps, 1)
                elif kind == "score":
                    i = step[1]
                    nk = N if i // HEADS else P
                    for m in range(2):
                        u = use(here, step, m)
                        act.wait_ge(maxes, l * (2 * TT * HEADS) + (2 * i + m + 1))
                        fn(PR[:, i % 2, m, 0:nk], u.t[:, 0:nk], ACT.Exp, bias=NMX[:, i % 2, m:m + 1],
                           accum_out=SMX[:, i % 2, m:m + 1]).then_inc(u.drained, 1)
                elif kind == "turn":
                    i = step[1]
                    u = use(here, step)
                    nk = N if i // HEADS else P
                    act.wait_ge(u.filled, u.after)
                    copy(PT[:, i % 2, 0:nk], u.t[:, 0:nk]).then_inc(u.drained, 1)
                elif kind == "att_y":
                    t = step[1]
                    u = use(here, ("value", t * HEADS))
                    tile_free(l, 0, t)
                    act.wait_ge(u.filled, u.after)
                    for h in range(HEADS):
                        fn(YTILE[:, t % 2, tile(h)], u.t[:, tile(h)], ACT.Square, accum_out=ST4[:, 0, h:h + 1])
                    rstd(ST4[:, 0, :], P).then_inc(y_rstd, 1)
                elif kind == "y_turn":
                    n, t = step[1:]
                    if n and t == 0:
                        for d in (KT - 2, KT - 1):
                            x = use(here, ("merge", n - 1, d))
                            act.wait_ge(x.filled, x.after)
                    u = use(here, step)
                    act.wait_ge(u.filled, u.after)
                    copy(YT[:, :, tile(t)], u.t[:, :].rearrange("p (j c) -> p j c", j=4)).then_inc(u.drained, 1)
                elif kind == "gate":
                    n, d = step[1:]
                    u = use(here, step)
                    if n:
                        x = use(here, ("merge", n - 1, d))
                        act.wait_ge(x.drained, x.after)
                    act.wait_ge(u.filled, u.after)
                    fn(GB[:, d, :], u.t[:, 0:N], ACT.Identity, bias=col("b_gate")[:, n * KT + d:n * KT + d + 1]
                       ).then_inc(u.drained, 1)
                elif kind == "merge":
                    d = step[2]
                    if d == 0:
                        fence()
                    fn(GB[:, d, :], GB[:, d, :], ACT.Sigmoid).then_inc(gate_sigmoid, 1)
                elif kind == "z":
                    u = use(here, step)
                    act.wait_ge(u.filled, u.after)
                    copy(Z[:, step[1], :], u.t[:, :]).then_inc(u.drained, 1)
                elif kind == "z_sig":
                    x = use(here, ("ada_turn", 11))
                    act.wait_ge(x.filled, x.after)
                    for t in range(TT):
                        fn(EB[:, t // 2, t % 2, :], Z[:, t, :], ACT.Sigmoid).then_inc(z_sigmoid, 1)
                elif kind == "mo_sig":
                    fence()
                    for t in range(TT):
                        last = fn(MO[:, t, :], MO[:, t, :], ACT.Sigmoid)
                    last.then_inc(o_sigmoid, 1)
                elif kind == "x":
                    j = step[1]
                    u = use(here, step)
                    act.wait_ge(u.filled, u.after)
                    copy(XB[:, j, 1:P + 1], u.t[:, 0:P])
                    copy(XB[:, j, P + 2:XW - 1], u.t[:, P:N]).then_inc(u.drained, 1)
                elif kind == "dt":
                    fn(EXPA[:, :], row("a_log"), ACT.Exp).then_inc(a_exp, 1)
                    act.wait_ge(dt_abs, l + 1)
                    fn(DTV[:, 1, :], DTV[:, 1, :], ACT.Exp, scale=-1.0)
                    fence()
                    fn(DTV[:, 1, :], DTV[:, 1, :], ACT.Ln, bias=1.0).then_inc(dt_ln, 1)
                elif kind == "conv":
                    j = step[1]
                    if j < 6:
                        act.wait_ge(conved, l * 6 + (j + 1))
                        fn(XB[:, j, 0:XW - 2], CX[:, j, 0:XW - 2], ACT.Sigmoid).then_inc(conv_sigmoid, 1)
                elif kind == "acum":
                    act.wait_ge(ac_ready, l + 1)
                    fn(EX3[:, :, :], DT3[:, :, :], ACT.Exp).then_inc(ac_exp, 1)
                elif kind == "xs_turn":
                    t = step[1]
                    u = use(here, step)
                    act.wait_ge(u.filled, u.after)
                    copy(XS[:, t, :], u.t[:, :]).then_inc(u.drained, 1)
                elif kind == "b_turn":
                    t = step[1]
                    u = use(here, step)
                    act.wait_ge(u.filled, u.after)
                    copy(BTK[:, t, :], u.t[:, 0:P])
                    copy(CB[:, t, :], u.t[:, P:N]).then_inc(u.drained, 1)
                elif kind == "decay":
                    t, g = step[1:]
                    for d in range(2):
                        u = use(here, step, d)
                        act.wait_ge(u.drained, u.after)
                        fn(EB[:, g, d, :], EB[:, g, d, :], ACT.Exp).then_inc(e_exp, 1)
                elif kind in ("mb_y", "ml_y"):
                    t = step[1]
                    n, parts = (1, 1) if kind == "mb_y" else (2, HEADS)
                    i = n * TT + t
                    tile_free(l, n, t)
                    act.wait_ge(y_sum, l * 6 + (i - TT + 1))
                    w = 512 // parts
                    for h in range(parts):
                        fn(YTILE[:, i % 2, h * w:(h + 1) * w], TMP[:, h * w:(h + 1) * w], ACT.Square,
                           accum_out=ST4[:, 0, h:h + 1])
                    rstd(ST4[:, 0, 0:parts], w).then_inc(y_rstd, 1)
                elif kind == "mq":
                    j = step[1]
                    u = use(here, step)
                    if j == 0:
                        act.wait_ge(k_out, l * 16 + 16)
                        act.wait_ge(v_out, l * 16 + 16)
                    act.wait_ge(u.filled, u.after)
                    if j < 2:
                        copy(MQ[:, j, :], u.t[:, 0:N]).then_inc(u.drained, 1)
                    else:
                        copy(MK[:, j - 2, :], u.t[:, 0:N], 0.125).then_inc(u.drained, 1)
                elif kind == "mv":
                    u = use(here, step)
                    act.wait_ge(u.filled, u.after)
                    copy(MV[:, step[1], :, P:P + 1], ones[:, 0:HEADS].unsqueeze(2))
                    copy(MV[:, step[1], :, 0:P], u.t[:, :].rearrange("p (h c) -> p h c", h=HEADS)).then_inc(u.drained, 1)
                elif kind == "mo":
                    u = use(here, step)
                    act.wait_ge(u.filled, u.after)
                    copy(MO[:, step[1], :], u.t[:, :]).then_inc(u.drained, 1)
                elif kind == "if":
                    act.wait_ge(lf_abs, l + 1)
                    fn(LAB, LAB, ACT.Exp, scale=-1.0)
                    fence()
                    fn(LAB, LAB, ACT.Ln, bias=1.0).then_inc(lf_ln, 1)
                elif kind == "k_turn":
                    t = step[1]
                    u = use(here, step)
                    act.wait_ge(u.filled, u.after)
                    copy(MKTOK[:, t, :], u.t[:, 0:2 * P]).then_inc(u.drained, 1)
                elif kind == "stab":
                    act.wait_ge(stab_ready, l + 1)
                    fn(MEXP[:, :, :], MARG[:, :, :], ACT.Exp).then_inc(stab_exp, 1)
                elif kind == "qk":
                    t = step[1]
                    u = use(here, step)
                    act.wait_ge(u.filled, u.after)
                    if t:
                        act.wait_ge(m_ready, l * 18 + (12 + 2 * t))
                    copy(QK, u.t[:, :]).then_inc(u.drained, 1)
                elif kind == "erow":
                    t, d = step[1:]
                    u = use(here, step)
                    act.wait_ge(u.drained, u.after)
                    fn(EB[:, t % 2, d, :], EB[:, t % 2, d, :], ACT.Exp, scale=-1.0).then_inc(e_exp, 1)
                elif kind == "h_turn":
                    t, f = step[1:]
                    u = use(here, step)
                    if t == 0 and f == 0:
                        act.wait_ge(ssm_out, l * 16 + 16)
                    act.wait_ge(u.filled, u.after)
                    copy(H2[:, t, f * 512:(f + 1) * 512], u.t[:, :]).then_inc(u.drained, 1)
                elif kind == "router":
                    u = use(here, step)
                    act.wait_ge(u.drained, u.after)
                    fn(AFF[:, :, 0:EXPERTS], AFF[:, :, 0:EXPERTS], ACT.Exp).then_inc(aff_exp, 1)

            def group_step(l, g, step):
                kind = step[0]
                if kind == "gather":
                    a = step[1]
                    u = use(here, step)
                    act.wait_ge(u.filled, u.after)
                    first, k = (0 if a < 2 else CAP_S), a % 2 * 4
                    copy(XE[:, k:k + 4, :, first:first + CAP_S].rearrange("p k e c -> p (k e) c"),
                         u.t[:, :].rearrange("p (x c) -> p x c", c=CAP_S)).then_inc(u.drained, 1)
                elif kind == "g_turn":
                    u = use(here, step)
                    act.wait_ge(u.filled, u.after)
                    copy(GT[:, :, :], u.t[:, 0:N].rearrange("p (t c) -> p t c", t=TT)).then_inc(u.drained, 1)
                elif kind == "up":
                    j, half = step[1:]
                    u = use(here, step, 0)
                    act.wait_ge(u.filled, u.after)
                    fn(SGE[:, half, :], u.t[:, 0:256], ACT.Sigmoid).then_inc(hid_sigmoid, 1)
                elif kind == "hid_turn":
                    u = use(here, step)
                    act.wait_ge(u.filled, u.after)
                    copy(HIDT[:, step[1] % 2, :, :], u.t[:, :].rearrange("p (f c) -> p f c", c=SLOTS)).then_inc(u.drained, 1)
                elif kind == "down":
                    j, half = step[1:]
                    u = use(here, step)
                    act.wait_ge(u.filled, u.after)
                    rows = slice(32 * j, 32 * j + 32)
                    for c in range(2):
                        at = slice(half * 512 + c * 256, half * 512 + c * 256 + 256)
                        copy(YES[rows, at], u.t[64 * c:64 * c + 32, 0:256])
                        last = copy(YEC[rows, at], u.t[64 * c + 32:64 * c + 64, 0:256])
                    last.then_inc(u.drained, 1)

            act.wait_ge(consts_in, 48)
            fn(LAM[:, 0:2 * KT].rearrange("p (k v) -> p k v", v=2), CVEC[:, :, :], ACT.Sigmoid).then_inc(c_sigmoid, 1)
            with act.Fori(0, DEPTH) as l:
                here.layer, here.part = l, "layer"
                act.wait_ge(small_in, l * 32 + 32)
                for step in STEPS:
                    mixer_step(l, step)
                    if step[0] in ACT_STEPS:
                        fence()
                with act.Fori(0, GROUPS) as g:
                    here.group, here.part = g, "group"
                    for step in GROUP_STEPS:
                        group_step(l, g, step)
                        if step[0] in ACT_STEPS:
                            fence()
            here.part = "end"
            norm(DEPTH, 0, 2, None)

        @block.vector
        def _(dve):
            here = Place()
            ve = nc.vector
            tt, ts, stt = ve.tensor_tensor, ve.tensor_scalar, ve.scalar_tensor_tensor
            fence = ve.drain

            def over(ap, n):
                return ap.unsqueeze(2).to_broadcast([ap.shape[0], ap.shape[1], n])

            def norm(l, i, name, scale):
                dve.wait_ge(rstd_ready, l * 2 + (i + 1))
                for kt in range(KT):
                    if scale is None:
                        stt(HT[:, kt, :], XT[:, kt, :], col("final")[:, kt:kt + 1], RS[:, :], ALU.mult,
                            ALU.mult).then_inc(y_final, 1)
                        continue
                    for v, a, b in SEGS:
                        stt(HT[:, kt, a:b], XT[:, kt, a:b], AMOD[:, scale, kt, v:v + 1], RS[:, a:b], ALU.mult,
                            ALU.mult).then_inc(scaled, 1)

            def rotate(x, rot):
                cos = const("cos").unsqueeze(1).to_broadcast([P, HEADS, NS])
                sin = const("sin").unsqueeze(1).to_broadcast([P, HEADS, NS])
                ve.stream_shuffle(rot, x, [(k + 16) % 32 for k in range(32)])
                fence()
                tt(x, x, cos, ALU.mult)
                tt(rot, rot, sin, ALU.mult)
                fence()
                return tt(x, x, rot, ALU.add)

            def mixer_step(l, step):
                kind = step[0]
                if kind == "ada":
                    c = step[1]
                    u = use(here, step)
                    dve.wait_ge(u.filled, u.after)
                    ve.tensor_copy(EB[:, 0, 0, tile(c % 2)], u.t[:, 0:P]).then_inc(u.drained, 1)
                elif kind == "ada_turn":
                    c = step[1]
                    u = use(here, step)
                    dve.wait_ge(u.filled, u.after)
                    half = c % 2 * 4
                    tt(MOD[:, c // 2, half:half + 4, :], u.t[:, 0:P].rearrange("p (j v) -> p j v", v=32)[:, :, 0:2],
                       over(col("ada_b")[:, c * 4:c * 4 + 4], 2), ALU.add).then_inc(u.drained, 1)
                    if c in (3, 9):
                        i = c // 6
                        fence()
                        stt(AMOD[:, i, :, :], MOD[:, c // 2, :, :], 1.0, over(col("n2" if i else "n1"), 2), ALU.add, ALU.mult)
                        fence()
                elif kind == "norm":
                    norm(l, step[1], step[1], step[1])
                elif kind == "rope":
                    for name in ("q", "k"):
                        for h in (HEADS - 2, HEADS - 1):
                            x = use(here, (name, h))
                            dve.wait_ge(x.drained, x.after)
                    lam = row("lam").rearrange("p (a b) -> p a b", a=4)
                    tt(TMP[:, 0:128].rearrange("p (a b) -> p a b", a=2), lam[:, 0:4:2, :], lam[:, 1:4:2, :], ALU.mult)
                    fence()
                    ve.tensor_reduce(LAM[:, 0:2], TMP[:, 0:128].rearrange("p (a b) -> p a b", a=2), AX.X,
                                     ALU.add).then_inc(lam_sums, 1)
                    ts(row("subln"), row("subln"), row("lam_rest"), None, ALU.mult)
                    rotate(QT[:, :, P:N], ROT)
                    fence()
                    rotate(KTT[:, :, 2 * P:4 * P], ROT).then_inc(rope_done, 1)
                elif kind == "v" and step[1] == TT - 1:
                    dve.wait_ge(lam_exps, l + 1)
                    tt(LAM[:, 4:5], LAM[:, 3:4], LAM[:, 2:3], ALU.subtract)
                    fence()
                    ts(LAM[:, 5:6], LAM[:, 4:5], row("lam_init"), None, ALU.subtract)
                elif kind == "score":
                    i = step[1]
                    nk = N if i // HEADS else P
                    for m in range(2):
                        u = use(here, step, m)
                        dve.wait_ge(u.filled, u.after)
                        ve.tensor_reduce(NMX[:, i % 2, m:m + 1], u.t[:, 0:nk], AX.X, ALU.max,
                                         negate=True).then_inc(maxes, 1)
                elif kind == "turn":
                    i = step[1]
                    nk = N if i // HEADS else P
                    for m in range(2):
                        s = use(here, ("score", i), m)
                        dve.wait_ge(s.drained, s.after)
                    ve.reciprocal(RCP[:, i % 2, :], SMX[:, i % 2, :])
                    fence()
                    ts(RCP[:, i % 2, 1:2], RCP[:, i % 2, 1:2], LAM[:, 5:6], None, ALU.mult)
                    ts(PR[:, i % 2, 0, 0:nk], PR[:, i % 2, 0, 0:nk], RCP[:, i % 2, 0:1], None, ALU.mult)
                    fence()
                    stt(PR[:, i % 2, 0, 0:nk], PR[:, i % 2, 1, 0:nk], RCP[:, i % 2, 1:2], PR[:, i % 2, 0, 0:nk],
                        ALU.mult, ALU.add).then_inc(probs_ready, 1)
                elif kind == "att_y":
                    t = step[1]
                    u = use(here, ("value", t * HEADS))
                    dve.wait_ge(y_rstd, l * 9 + (t + 1))
                    for h in range(HEADS):
                        last = stt(YTILE[:, t % 2, tile(h)], u.t[:, tile(h)], ST4[:, 0, h:h + 1], row("subln"),
                                   ALU.mult, ALU.mult)
                    last.then_inc(u.drained, 1)
                elif kind == "merge":
                    n, d = step[1:]
                    u = use(here, step)
                    dve.wait_ge(gate_sigmoid, l * (3 * KT) + (n * KT + d + 1))
                    dve.wait_ge(u.filled, u.after)
                    if n == 0:
                        tt(MG[:, d, :], GB[:, d, :], u.t[:, 0:N], ALU.mult).then_inc(u.drained, 1)
                    else:
                        tt(TMP[:, 0:N], GB[:, d, :], u.t[:, 0:N], ALU.mult).then_inc(u.drained, 1)
                        fence()
                        tt(MG[:, d, :], MG[:, d, :], TMP[:, 0:N], ALU.add).then_inc(merged, 1)
                elif kind == "z_sig":
                    for t in range(TT):
                        dve.wait_ge(z_sigmoid, l * TT + (t + 1))
                        tt(Z[:, t, :], Z[:, t, :], EB[:, t // 2, t % 2, :], ALU.mult)
                elif kind == "dt":
                    u = use(here, step)
                    dve.wait_ge(u.filled, u.after)
                    tt(DTV[:, 0, :].rearrange("p (t c) -> p t c", t=TT), u.t[:, 0:48].rearrange("p (t c) -> p t c", t=TT),
                       row("dt_b").unsqueeze(1).to_broadcast([P, TT, 16]), ALU.add).then_inc(u.drained, 1)
                    fence()
                    stt(DTV[:, 1, :], DTV[:, 0, :], -1.0, DTV[:, 0, :], ALU.mult, ALU.max).then_inc(dt_abs, 1)
                elif kind == "conv":
                    j = step[1]
                    w = col("conv_w").rearrange("p (k j) -> p k j", k=3)
                    n = XW - 2
                    if j == 0:
                        dve.wait_ge(dt_ln, l + 1)
                        stt(DTV[:, 2, :], DTV[:, 0, :], 0.0, DTV[:, 1, :], ALU.max, ALU.add)
                        fence()
                        dve.wait_ge(a_exp, l + 1)
                        stt(DTV[:, 3, :].rearrange("p (t c) -> p t c", t=TT), DTV[:, 2, :].rearrange("p (t c) -> p t c", t=TT),
                            -1.0, EXPA.unsqueeze(1).to_broadcast([P, TT, 16]), ALU.mult, ALU.mult).then_inc(dta_ready, 1)
                        for x in (4, 5):
                            v = use(here, ("x", x))
                            dve.wait_ge(v.drained, v.after)
                        for c in (0, P + 1, XW - 1):
                            ve.memset(XB[:, :, c:c + 1], 0.0)
                        fence()
                    if j < 6:
                        ts(CX[:, j, 0:n], XB[:, j, 1:1 + n], w[:, 1, j:j + 1], col("conv_b")[:, j:j + 1], ALU.mult, ALU.add)
                        fence()
                        stt(CX[:, j, 0:n], XB[:, j, 0:n], w[:, 0, j:j + 1], CX[:, j, 0:n], ALU.mult, ALU.add)
                        fence()
                        stt(CX[:, j, 0:n], XB[:, j, 2:2 + n], w[:, 2, j:j + 1], CX[:, j, 0:n], ALU.mult,
                            ALU.add).then_inc(conved, 1)
                    if j:
                        dve.wait_ge(conv_sigmoid, l * 6 + j)
                        tt(CX[:, j - 1, 0:n], CX[:, j - 1, 0:n], XB[:, j - 1, 0:n], ALU.mult).then_inc(conv_done, 1)
                elif kind == "acum":
                    u = use(here, step)
                    dve.wait_ge(u.filled, u.after)
                    ve.tensor_copy(DT3[:, 0, :], u.t[:, 0:48])
                    ve.tensor_copy(DT3[:, 2, :], u.t[:, 48:96]).then_inc(u.drained, 1)
                    fence()
                    tt(DT3[:, 1, :], DT3[:, 2, :], DT3[:, 0, :], ALU.subtract).then_inc(ac_ready, 1)
                    dve.wait_ge(ac_exp, l + 1)
                    tt(DTV[:, 1, :], DTV[:, 2, :], EX3[:, 1, :], ALU.mult)
                    fence()
                elif kind == "state":
                    i = step[1]
                    t, d = STATES[i]
                    x = use(here, ("xs_turn", t))
                    dve.wait_ge(x.drained, x.after)
                    c = t * 16 + d * 8
                    tt(XWT.rearrange("p (h c) -> p h c", h=8), XS[:, t, :].rearrange("p (h c) -> p h c", h=8),
                       over(DTV[:, 1, c:c + 8], 64), ALU.mult).then_inc(xw_ready, 1)
                    u = use(here, step)
                    if i >= 2:
                        dve.wait_ge(ssm_out, l * 16 + 16)
                        dve.wait_ge(ssm_in, l * 16 + 16)
                        for g in range(2):
                            half = slice(64 * g, 64 * g + 64)
                            tt(HC[half, d, :].rearrange("p (h c) -> p h c", h=4),
                               HS[half, d, :].rearrange("p (h c) -> p h c", h=4),
                               over(EX3[half, 2, c + 4 * g:c + 4 * g + 4], 64), ALU.mult)
                        fence()
                        dve.wait_ge(u.filled, u.after)
                        tt(HC[:, d, :], HC[:, d, :], u.t[:, 0:256], ALU.add).then_inc(u.drained, 1)
                    else:
                        dve.wait_ge(u.filled, u.after)
                        ve.tensor_copy(HC[:, d, :], u.t[:, 0:256]).then_inc(u.drained, 1)
                elif kind == "xd":
                    t = step[1]
                    for d in range(2):
                        last = tt(XD[:, d, :].rearrange("p (h c) -> p h c", h=8), XS[:, t, :].rearrange("p (h c) -> p h c", h=8),
                                  over(DTV[:, 2, t * 16 + d * 8:t * 16 + d * 8 + 8], 64), ALU.mult)
                    last.then_inc(xd_ready, 1)
                elif kind == "decay":
                    t, g = step[1:]
                    for d in range(2):
                        u = use(here, step, d)
                        dve.wait_ge(u.filled, u.after)
                        for h in range(4):
                            c = t * 16 + d * 8 + g * 4 + h
                            last = stt(EB[:, g, d, tile(h)], u.t[:, tile(h)], DT3[:, 0, c:c + 1], NEGT[d],
                                       ALU.subtract, ALU.add)
                        last.then_inc(u.drained, 1)
                elif kind == "diag":
                    t, g = step[1:]
                    for d in range(2):
                        dve.wait_ge(e_exp, l * 18 + ((t * 2 + g) * 2 + d + 1))
                        e = EB[:, g, d, :].rearrange("p (h c) -> p h c", h=4)
                        tt(e, e, CB[:, t, tile(g)].unsqueeze(1).to_broadcast([P, 4, P]), ALU.mult).then_inc(m_ready, 1)
                elif kind == "mb_y":
                    t = step[1]
                    u = use(here, ("diag", t, 0))
                    tt(TMP[:, :].rearrange("p (h c) -> p h c", h=8), XS[:, t, :].rearrange("p (h c) -> p h c", h=8),
                       over(row("mb_d"), 64), ALU.mult)
                    fence()
                    dve.wait_ge(u.filled, u.after)
                    tt(TMP[:, :], TMP[:, :], u.t[:, :], ALU.add).then_inc(u.drained, 1)
                    for d in range(2 if t else 0):
                        o = use(here, ("off", t, d))
                        dve.wait_ge(o.filled, o.after)
                        tt(XWT.rearrange("p (h c) -> p h c", h=8), o.t[:, :].rearrange("p (h c) -> p h c", h=8),
                           over(EX3[:, 0, t * 16 + d * 8:t * 16 + d * 8 + 8], 64), ALU.mult).then_inc(o.drained, 1)
                        fence()
                        tt(TMP[:, :], TMP[:, :], XWT, ALU.add)
                        fence()
                    fence()
                    tt(TMP[:, :], TMP[:, :], Z[:, t, :], ALU.mult).then_inc(y_sum, 1)
                    dve.wait_ge(y_rstd, l * 9 + (TT + t + 1))
                    stt(YTILE[:, (TT + t) % 2, :], TMP[:, :], ST4[:, 0, 0:1], row("mb_g"), ALU.mult,
                        ALU.mult).then_inc(y_ready, 1)
                    fence()
                elif kind == "if":
                    u = use(here, step)
                    dve.wait_ge(u.filled, u.after)
                    tt(PRE.rearrange("p (t c) -> p t c", t=TT), u.t[:, 0:48].rearrange("p (t c) -> p t c", t=TT),
                       row("gate_b").unsqueeze(1).to_broadcast([P, TT, 16]), ALU.add).then_inc(u.drained, 1)
                    fence()
                    f = PRE.rearrange("p (x k h) -> p k x h", k=2, h=4)[:, 1, :, :]
                    stt(LAB.rearrange("p (x h) -> p x h", h=4), f, -1.0, f, ALU.mult, ALU.max).then_inc(lf_abs, 1)
                elif kind == "bcum":
                    f = PRE.rearrange("p (x k h) -> p k x h", k=2, h=4)[:, 1, :, :]
                    i_ = PRE.rearrange("p (x k h) -> p k x h", k=2, h=4)[:, 0, :, :]
                    dve.wait_ge(lf_ln, l + 1)
                    stt(LFF.rearrange("p (x h) -> p x h", h=4), f, 0.0, LAB.rearrange("p (x h) -> p x h", h=4), ALU.min,
                        ALU.subtract).then_inc(lf_ready, 1)
                    u = use(here, step)
                    dve.wait_ge(u.filled, u.after)
                    ve.tensor_copy(BC, u.t[:, 0:24])
                    ve.tensor_copy(TB, u.t[:, 24:48]).then_inc(u.drained, 1)
                    fence()
                    tt(UU.rearrange("p (x h) -> p x h", h=4), i_, BC.rearrange("p (x h) -> p x h", h=4),
                       ALU.subtract).then_inc(u_ready, 1)
                elif kind == "urow":
                    t, d = step[1:]
                    u = use(here, step)
                    c = t * 8 + d * 4
                    dve.wait_ge(u.filled, u.after)
                    rows = u.t[:, :].rearrange("p (h c) -> p h c", h=4)
                    ve.tensor_reduce(UM[:, c:c + 4], rows, AX.X, ALU.max)
                    tmp = TMP[:, :].rearrange("p (h c) -> p h c", h=4)
                    fence()
                    tt(tmp, rows, NEGT[1 - d].unsqueeze(1).to_broadcast([P, 4, P]), ALU.add).then_inc(u.drained, 1)
                    fence()
                    ve.tensor_reduce(PM[:, c:c + 4], tmp, AX.X, ALU.max)
                elif kind == "stab":
                    m0 = row("m0")
                    ve.memset(MS[:, 0:8], 0.0)
                    ve.tensor_copy(MS[:, 8:12], m0[:, 0:4])
                    ve.tensor_copy(MS[:, 20:24], m0[:, 4:8])
                    fence()
                    tt(MXX[:, 8:12], MS[:, 8:12], UM[:, 8:12], ALU.max)
                    tt(MXX[:, 20:24], MS[:, 20:24], UM[:, 20:24], ALU.max)
                    fence()
                    tt(MS[:, 16:20], TB[:, 8:12], MXX[:, 8:12], ALU.add)
                    tt(MS[:, 12:16], TB[:, 20:24], MXX[:, 20:24], ALU.add)
                    fence()
                    tt(MXX, MS, UM, ALU.max)
                    tt(NRR, MS, PM, ALU.max)
                    fence()
                    tt(MARG[:, 0, :], MS, NRR, ALU.subtract)
                    tt(MARG[:, 1, :], MS, MXX, ALU.subtract)
                    tt(MARG[:, 2, :], UU, MXX, ALU.subtract)
                    stt(MARG[:, 3, :], BC, -1.0, NRR, ALU.mult, ALU.subtract)
                    tt(MNEW, TB, MXX, ALU.add).then_inc(stab_ready, 1)
                    dve.wait_ge(stab_exp, l + 1)
                elif kind == "cstate":
                    i = step[1]
                    t, d = STATES[i]
                    c = t * 8 + d * 4
                    x = use(here, ("k_turn", t))
                    dve.wait_ge(x.drained, x.after)
                    tt(KW.rearrange("p (h c) -> p h c", h=4), MKTOK[:, t, :].rearrange("p (h c) -> p h c", h=4),
                       over(MEXP[:, 2, c:c + 4], 64), ALU.mult).then_inc(kw_ready, 1)
                    u = use(here, step)
                    new = u.t[:, 0:260].rearrange("p (a b) -> p a b", a=2)[:, :, 0:P + 1]
                    if i < 2:
                        dve.wait_ge(u.filled, u.after)
                        ve.tensor_copy(CC[:, d, :, :], new).then_inc(u.drained, 1)
                    else:
                        dve.wait_ge(c_out, l * 16 + 16)
                        dve.wait_ge(c0_in, l * 16 + 16)
                        dve.wait_ge(u.filled, u.after)
                        for h in range(HEADS):
                            half = slice(64 * (h % 2), 64 * (h % 2) + 64)
                            last = stt(CC[half, d, h // 2, :], CS[half, d, h // 2, :], MEXP[half, 1, c + h:c + h + 1],
                                       new[half, h // 2, :], ALU.mult, ALU.add)
                        last.then_inc(u.drained, 1)
                elif kind == "erow":
                    t, d = step[1:]
                    u = use(here, step)
                    dve.wait_ge(u.filled, u.after)
                    for h in range(4):
                        c = t * 8 + d * 4 + h
                        last = stt(EB[:, t % 2, d, tile(h)], u.t[:, tile(h)], UU[:, c:c + 1], NEGT[d],
                                   ALU.subtract, ALU.subtract)
                    last.then_inc(u.drained, 1)
                    if d == 1:
                        q = use(here, ("qk", t))
                        dve.wait_ge(q.drained, q.after)
                        for x in range(2):
                            dve.wait_ge(e_exp, l * 18 + (12 + t * 2 + x + 1))
                            tt(EB[:, t % 2, x, :], EB[:, t % 2, x, :], QK, ALU.mult).then_inc(m_ready, 1)
                elif kind == "num":
                    t, d = step[1:]
                    c = t * 8 + d * 4
                    ha = HA.rearrange("p (h c) -> p h c", h=4)
                    if t:
                        for k in range(2):
                            u = use(here, step, 2 + k)
                            dve.wait_ge(u.filled, u.after)
                            x = u.t[:, :].rearrange("p (a c) -> p a c", a=2)[:, :, 0:P + 1]
                            tt(ha[:, k:4:2, 0:P + 1], x, over(MEXP[:, 0, c + k:c + 4:2], P + 1), ALU.mult).then_inc(u.drained, 1)
                        fence()
                    for k in range(2):
                        u = use(here, step, k)
                        dve.wait_ge(u.filled, u.after)
                        x = u.t[:, :].rearrange("p (a c) -> p a c", a=2)[:, :, 0:P + 1]
                        if t:
                            tt(ha[:, 2 * k:2 * k + 2, 0:P + 1], ha[:, 2 * k:2 * k + 2, 0:P + 1], x, ALU.add).then_inc(u.drained, 1)
                        else:
                            ve.tensor_copy(ha[:, 2 * k:2 * k + 2, 0:P + 1], x).then_inc(u.drained, 1)
                    fence()
                    den = ha[:, :, P]
                    stt(DEN[:, 4:8], den, -1.0, den, ALU.mult, ALU.max)
                    fence()
                    tt(DEN[:, 4:8], DEN[:, 4:8], MEXP[:, 3, c:c + 4], ALU.max)
                    fence()
                    ve.reciprocal(DEN[:, 0:4], DEN[:, 4:8])
                    fence()
                    tmp = TMP[:, :].rearrange("p (h c) -> p h c", h=4)
                    if d == 0:
                        tt(tmp, ha[:, :, 0:P], over(DEN[:, 0:4], P), ALU.mult)
                    else:
                        tt(ha[:, :, 0:P], ha[:, :, 0:P], over(DEN[:, 0:4], P), ALU.mult)
                        fence()
                        tt(tmp, tmp, ha[:, :, 0:P], ALU.add).then_inc(y_sum, 1)
                    fence()
                elif kind == "ml_y":
                    t = step[1]
                    dve.wait_ge(y_rstd, l * 9 + (2 * TT + t + 1))
                    if t == 0:
                        dve.wait_ge(o_sigmoid, l + 1)
                    for h in range(HEADS):
                        stt(TMP[:, tile(h)], TMP[:, tile(h)], ST4[:, 0, h:h + 1], row("ml_g")[:, tile(h)], ALU.mult, ALU.mult)
                    fence()
                    tt(YTILE[:, (2 * TT + t) % 2, :], TMP[:, :], MO[:, t, :], ALU.mult).then_inc(y_ready, 1)
                    fence()
                elif kind == "out":
                    d = step[1]
                    u = use(here, step)
                    dve.wait_ge(u.filled, u.after)
                    for v, a, b in SEGS:
                        last = stt(XT[:, d, a:b], u.t[:, a:b], MOD[:, 2, d, v:v + 1], XT[:, d, a:b], ALU.mult, ALU.add)
                    last.then_inc(u.drained, 1)
                    if d == KT - 1:
                        ve.memset(MG[:, :, :], 0.0)
                elif kind == "rank":
                    rank(use(here, step), step[1], 0)
                elif kind == "router":
                    u = use(here, step)
                    dve.wait_ge(u.filled, u.after)
                    logits = u.t[:, 0:TT * EXPERTS].rearrange("p (t e) -> p t e", t=TT)
                    ve.tensor_reduce(R3[:, 0:3], logits, AX.X, ALU.max)
                    fence()
                    tt(AFF[:, :, 0:EXPERTS], logits, over(R3[:, 0:3], EXPERTS), ALU.subtract).then_inc(u.drained, 1)
                    ve.memset(AFF[:, :, EXPERTS:EXPERTS + GE], 0.0)
                    dve.wait_ge(aff_exp, l + 1)
                    ve.tensor_reduce(R3[:, 3:6], AFF[:, :, 0:EXPERTS], AX.X, ALU.add)
                    fence()
                    ve.reciprocal(R3[:, 0:3], R3[:, 3:6])
                    fence()
                    tt(AFF[:, :, 0:EXPERTS], AFF[:, :, 0:EXPERTS], over(R3[:, 0:3], EXPERTS), ALU.mult)
                    fence()

            def rank(u, j, group):
                if j == 0:
                    at = slice(0, GE) if isinstance(group, int) else bass.ds(group * GE, GE)
                    ve.tensor_copy(AG[:, :, :], AFF[:, :, at]).then_inc(ag_ready, 1)
                    fence()
                dve.wait_ge(u.filled, u.after)
                for t in range(TT):
                    own = AG[:, t, j:j + 1]
                    a, b = (P, N) if t else (0, P)
                    first = before_at + {0: 1, 1: 1, 2: 0}[t] * P
                    mask = CT[:, first:first + b - a]
                    rank = RK[:, t:t + 1]
                    stt(TMP[:, 0:b - a], u.t[:, a:b], own, mask, ALU.is_equal, ALU.mult)
                    fence()
                    last = stt(TMP[:, 256:256 + b - a], u.t[:, a:b], own, TMP[:, 0:b - a], ALU.is_gt, ALU.add, accum_out=rank)
                    if t == TT - 1:
                        last.then_inc(u.drained, 1)
                    fence()
                    slot = const("slot_s" if t else "slot_c")
                    at = slice(j * CAP_S, (j + 1) * CAP_S)
                    ts(PO[:, t, at], slot, rank, None, ALU.is_equal)
                    last = ts(GO[:, t, at], slot, rank, own, ALU.is_equal, ALU.mult)
                    if t == TT - 1:
                        last.then_inc(picked, 1)

            def group_step(l, g, step):
                kind = step[0]
                if kind == "next_rank":
                    if step[1] == 0:
                        for x in [use(here, ("gather", a)) for a in (2, 3)] + [use(here, ("g_turn",))]:
                            dve.wait_ge(x.filled, x.after)
                    rank(use(here, step), step[1], g + 1)
                elif kind == "up":
                    j, half = step[1:]
                    gate, up = use(here, step, 0), use(here, step, 1)
                    dve.wait_ge(hid_sigmoid, l * (GROUPS * GE * 2) + g * (GE * 2) + (j * 2 + half + 1))
                    tt(SGE[:, half, :], SGE[:, half, :], gate.t[:, 0:256], ALU.mult).then_inc(gate.drained, 1)
                    fence()
                    dve.wait_ge(up.filled, up.after)
                    tt(HH[:, half, :], SGE[:, half, :], up.t[:, 0:256], ALU.mult).then_inc(up.drained, 1)
                elif kind == "scatter":
                    d = step[1]
                    u = use(here, step)
                    dve.wait_ge(u.filled, u.after)
                    tt(MG[:, d, :], MG[:, d, :], u.t[:, 0:N], ALU.add).then_inc(u.drained, 1)

            ve.memset(CSIG[:, :, :], 0.0)
            fence()
            dve.wait_ge(c_sigmoid, 1)
            tt(CSIG[:, :, 0:2], LAM[:, 0:2 * KT].rearrange("p (k v) -> p k v", v=2), CVEC[:, :, :], ALU.mult).then_inc(c_ready, 1)
            with dve.Fori(0, DEPTH) as l:
                here.layer, here.part = l, "layer"
                dve.wait_ge(small_in, l * 32 + 32)
                for step in STEPS:
                    mixer_step(l, step)
                    if step[0] in DVE_STEPS:
                        fence()
                with dve.Fori(0, GROUPS) as g:
                    here.group, here.part = g, "group"
                    for step in GROUP_STEPS:
                        group_step(l, g, step)
                        if step[0] in DVE_STEPS:
                            fence()
                for kt in range(KT):
                    for v, a, b in SEGS:
                        last = stt(XT[:, kt, a:b], MG[:, kt, a:b], MOD[:, 5, kt, v:v + 1], XT[:, kt, a:b], ALU.mult, ALU.add)
                fence()
                ve.tensor_copy(R3[:, 0:1], R3[:, 0:1]).then_inc(layer_done, 1)
            here.part = "end"
            norm(DEPTH, 0, 2, None)


_WEIGHTS = ["ada_w", "w_in", "w_branch", "w_mgate", "w_out", "ex_w_gate", "ex_w_up", "ex_w_down"]
_OUTS = {
    "k_out": (DEPTH, P, HEADS, P), "v_out": (DEPTH, P, 512), "ssm_out": (DEPTH, 2, P, 256),
    "c_out": (DEPTH, P, 2, 2, P + 1), "m_out": (DEPTH, 8), "y_out": (P, KT, N),
}


def _columns(a, parts):
    return np.ascontiguousarray(a.reshape(parts, P).T)


def kernel(**inputs):
    import numpy as _np
    import concourse.bacc as _bacc
    from concourse.bass_utils import run_bass_kernel_spmd as _run

    a = {k: _np.asarray(v) for k, v in inputs.items()}
    arrays = {k: _np.ascontiguousarray(a[k]) for k in _WEIGHTS}
    arrays["constants"] = CONSTANTS
    x = _np.concatenate([a["x_prompt"][0], a["x_sample"][0]], axis=0)
    arrays["x_t"] = _np.ascontiguousarray(x.reshape(N, KT, P).transpose(2, 1, 0))
    arrays["c_t"] = _np.stack([_columns(a["c_ctx"], KT), _columns(a["c"][0], KT)], axis=2)
    rows, cols = [], []
    for l in range(DEPTH):
        lam_init = 0.8 - 0.6 * math.exp(-0.3 * l)
        rows.append(_np.concatenate([
            a["mb_dt_bias"][l].reshape(-1), a["mb_a_log"][l].reshape(-1), a["mb_d"][l], a["ml_gate_b"][l].reshape(-1),
            a["state_mlstm_m"][0, l].reshape(-1), a["da_lambda"][l].reshape(-1), a["da_subln_g"][l],
            a["mb_norm_g"][l], a["ml_norm_g"][l].reshape(-1),
            _np.array([lam_init, 1.0 - lam_init], _np.float32)]))
        cols.append(_np.concatenate([
            _columns(a["ada_b"][l], 48), _columns(a["norm1_g"][l], KT), _columns(a["norm2_g"][l], KT),
            _columns(a["b_mgate"][l], 24), _columns(a["mb_conv_w"][l].reshape(-1), 18), _columns(a["mb_conv_b"][l], 6),
            a["router_w"][l].reshape(KT, P, EXPERTS).transpose(1, 0, 2).reshape(P, KT * EXPERTS),
            _columns(a["final_g"], KT)], axis=1))
    arrays["rows"], arrays["cols"] = _np.stack(rows), _np.stack(cols)
    arrays["cache_k_t"] = _np.ascontiguousarray(
        a["cache_k"][0].reshape(DEPTH, P, HEADS, 2 * 64).transpose(0, 3, 2, 1))
    arrays["cache_v"] = _np.ascontiguousarray(a["cache_v"][0].reshape(DEPTH, P, 512))
    arrays["ssm_t"] = _np.ascontiguousarray(
        a["state_ssm"][0].reshape(DEPTH, 2, 2, 4, 64, 64).transpose(0, 1, 2, 5, 3, 4).reshape(DEPTH, 2, P, 256))
    cn = _np.concatenate([a["state_mlstm_c"][0], a["state_mlstm_n"][0][..., None]], axis=-1)
    arrays["c_t0"] = _np.ascontiguousarray(
        cn.reshape(DEPTH, 2, 2, 2, 64, P + 1).transpose(0, 3, 4, 1, 2, 5).reshape(DEPTH, P, 2, 2, P + 1))

    nc = _bacc.Bacc("TRN2", target_bir_lowering=False, num_devices=1)
    aps = {k: nc.dram_tensor(k, v.shape, F, kind="ExternalInput").ap() for k, v in arrays.items()}
    aps.update({k: nc.dram_tensor(k, s, F, kind="ExternalOutput").ap() for k, s in _OUTS.items()})
    build(nc, aps)
    r = _run(nc, [arrays], core_ids=[0]).results[0]

    y = r["y_out"].transpose(2, 1, 0).reshape(N, D)
    k = r["k_out"].transpose(0, 3, 2, 1).reshape(1, DEPTH, P, HEADS, 2, 64)
    v = r["v_out"].reshape(1, DEPTH, P, HEADS, 2 * 64)
    ssm = r["ssm_out"].reshape(DEPTH, 2, 2, 64, 4, 64).transpose(0, 1, 2, 4, 5, 3).reshape(1, DEPTH, 2, 8, 64, 64)
    c = r["c_out"].reshape(DEPTH, 2, 64, 2, 2, P + 1).transpose(0, 3, 4, 1, 2, 5).reshape(1, DEPTH, 2, HEADS, 64, P + 1)
    m = r["m_out"].reshape(1, DEPTH, 2, HEADS)
    return (y[None, :P], y[None, P:], k, v, ssm, c[..., :P], c[..., P], m)
```

```python
import math
from contextlib import ExitStack

import numpy as np
import concourse.bass as bass
from concourse import mybir

F = mybir.dt.float32
ALU = mybir.AluOpType
ACT = mybir.ActivationFunctionType
AX = mybir.AxisListType

P = 128
D = 1024
KT = D // P
DEPTH = 2
TT = 3
N = TT * P
NS = 2 * P
SEGS = ((0, 0, P), (1, P, N))
EPS = 1e-6
HEADS = 4
RING = 8
MIX_RING = 3
SLOT_ORDER = (3, 4, 5, 6, 0, 1, 2, 7)
CH = 512
EXPERTS = 16
GE = 4
GROUPS = EXPERTS // GE
CAP_S, CAP_C = 32, 16
SLOTS = 64
NEG = -1.0e30
XW = N + 3

Q0, K0, V0, Z0, X0, DT0, MQ0, MV0, MO0, IF0 = 0, 512, 1024, 1536, 2048, 2816, 2832, 3344, 3856, 4368
WIN = 4384

MIX_CHUNKS = (
    [("ada", c * CH) for c in range(4)]
    + [("q", Q0), ("k", K0), ("v", V0), ("z", Z0), ("x0", X0), ("x1", X0 + CH)]
    + [("ada", c * CH) for c in range(4, 8)]
    + [("gate", 0), ("gate", 1), ("branch", 0), ("branch", 1)]
    + [("mq", MQ0), ("if", IF0 - 16), ("ada", 8 * CH), ("ada", 9 * CH), ("gate", 2), ("gate", 3), ("mv", MV0)]
    + [("branch", 2), ("branch", 3), ("mo", MO0), ("gate", 4), ("gate", 5), ("branch", 4), ("branch", 5)]
    + [("out", 0), ("out", 1), ("ada", 10 * CH), ("ada", 11 * CH)]
)
EXPERT_CHUNKS = ["gate0", "gate1", "up0", "up1", "down0", "down1"]
CHUNKS = len(MIX_CHUNKS) + EXPERTS * len(EXPERT_CHUNKS)
assert len(MIX_CHUNKS) % MIX_RING == 0 and (GE * len(EXPERT_CHUNKS)) % RING == 0

STATES = [(0, 0), (0, 1), (1, 0), (2, 1)]
STARTED = [(1, 0), (2, 1), (1, 1), (2, 0)]


def schedule():
    s, fillers = [], []
    for c in range(4):
        s += [("ada", c)] + ([("ada_turn", c - 1)] if c else [])
    s += [("ada_turn", 3), ("norm", 0)]
    s += [("q", h) for h in range(HEADS)] + [("k", h) for h in range(HEADS)] + [("rope",)]
    s += [("v", t) for t in range(TT)]
    dense = [[("z", t)] for t in range(TT)] + [[("x", j)] for j in range(6)] + [[("dt",)]]
    fold = {"dt": ("dt_fold",), "if": ("if_fold",)}
    dense += [[("ada", 4), ("ada", 5)], [("ada_turn", 4), ("ada_turn", 5), ("ada", 6), ("ada", 7)]]
    dense += [([] if d else [("ada_turn", 6), ("ada_turn", 7)]) + [("gate", 0, d)] for d in range(KT)]

    def take(k=1):
        for _ in range(k):
            if dense:
                fillers.append([step for step in dense[0] if step[0] != "ada_turn"])
                s.extend(dense.pop(0))
                if len(fillers) > 1 and fillers[-2][0][0] in fold:
                    s.append(fold[fillers[-2][0][0]])

    n = TT * HEADS
    for i in range(n + 2):
        if i < n:
            s.append(("score", i))
        if len(dense) > 2:
            take()
        if 0 <= i - 1 < n:
            s.append(("turn", i - 1))
        if i > HEADS and len(dense) > 2:
            take()
        if 0 <= i - 2 < n:
            s.append(("value", i - 2))
            if (i - 2) % HEADS == HEADS - 1:
                s += [("att_y", (i - 2) // HEADS)]
        if i >= n - 4:
            s += [("conv", i - (n - 4))]
        if i - 4 >= 0 and (i - 4) % HEADS == HEADS - 1:
            s += [("y_turn", 0, (i - 4) // HEADS)]
    take(len(dense))
    s += [("y_turn", 0, 2)]
    for d in range(KT):
        s += [("merge", 0, d)] + ([("conv_out", d - 1)] if 1 <= d <= 6 else [])
    s += [("z_sig",)]
    dense += [[("mq", j)] for j in range(4)] + [[("if",)], [("ada", 8), ("ada", 9)]]
    dense += [([] if d else [("ada_turn", 8), ("ada_turn", 9)]) + [("gate", 1, d)] for d in range(KT)]
    dense += [[("mv", t)] for t in range(TT)]
    take()
    s += [("acum",)]
    take()
    for t in range(TT):
        s += [("xs_turn", t), ("b_turn", t)]
    for i in range(4):
        s += [("state", i)]
        if i < 3:
            take()
    small = [[("bcum",)], [("urow", 0, 0)], [("urow", 0, 1)], [("urow", 1, 0)], [("urow", 1, 1)], [("urow", 2, 0)],
             [("urow", 2, 1)], [("stab",)]]
    for t in range(TT):
        s += [("xd", t), ("decay", t, 0)]
        take()
        if t:
            s += [("mb_gain", t - 1)]
        s += [("decay", t, 1)]
        if t:
            s += [("y_turn", 1, t - 1)] + small.pop(0)
        take()
        s += [("diag", t, 0)] + small.pop(0)
        take()
        s += [("diag", t, 1)]
        if t:
            s += [("off", t, 0), ("off", t, 1)]
        s += [("mb_y", t)]
        if t < TT - 1:
            take()
    take(len(dense))
    s += [("mb_gain", TT - 1), ("y_turn", 1, TT - 1)]
    for d in range(KT):
        s += [("merge", 1, d)]
        if small and d % 2:
            s += small.pop(0)
    for x in small:
        s += x
    dense += [[("mo", t)] for t in range(TT)] + [[("gate", 2, d)] for d in range(KT)]
    s += [("k_turn", t) for t in range(TT)]
    take()
    for i in range(4):
        s += [("cstate", i)]
        if i < 2:
            take()
    s += [("mo_sig",)]
    for t in range(TT + 1):
        if t < TT:
            s += [("qk", t), ("erow", t, 0)]
            if t > 1:
                s += [("ml_gain", t - 2)]
            s += [("erow", t, 1)]
            take()
        elif t > 1:
            s += [("ml_gain", t - 2)]
        if t:
            s += [("num", t - 1, 0)]
            take()
            s += [("num", t - 1, 1)]
            if t > 1:
                s += [("y_turn", 2, t - 2)]
            s += [("ml_y", t - 1)]
    take(len(dense))
    s += [("ml_gain", TT - 1), ("y_turn", 2, TT - 1)]
    s += [("merge", 2, d) for d in range(KT)]
    s += [("out", d) for d in range(KT)]
    s += [("norm", 1), ("ada", 10)]
    s += [("h_turn", t, 0) for t in range(TT)] + [("router",)]
    s += [("h_turn", t, 1) for t in range(2)] + [("router_fold",), ("h_turn", 2, 1)]
    s += [("ada", 11), ("ada_turn", 10)]
    s += [("rank", 0), ("ada_turn", 11)] + [("rank", j) for j in range(1, GE)] + [("pick",)]
    return s, fillers


def take_late(steps, fillers):
    unit = {step: i for i, f in enumerate(fillers) for step in f}
    out, held, last = [], [], None
    for step in steps:
        i = unit.get(step)
        if (i is not None and i != last) or step[0] in FLUSH:
            out += held
            held = []
        if i is None:
            out.append(step)
        else:
            held.append(step)
            last = i
    return out + held


def group_schedule():
    s = [("gather", a) for a in range(4)] + [("g_turn",)]
    for j in range(GE):
        s += [("up", j, 0), ("up", j, 1), ("hid_turn", j), ("next_rank", j)]
        s += ([("next_pick",)] if j == GE - 1 else []) + [("down", j, 0), ("down", j, 1)]
    s += [("scatter", d) for d in range(KT)]
    return s


FLUSH = ("ada_turn", "y_turn", "merge", "k_turn", "cstate", "mo_sig", "out", "norm")
STEPS, FILLERS = schedule()
assert STEPS.index(("dt_fold",)) < STEPS.index(("y_turn", 0, 0))
assert STEPS.index(("merge", 0, KT - 1)) < STEPS.index(("if",)) < STEPS.index(("if_fold",)) < STEPS.index(("y_turn", 1, 0))
LATE_STEPS = take_late(STEPS, FILLERS)
GROUP_STEPS = group_schedule()
END_STEPS = [("norm", 2)]

ACT_STEPS = {"score", "att_y", "merge", "conv", "mb_y", "ml_y", "norm", "decay", "erow", "gather", "router_fold", "up",
             "turn", "dt_fold", "if_fold", "stab", "acum", "y_turn", "z_sig", "mo_sig", "xs_turn", "b_turn", "h_turn"}
DVE_STEPS = {"ada", "ada_turn", "norm", "rope", "v", "turn", "score", "att_y", "merge", "z_sig", "dt_fold", "conv", "acum", "state", "xd",
             "decay", "diag", "mb_y", "if_fold", "bcum", "urow", "cstate", "erow", "num", "ml_y", "out", "router_fold", "rank", "next_rank", "pick", "next_pick",
             "up", "scatter"}

BANKS = ("D0", "D1", "T0", "T1", "R0", "R1", "Y0", "Y1")


def banks_of(step, turn):
    kind = step[0]

    def rot(k):
        turn[k] += 1
        return f"{k}{turn[k] % 2}"

    if kind in ("ada", "router", "norm", "q", "k", "v", "z", "x", "dt", "mq", "mv", "mo", "if", "out",
                "gate", "merge"):
        return [rot("D")]
    if kind == "up":
        return [rot("D"), rot("D")]
    if kind in ("turn", "y_turn", "xs_turn", "b_turn", "acum", "state", "off", "bcum", "k_turn", "cstate", "qk",
                "h_turn", "dt_fold", "if_fold", "router_fold", "g_turn", "ada_turn", "hid_turn"):
        return [rot("T")]
    if kind == "score":
        return ["R0", "R1"]
    if kind == "decay":
        return ["R0", "R1"]
    if kind in ("urow", "erow"):
        return [f"R{step[2]}"]
    if kind in ("rank", "next_rank"):
        return [f"R{step[1] % 2}"]
    if kind == "value":
        return [f"Y{step[1] // HEADS % 2}"] if step[1] % HEADS == 0 else []
    if kind == "diag":
        return [f"Y{step[1] % 2}"] if step[2] == 0 else []
    if kind == "num":
        return ["Y0", "Y1"] + ([rot("T"), rot("T")] if step[1] else [])
    if kind == "gather":
        return [f"Y{step[1] % 2}"]
    if kind == "down":
        return [f"Y{step[2]}"]
    if kind == "scatter":
        return [f"R{step[1] % 2}"]
    return []


def bank_uses():
    uses = {b: {"layer": [], "group": [], "end": []} for b in BANKS}
    where = {}
    turn = {"D": 0, "T": 0}
    for part, steps in (("layer", STEPS), ("group", GROUP_STEPS), ("end", END_STEPS)):
        for step in steps:
            for k, b in enumerate(banks_of(step, turn)):
                where[(part, step, k)] = (b, len(uses[b][part]))
                uses[b][part].append((step, k))
    return uses, where


BANK_USES, WHERE = bank_uses()


class Place:

    def __init__(self):
        self.layer, self.group, self.part = 0, 0, "layer"


class Use:

    def __init__(self, hw, place, step, k=0, part=None, group=None):
        part = part or ("layer" if ("layer", step, k) in WHERE and place.part != "end" else place.part)
        name, i = WHERE[(part, step, k)]
        uses = BANK_USES[name]
        per_layer = len(uses["layer"]) + GROUPS * len(uses["group"])
        n = place.layer * per_layer
        if part == "layer":
            i += 0
        elif part == "group":
            i += len(uses["layer"])
            g = place.group if group is None else group
            if isinstance(g, int):
                i += g * len(uses["group"])
            else:
                n = n + g * len(uses["group"])
        else:
            n, i = DEPTH * per_layer, i
        self.t, self.filled, self.drained = hw.banks[name], hw.filled[name], hw.drained[name]
        self.before, self.after = n + (i + 1), n + (i + 2)
        self.bank, self.order = name, (part, i)


def drains(after, before=()):
    last = {}
    for u, value, i in [(u, u.after, 1) for u in after] + [(u, u.before, 0) for u in before]:
        place = (u.order[0] != "layer", u.order[1] + i)
        if u.bank not in last or last[u.bank][0] < place:
            last[u.bank] = (place, u.drained, value)
    return [(semaphore, value) for _, semaphore, value in last.values()]


def constant_table():
    i, j = np.meshgrid(np.arange(P), np.arange(P), indexing="ij")
    parts = {
        "ident": (i == j), "tri_f": (i <= j), "tri_b": (i >= j),
        "neg_f": np.where(i <= j, 0.0, NEG), "neg_b": np.where(i >= j, 0.0, NEG),
        "ones": np.ones((P, P)), "before": (j < i), "none": np.zeros((P, P)),
    }
    t = np.arange(NS)
    pos = np.stack([t // 64, t % 64]).astype(np.float32)
    inv = (np.float32(10000.0) ** (-np.arange(16, dtype=np.float32) / np.float32(16))).astype(np.float32)
    ch = np.arange(P) % 64
    ang = pos[ch // 32] * inv[ch % 16][:, None]
    parts["cos"] = np.cos(ang)
    parts["sin"] = np.sin(ang) * np.where(ch % 32 < 16, -1.0, 1.0)[:, None]
    parts["slot_s"] = np.broadcast_to(np.arange(CAP_S), (P, CAP_S))
    parts["slot_c"] = np.broadcast_to(np.where(np.arange(CAP_S) < CAP_C, np.arange(CAP_S), -1), (P, CAP_S))
    parts["fold"] = np.arange(P)[:, None] % 32 == 16 + np.arange(16)
    parts["eps"] = np.full((P, 1), EPS)
    parts["minus_half"] = np.full((P, 1), -0.5)
    where, at = {}, 0
    for k, v in parts.items():
        where[k] = (at, at + v.shape[1])
        at += v.shape[1]
    return np.concatenate([np.asarray(v, np.float32) for v in parts.values()], axis=1), where


CONSTANTS, CONST_AT = constant_table()


def offsets(sizes):
    where, at = {}, 0
    for k, n in sizes:
        where[k] = (at, at + n)
        at += n
    return where, at


ROW_SIZES = [("dt_b", 16), ("a_log", 16), ("mb_d", 8), ("gate_b", 16), ("m0", 8), ("lam", 256), ("subln", P),
             ("mb_g", 512), ("ml_g", 512), ("lam_init", 1), ("lam_rest", 1)]
ROW_AT, ROW_N = offsets(ROW_SIZES)
COL_SIZES = [("ada_b", 48), ("n1", KT), ("n2", KT), ("b_gate", 24), ("conv_w", 18), ("conv_b", 6),
             ("router", KT * EXPERTS), ("final", KT)]
COL_AT, COL_N = offsets(COL_SIZES)



def last_uses():
    out = []
    for kind, c in MIX_CHUNKS:
        if kind == "ada":
            out.append((("ada", c // CH), 0))
        elif kind in ("gate", "branch"):
            out.append((("gate" if kind == "gate" else "merge", c // 2, c % 2 * 4 + 3), 0))
        elif kind == "out":
            out.append((("out", c * 4 + 3), 0))
        else:
            out.append(({"q": ("q", 3), "k": ("k", 3), "v": ("v", 2), "z": ("z", 2), "x0": ("x", 3), "x1": ("dt",),
                         "mq": ("mq", 3), "mv": ("mv", 2), "mo": ("mo", 2), "if": ("if",)}[kind], 0))
    return out


LAST_USE = last_uses()
GROUP_LAST_USE = [use for j in range(GE) for use in
                  ((("up", j, 0), 0), (("up", j, 1), 0), (("up", j, 0), 1), (("up", j, 1), 1),
                   (("down", j, 0), 0), (("down", j, 1), 0))]
GROUP_CHUNKS = len(GROUP_LAST_USE)
CHUNK_AT = {}
for _i, (_kind, _c) in enumerate(MIX_CHUNKS):
    CHUNK_AT[(_kind, _c // CH if _kind == "ada" else _c if _kind in ("gate", "branch", "out") else 0)] = _i


def expert_slot(i):
    return SLOT_ORDER[i % RING]


def mix_loads(slot):
    return len(MIX_CHUNKS) // MIX_RING if slot < MIX_RING else 0


def slot_loads(slot):
    return mix_loads(slot) + GROUPS * GROUP_CHUNKS // RING


class Hardware:
    pass


def build(nc, A):
    ctx = ExitStack()
    with ctx:
        hw = Hardware()
        hw.banks = {b: ctx.enter_context(nc.psum_tensor(f"bank_{b}", [P, 512], F)) for b in BANKS}
        hw.filled = {b: ctx.enter_context(nc.semaphore(f"filled_{b}")) for b in BANKS}
        hw.drained = {b: ctx.enter_context(nc.semaphore(f"drained_{b}")) for b in BANKS}

        def sb(name, *shape):
            return ctx.enter_context(nc.sbuf_tensor(name, [P, *shape], F))

        def sem(name):
            return ctx.enter_context(nc.semaphore(name))

        ring = sb("ring", MIX_RING + 1, KT * CH)
        XT, HM = sb("XT", KT, N), sb("HM", 2 * KT, N)
        HT, MG = HM[:, 0:KT, :], HM[:, KT:2 * KT, :]
        CT = sb("CT", CONSTANTS.shape[1])
        ROWS, COLS = sb("ROWS", ROW_N), sb("COLS", COL_N)
        CSIG = sb("CSIG", KT, 32)
        MOD, AMOD = sb("MOD", 6, KT, 2), sb("AMOD", 2, KT, 2)
        RS = sb("RS", N)
        GB = ring[:, MIX_RING, 0:KT * N].rearrange("p (k n) -> p k n", k=KT)
        LAM = sb("LAM", 2 * KT)
        EB = sb("EB", 2, 2, HEADS * P)
        YTILE, YT = sb("YTILE", 2, 512), sb("YT", 4, N)
        TMP, AD = sb("TMP", 512), sb("AD", 2, P)
        ST4 = sb("ST4", 2, HEADS)

        def const(name):
            a, b = CONST_AT[name]
            return CT[:, a:b]

        def row(name):
            a, b = ROW_AT[name]
            return ROWS[:, a:b]

        def col(name):
            a, b = COL_AT[name]
            return COLS[:, a:b]

        ident, ones = const("ident"), const("ones")
        TRI = (const("tri_f"), const("tri_b"))
        NEGT = (const("neg_f"), const("neg_b"))
        before_at = CONST_AT["ones"][0]

        def views(arena, sizes):
            out, at = [], 0
            for shape in sizes:
                n = math.prod(shape)
                v = arena[:, at:at + n]
                if len(shape) == 2:
                    v = v.rearrange("p (a b) -> p a b", a=shape[0])
                if len(shape) == 3:
                    v = v.rearrange("p (a b c) -> p a b c", a=shape[0], b=shape[1])
                out.append(v)
                at += n
            assert at <= arena.shape[1], (at, arena.shape)
            return out

        arena_a, arena_b = sb("arena_a", 2 * KT * CH), sb("arena_b", 9876)
        CVEC, = views(arena_b, [(KT, 2)])

        def slot(i):
            n = KT * CH
            if i < 4:
                return ring[:, i, :]
            if i < 6:
                return arena_a[:, (i - 4) * n:(i - 3) * n]
            if i == 6:
                return arena_b[:, arena_b.shape[1] - n:arena_b.shape[1]]
            return HM.rearrange("p a b -> p (a b)")[:, 0:n]

        QT, KTT, V, VC, PR, PT, NMX, SMX, RCP = views(
            arena_a, [(HEADS, N), (HEADS, 4 * P), (TT, 512), (512,), (2, 2, N), (2, N), (2, 2), (2, 2), (2, 2)])
        ROT = PR.rearrange("p a b c -> p (a b c)")[:, 0:HEADS * NS].rearrange("p (a b) -> p a b", a=HEADS)
        MQ, MK, MKTOK, MV, MO, CS, CC, PRE, LG, UB, MARG, MEXP, HC = views(
            arena_a, [(2, N), (2, N), (TT, 2 * P), (TT, HEADS, 129), (TT, 512), (2, 2, 129), (2, 2, 129),
                      (48,), (3, 24), (8, 24), (4, 24), (4, 24), (2, 256)])
        UM, PM, MS, MXX, NRR, MNEW, BC, TB = [UB[:, k, :] for k in range(8)]
        LAB, LFF, UU = [LG[:, k, :] for k in range(3)]
        Z, XB, CX, XD, XWT, HS, CB, BTK, DT3, EX3, DTV, EXPA = views(
            arena_b, [(TT, 512), (6, XW), (6, XW), (2, 512), (512,), (2, 256), (TT, 256), (TT, P),
                      (3, 48), (3, 48), (4, 48), (16,)])
        XS = XB.rearrange("p a b -> p (a b)")[:, 0:TT * 512].rearrange("p (a b) -> p a b", a=TT)
        OFF = (0, P + 1, 2 * P + 1)
        HA, DEN, QK, KW = views(arena_b, [(HEADS * 130,), (8,), (512,), (2 * P,)])
        XE, = views(HM.rearrange("p a b -> p (a b)")[:, KT * CH:2 * KT * N], [(KT, GE, SLOTS)])
        YES, = views(YT.rearrange("p a b -> p (a b)"), [(D,)])
        H2, PO, GO, GT, YEC, RK, AFF, AG, R3 = views(
            arena_b[:, 0:arena_b.shape[1] - KT * CH],
            [(TT, D), (TT, GE * CAP_S), (TT, GE * CAP_S), (TT, P), (D,), (16,), (TT, EXPERTS + GE), (TT, GE), (8,)])
        SGE, HH, HIDT = views(EB[:, :, :, :].rearrange("p a b c -> p (a b c)"), [(2, 256), (2, 256), (2, KT, SLOTS)])

        def tile(t):
            return slice(t * P, (t + 1) * P)

        slot_in = [sem(f"slot_in_{k}") for k in range(RING)]
        consts_in, x_in, cols_in, rows_in, cache_in, ssm_in, c0_in = (
            sem(x) for x in ("consts_in", "x_in", "cols_in", "rows_in", "cache_in", "ssm_in", "c0_in"))
        layer_done, arena_free = sem("layer_done"), sem("arena_free")
        c_in, c_sigmoid, c_ready = sem("c_in"), sem("c_sigmoid"), sem("c_ready")
        squares, rstd_ready, scaled, h_ready = sem("squares"), sem("rstd_ready"), sem("scaled"), sem("h_ready")
        lam_sums, lam_exps = sem("lam_sums"), sem("lam_exps")
        rope_done, maxes, probs_ready = sem("rope_done"), sem("maxes"), sem("probs_ready")
        y_sum, y_squares, y_rstd, y_ready = (
            sem(x) for x in ("y_sum", "y_squares", "y_rstd", "y_ready"))
        gate_sigmoid, o_sigmoid, merged = sem("gate_sigmoid"), sem("o_sigmoid"), sem("merged")
        z_sigmoid, dt_abs, dt_ln, a_exp, dta_ready = (
            sem(x) for x in ("z_sigmoid", "dt_abs", "dt_ln", "a_exp", "dta_ready"))
        conved, conv_sigmoid, conv_done = sem("conved"), sem("conv_sigmoid"), sem("conv_done")
        ac_ready, ac_exp, xd_ready, xw_ready = sem("ac_ready"), sem("ac_exp"), sem("xd_ready"), sem("xw_ready")
        e_exp, m_ready = sem("e_exp"), sem("m_ready")
        lf_abs, lf_ln, lf_ready, u_ready = sem("lf_abs"), sem("lf_ln"), sem("lf_ready"), sem("u_ready")
        stab_ready, stab_exp, kw_ready = sem("stab_ready"), sem("stab_exp"), sem("kw_ready")
        aff_exp, ag_ready, picked, weighted, hid_sigmoid = sem("aff_exp"), sem("ag_ready"), sem("picked"), sem("weighted"), sem("hid_sigmoid")
        k_out, v_out, ssm_out, c_out, m_out, y_out = (sem(x) for x in ("k_out", "v_out", "ssm_out", "c_out", "m_out", "y_out"))
        y_final = sem("y_final")

        def use(place, step, k=0, part=None, group=None):
            return Use(hw, place, step, k, part, group)

        block = ctx.enter_context(nc.Block())

        @block.sync
        def _(sp):
            here = Place()

            def load_mix(l, i):
                kind, c = MIX_CHUNKS[i]
                one = bass.ds(l, 1)
                kt, n = KT, CH
                if kind == "ada":
                    src = A["ada_w"][one, :, c:c + CH]
                elif kind == "gate":
                    src = A["w_mgate"][one, :, c * CH:(c + 1) * CH]
                elif kind == "branch":
                    kt = KT // 2
                    src = A["w_branch"][one, c // 2, :, c % 2 * CH:(c % 2 + 1) * CH]
                elif kind == "out":
                    src = A["w_out"][one, :, c * CH:(c + 1) * CH]
                else:
                    n = {"x1": MQ0 - X0 - CH, "if": 32}.get(kind, CH)
                    src = A["w_in"][one, :, c:c + n]
                sp.dma_start(ring[:, i % MIX_RING, 0:kt * n].rearrange("p (k n) -> p k n", k=kt),
                             src.rearrange("a (k p) n -> p (a k) n", p=P),
                             allow_slow_non_contiguous=True).then_inc(slot_in[i % MIX_RING], 16)

            def expert_source(l, g, i):
                j, what = i // 6, EXPERT_CHUNKS[i % 6]
                half = int(what[-1])
                src = A["ex_w_" + what[:-1]][bass.ds(l, 1), bass.ds(g * GE + j, 1), :, half * CH:(half + 1) * CH]
                return src.rearrange("a e (k p) n -> p (a e k) n", p=P)

            def load_expert(src, i):
                sp.dma_start(slot(expert_slot(i)).rearrange("p (k n) -> p k n", k=KT), src
                             ).then_inc(slot_in[expert_slot(i)], 16)

            with sp.Fori(0, DEPTH) as l:
                here.layer = l
                for i in range(len(MIX_CHUNKS)):
                    if i < MIX_RING:
                        step, k = GROUP_LAST_USE[GROUP_CHUNKS - RING + SLOT_ORDER.index(i)]
                        at_1 = Place()
                        at_1.layer = 0
                        last = use(at_1, step, k, "group", GROUPS - 1)
                        sp.wait_ge(last.filled, l * (last.after - 1) + 1)
                    else:
                        last = use(here, *LAST_USE[i - MIX_RING])
                        sp.wait_ge(last.filled, last.after)
                    load_mix(l, i)
                for i in range(RING):
                    src = expert_source(l, 0, i)
                    if i == 0:
                        last = use(here, ("merge", 2, KT - 1))
                        sp.wait_ge(last.drained, last.after)
                        for s in (ssm_out, m_out, c_out):
                            sp.wait_ge(s, l * 16 + 16)
                    elif expert_slot(i) < MIX_RING:
                        last = use(here, *LAST_USE[len(MIX_CHUNKS) - MIX_RING + expert_slot(i)])
                        sp.wait_ge(last.filled, last.after)
                    elif i == RING - 1:
                        last = use(here, ("h_turn", TT - 1, 1))
                        sp.wait_ge(last.filled, last.after)
                    load_expert(src, i)
                with sp.Fori(0, GROUPS - 1) as g:
                    for i in range(RING, GROUP_CHUNKS + RING):
                        step, k = GROUP_LAST_USE[i - RING]
                        last = use(here, step, k, "group", g)
                        sp.wait_ge(last.filled, last.after)
                        load_expert(expert_source(l, g + i // GROUP_CHUNKS, i % GROUP_CHUNKS), i % GROUP_CHUNKS)
                for i in range(RING, GROUP_CHUNKS):
                    step, k = GROUP_LAST_USE[i - RING]
                    last = use(here, step, k, "group", GROUPS - 1)
                    sp.wait_ge(last.filled, last.after)
                    load_expert(expert_source(l, GROUPS - 1, i), i)

        @block.gpsimd
        def _(pool):
            here = Place()
            for b in BANKS:
                pool.sem_inc(hw.filled[b], 1)
                pool.sem_inc(hw.drained[b], 1)
            pool.sem_inc(layer_done, 1)

            def rstd(x):
                nc.gpsimd.tensor_scalar(x, x, EPS, None, ALU.add)
                nc.gpsimd.drain()
                return nc.gpsimd.tensor_tensor(x, x, const("minus_half").to_broadcast([P, x.shape[1]]), ALU.pow)

            def head_norms(l, n, width):
                for t in range(TT):
                    pool.wait_ge(y_squares, l * 9 + n * TT + t + 1)
                    rstd(ST4[:, 0, 0:width]).then_inc(y_rstd, 1)

            for l in range(DEPTH):
                here.layer = l
                one = slice(l, l + 1)
                if l:
                    before = Place()
                    before.layer = l - 1
                    u = use(before, ("ada_turn", 11))
                    pool.wait_ge(u.drained, u.after)
                pool.dma_start(COLS[:, :], A["cols"][one].rearrange("a p n -> p (a n)")).then_inc(cols_in, 16)
                if l == 0:
                    pool.dma_start(XT[:, :, :], A["x_t"]).then_inc(x_in, 16)
                    u = use(here, ("ada", 2))
                    pool.wait_ge(u.filled, u.after)
                pool.dma_start(ROWS[:, :], A["rows"][one].to_broadcast([P, ROW_N])).then_inc(rows_in, 16)
                if l:
                    pool.wait_ge(layer_done, l * GROUPS + 1)
                    pool.wait_ge(c_out, l * 16)
                    pool.wait_ge(m_out, l * 16)
                pool.sem_inc(arena_free, 1)
                pool.dma_start(KTT[:, :, P:2 * P], A["cache_k_t"][one].rearrange("a p h t -> p (a h) t")).then_inc(cache_in, 16)
                pool.dma_start(VC[:, :], A["cache_v"][one].rearrange("a p n -> p (a n)")).then_inc(cache_in, 16)
                pool.dma_start(HS[:, :, :], A["ssm_t"][one].rearrange("a d p n -> p (a d) n")).then_inc(ssm_in, 16)
                for h in (HEADS - 2, HEADS - 1):
                    u = use(here, ("k", h))
                    pool.wait_ge(u.drained, u.after)
                pool.dma_start(A["k_out"][one].rearrange("a p h t -> p (a h) t"), KTT[:, :, 0:P]).then_inc(k_out, 16)
                u = use(here, ("v", 0))
                pool.wait_ge(u.drained, u.after)
                pool.dma_start(A["v_out"][one].rearrange("a p n -> p (a n)"), V[:, 0, :]).then_inc(v_out, 16)
                head_norms(l, 0, HEADS)
                u = use(here, ("value", (TT - 1) * HEADS))
                pool.wait_ge(u.drained, u.after)
                pool.wait_ge(k_out, l * 16 + 16)
                pool.wait_ge(v_out, l * 16 + 16)
                pool.dma_start(CS[:, :, :, :], A["c_t0"][one].rearrange("a p d t n -> p (a d) t n")).then_inc(c0_in, 16)
                for i in (0, 1):
                    u = use(here, ("state", i))
                    pool.wait_ge(u.drained, u.after)
                pool.dma_start(A["ssm_out"][one].rearrange("a d p n -> p (a d) n"), HC[:, :, :]).then_inc(ssm_out, 16)
                head_norms(l, 1, 1)
                pool.wait_ge(stab_ready, l + 1)
                pool.dma_start(A["m_out"][one], MNEW[0:1, 0:8]).then_inc(m_out, 16)
                for i in (0, 1):
                    u = use(here, ("cstate", i))
                    pool.wait_ge(u.drained, u.after)
                pool.dma_start(A["c_out"][one].rearrange("a p d t n -> p (a d) t n"), CC[:, :, :, :]).then_inc(c_out, 16)
                head_norms(l, 2, HEADS)
            pool.wait_ge(y_final, KT)
            pool.dma_start(A["y_out"], HT[:, :, :]).then_inc(y_out, 16)
            pool.wait_ge(y_out, 16)
            for s in (k_out, v_out, ssm_out, c_out, m_out):
                pool.wait_ge(s, DEPTH * 16)

        @block.tensor
        def _(pe):
            here = Place()
            mm, turn = nc.tensor.matmul, nc.tensor.transpose
            row_fence = nc.tensor.drain

            def chunk(l, name, n=CH, kt=KT):
                i = CHUNK_AT[name]
                pe.wait_ge(slot_in[i % MIX_RING], 16 * (l * slot_loads(i % MIX_RING)) + 16 * (i // MIX_RING + 1))
                return ring[:, i % MIX_RING, 0:kt * n].rearrange("p (k n) -> p k n", k=kt)

            def expert_chunk(l, g, i):
                at = expert_slot(i)
                n = l * slot_loads(at) + g * (GROUP_CHUNKS // RING)
                pe.wait_ge(slot_in[at], n * 16 + 16 * (mix_loads(at) + i // RING + 1))
                return slot(at).rearrange("p (k n) -> p k n", k=KT)

            def to_channels(u, w, c, src=HT, ready=None):
                for kt in range(KT):
                    if ready is not None:
                        pe.wait_ge(h_ready, ready + (kt + 1))
                    last = mm(u.t[:, 0:N], w[:, kt, c * P:(c + 1) * P], src[:, kt, :], start=kt == 0, stop=kt == KT - 1)
                last.then_inc(u.filled, 1)

            def to_tokens(u, w, t):
                for kt in range(KT):
                    last = mm(u.t[:, :], HT[:, kt, tile(t)], w[:, kt, 0:CH], start=kt == 0, stop=kt == KT - 1)
                last.then_inc(u.filled, 1)

            def spread(u, cols):
                for k, c in enumerate(cols):
                    last = turn(u.t[:, tile(k)], c.to_broadcast([P, P]), ident)
                last.then_inc(u.filled, 1)

            def norm(l, i, name):
                u = use(here, ("norm", name))
                pe.wait_ge(u.drained, u.before)
                for kt in range(KT):
                    pe.wait_ge(squares, l * (2 * KT) + (i * KT + kt + 1))
                    last = mm(u.t[:, 0:N], ones, HT[:, kt, :], start=kt == 0, stop=kt == KT - 1)
                last.then_inc(u.filled, 1)

            def mixer_step(l, step):
                kind = step[0]
                if kind == "ada":
                    c = step[1]
                    u = use(here, step)
                    w = chunk(l, ("ada", c))
                    pe.wait_ge(c_ready, 1)
                    pe.wait_ge(u.drained, u.before)
                    for kt in range(KT):
                        for j in range(4):
                            last = mm(u.t[32 * j:32 * j + 32, 0:P], CSIG[:, kt, :], w[:, kt, tile(j)],
                                      start=kt == 0, stop=kt == KT - 1)
                    last.then_inc(u.filled, 1)
                elif kind == "ada_turn":
                    c = step[1]
                    u, a = use(here, step), use(here, ("ada", c))
                    pe.wait_ge(a.drained, a.after)
                    if c == 0:
                        pe.wait_ge(consts_in, 16)
                    pe.wait_ge(u.drained, u.before)
                    turn(u.t[:, 0:P], AD[:, c % 2, :], ident).then_inc(u.filled, 1)
                elif kind == "norm":
                    norm(l, step[1], step[1])
                elif kind in ("q", "k", "mq"):
                    u = use(here, step)
                    w = chunk(l, (kind, 0))
                    pe.wait_ge(u.drained, u.before)
                    to_channels(u, w, step[1], ready=l * (2 * KT) if step == ("q", 0) else None)
                elif kind in ("v", "z", "mv", "mo"):
                    u = use(here, step)
                    w = chunk(l, (kind, 0))
                    pe.wait_ge(u.drained, u.before)
                    to_tokens(u, w, step[1])
                elif kind == "x":
                    j = step[1]
                    u = use(here, step)
                    w = chunk(l, ("x0", 0)) if j < 4 else chunk(l, ("x1", 0), MQ0 - X0 - CH)
                    pe.wait_ge(u.drained, u.before)
                    to_channels(u, w, j % 4)
                elif kind in ("dt", "if", "router"):
                    u = use(here, step)
                    if kind == "dt":
                        w = chunk(l, ("x1", 0), MQ0 - X0 - CH)
                        w = [w[:, kt, 240:272] for kt in range(KT)]
                    elif kind == "if":
                        w = chunk(l, ("if", 0), 32)
                        w = [w[:, kt, :] for kt in range(KT)]
                    else:
                        at = COL_AT["router"][0] - 16
                        w = [COLS[:, at + kt * EXPERTS:at + kt * EXPERTS + 32] for kt in range(KT)]
                        pe.wait_ge(h_ready, l * (2 * KT) + 2 * KT)
                    pe.wait_ge(u.drained, u.before)
                    for kt in range(KT):
                        j = kt % 4
                        last = mm(u.t[32 * j:32 * j + 32, 0:N], w[kt], HT[:, kt, :], start=kt < 4, stop=kt >= 4)
                    last.then_inc(u.filled, 1)
                elif kind in ("dt_fold", "if_fold", "router_fold"):
                    u, parts = use(here, step), use(here, (kind[:-5],))
                    pe.wait_ge(parts.drained, parts.after)
                    pe.wait_ge(u.drained, u.before)
                    for t in range(TT):
                        last = mm(u.t[:, t * 16:(t + 1) * 16], YT[:, 0, tile(t)], const("fold"), start=True, stop=True)
                    last.then_inc(u.filled, 1)
                elif kind == "score":
                    t, h = divmod(step[1], HEADS)
                    keys = slice(P, 4 * P) if t else slice(0, P)
                    if step[1] == 0:
                        pe.wait_ge(rope_done, l + 1)
                        pe.wait_ge(cache_in, l * 32 + 32)
                    for m in range(2):
                        u = use(here, step, m)
                        pe.wait_ge(u.drained, u.before)
                        half = slice(64 * m, 64 * m + 64)
                        mm(u.t[:, 0:keys.stop - keys.start], QT[half, h, tile(t)], KTT[half, h, keys],
                           start=True, stop=True).then_inc(u.filled, 1)
                elif kind == "turn":
                    i = step[1]
                    u = use(here, step)
                    pe.wait_ge(probs_ready, l * (TT * HEADS) + (i + 1))
                    pe.wait_ge(u.drained, u.before)
                    for b in range(3 if i // HEADS else 1):
                        last = turn(u.t[:, tile(b)], PR[:, i % 2, 0, tile(b)], ident)
                    last.then_inc(u.filled, 1)
                elif kind == "value":
                    i = step[1]
                    t, h = divmod(i, HEADS)
                    u = use(here, ("value", t * HEADS))
                    if h == 0:
                        pe.wait_ge(u.drained, u.before)
                    if i == 0:
                        for semaphore, value in drains([use(here, ("v", s)) for s in range(TT)]):
                            pe.wait_ge(semaphore, value)
                    p = use(here, ("turn", i))
                    pe.wait_ge(p.drained, p.after)
                    head = slice(h * P, (h + 1) * P)
                    vs = [VC[:, head], V[:, 1, head], V[:, 2, head]] if t else [V[:, 0, head]]
                    for b, v in enumerate(vs):
                        last = mm(u.t[:, head], PT[:, i % 2, tile(b)], v, start=b == 0, stop=b == len(vs) - 1)
                    if h == HEADS - 1:
                        last.then_inc(u.filled, 1)
                elif kind == "y_turn":
                    n, t = step[1:]
                    u = use(here, step)
                    if n == 0:
                        y = use(here, ("value", t * HEADS))
                        pe.wait_ge(y.drained, y.after)
                    else:
                        pe.wait_ge(y_ready, l * 6 + ((n - 1) * TT + t + 1))
                    pe.wait_ge(u.drained, u.before)
                    for j in range(4):
                        last = turn(u.t[:, tile(j)], YTILE[:, (n * TT + t) % 2, tile(j)], ident)
                    last.then_inc(u.filled, 1)
                elif kind == "merge":
                    n, d = step[1:]
                    proj = use(here, step)
                    w = chunk(l, ("branch", 2 * n + d // 4), kt=4)
                    if d == 0:
                        for semaphore, value in drains([use(here, ("y_turn", n, t)) for t in range(TT)]):
                            pe.wait_ge(semaphore, value)
                    pe.wait_ge(proj.drained, proj.before)
                    for kt in range(4):
                        last = mm(proj.t[:, 0:N], w[:, kt, (d % 4) * P:(d % 4 + 1) * P], YT[:, kt, :],
                                  start=kt == 0, stop=kt == 3)
                    last.then_inc(proj.filled, 1)
                elif kind == "gate":
                    n, d = step[1:]
                    u = use(here, step)
                    w = chunk(l, ("gate", 2 * n + d // 4))
                    pe.wait_ge(u.drained, u.before)
                    to_channels(u, w, d % 4)
                elif kind in ("acum", "bcum"):
                    u = use(here, step)
                    w, src = (8, DTV[:, 3, :]) if kind == "acum" else (4, LFF)
                    pe.wait_ge(*((dta_ready, l + 1) if kind == "acum" else (lf_ready, l + 1)))
                    pe.wait_ge(u.drained, u.before)
                    for x in range(2 * TT):
                        mm(u.t[:, x * w:(x + 1) * w], TRI[x % 2], src[:, x * w:(x + 1) * w], start=True, stop=True)
                    mm(u.t[:, 6 * w:12 * w], ones, src, start=True, stop=True).then_inc(u.filled, 1)
                elif kind == "xs_turn":
                    t = step[1]
                    u = use(here, step)
                    pe.wait_ge(conv_done, l * 6 + 6)
                    pe.wait_ge(u.drained, u.before)
                    for j in range(4):
                        last = turn(u.t[:, tile(j)], CX[:, j, OFF[t]:OFF[t] + P], ident)
                    last.then_inc(u.filled, 1)
                elif kind == "b_turn":
                    t = step[1]
                    u = use(here, step)
                    pe.wait_ge(u.drained, u.before)
                    at = slice(OFF[t], OFF[t] + P)
                    turn(u.t[:, 0:P], CX[:, 4, at], ident)
                    for g in range(2):
                        half = slice(64 * g, 64 * g + 64)
                        if g:
                            row_fence()
                        last = mm(u.t[:, tile(1 + g)], CX[half, 4, at], CX[half, 5, at], start=True, stop=True)
                    last.then_inc(u.filled, 1)
                elif kind == "state":
                    t, _ = STATES[step[1]]
                    u = use(here, step)
                    pe.wait_ge(xw_ready, l * 4 + (step[1] + 1))
                    turned = [use(here, ("b_turn", s)) for s in range(TT)] if step[1] == 0 else []
                    for semaphore, value in drains(turned, [u]):
                        pe.wait_ge(semaphore, value)
                    for g in range(2):
                        last = mm(u.t[64 * g:64 * g + 64, 0:256], BTK[:, t, 64 * g:64 * g + 64],
                                  XWT[:, g * 256:(g + 1) * 256], start=True, stop=True)
                    last.then_inc(u.filled, 1)
                elif kind == "decay":
                    t, g = step[1:]
                    pe.wait_ge(ac_ready, l + 1)
                    for d in range(2):
                        u = use(here, step, d)
                        pe.wait_ge(u.drained, u.before)
                        c = t * 16 + d * 8 + g * 4
                        spread(u, [DT3[:, 0, c + h:c + h + 1] for h in range(4)])
                elif kind == "diag":
                    t, g = step[1:]
                    u = use(here, ("diag", t, 0))
                    if g == 0:
                        pe.wait_ge(u.drained, u.before)
                        pe.wait_ge(xd_ready, l * TT + (t + 1))
                    pe.wait_ge(m_ready, l * 18 + ((t * 2 + g) * 2 + 2))
                    for h in range(4):
                        head = slice((g * 4 + h) * 64, (g * 4 + h) * 64 + 64)
                        for d in range(2):
                            last = mm(u.t[:, head], EB[:, g, d, tile(h)], XD[:, d, head], start=d == 0, stop=d == 1)
                    if g == 1:
                        last.then_inc(u.filled, 1)
                elif kind == "off":
                    t, d = step[1:]
                    u = use(here, step)
                    if (t, d) in ((1, 0), (2, 1)):
                        pe.wait_ge(ssm_in, l * 16 + 16)
                        state, closed = HS, []
                    else:
                        state, closed = HC, [use(here, ("state", 2 + d))]
                    for semaphore, value in drains(closed, [u]):
                        pe.wait_ge(semaphore, value)
                    for g in range(2):
                        half = slice(64 * g, 64 * g + 64)
                        if g:
                            row_fence()
                        last = mm(u.t[:, g * 256:(g + 1) * 256], CX[half, 5, OFF[t]:OFF[t] + P], state[half, d, :],
                                  start=True, stop=True)
                    last.then_inc(u.filled, 1)
                elif kind == "k_turn":
                    t = step[1]
                    u = use(here, step)
                    keys = [use(here, ("mq", j)) for j in (2, 3)] if t == 0 else []
                    for semaphore, value in drains(keys, [u]):
                        pe.wait_ge(semaphore, value)
                    for j in range(2):
                        last = turn(u.t[:, tile(j)], MK[:, j, tile(t)], ident)
                    last.then_inc(u.filled, 1)
                elif kind in ("urow", "erow"):
                    t, d = step[1:]
                    u = use(here, step)
                    pe.wait_ge(*((u_ready, l + 1) if kind == "urow" else (stab_ready, l + 1)))
                    pe.wait_ge(u.drained, u.before)
                    src = UU if kind == "urow" else NRR
                    c = t * 8 + d * 4
                    spread(u, [src[:, c + h:c + h + 1] for h in range(4)])
                elif kind == "cstate":
                    i = step[1]
                    t, d = STATES[i]
                    u = use(here, step)
                    pe.wait_ge(kw_ready, l * 4 + (i + 1))
                    values = [use(here, ("mv", s)) for s in range(TT)] if i == 0 else []
                    for semaphore, value in drains(values, [u]):
                        pe.wait_ge(semaphore, value)
                    for h in range(HEADS):
                        half, at = slice(64 * (h % 2), 64 * (h % 2) + 64), (h // 2) * 130
                        k = KW[:, h * 64:(h + 1) * 64]
                        last = mm(u.t[half, at:at + P + 1], k, MV[:, t, h, :], start=True, stop=True)
                    last.then_inc(u.filled, 1)
                elif kind == "qk":
                    t = step[1]
                    u = use(here, step)
                    pe.wait_ge(u.drained, u.before)
                    for h in (0, 2, 1, 3):
                        half = slice(64 * (h % 2), 64 * (h % 2) + 64)
                        if h == 1:
                            row_fence()
                        last = mm(u.t[:, tile(h)], MK[half, h // 2, tile(t)], MQ[half, h // 2, tile(t)],
                                  start=True, stop=True)
                    last.then_inc(u.filled, 1)
                elif kind == "num":
                    t, d = step[1:]
                    pe.wait_ge(m_ready, l * 18 + (12 + t * 2 + d + 1))
                    for k in range(2):
                        u = use(here, step, k)
                        pe.wait_ge(u.drained, u.before)
                        for h in (2 * k, 2 * k + 1):
                            at = h % 2 * 256
                            last = mm(u.t[:, at:at + P + 1], EB[:, t % 2, d, tile(h)], MV[:, t, h, :], start=True, stop=True)
                        last.then_inc(u.filled, 1)
                    if t:
                        banks = [use(here, step, 2), use(here, step, 3)]
                        if (t, d) in ((1, 0), (2, 1)):
                            pe.wait_ge(c0_in, l * 16 + 16)
                            state, closed = CS, []
                        else:
                            state, closed = CC, [use(here, ("cstate", 2 + d))]
                        for semaphore, value in drains(closed, banks):
                            pe.wait_ge(semaphore, value)
                        for k in range(2):
                            half = slice(64 * k, 64 * k + 64)
                            for pair in range(2):
                                last = mm(banks[k].t[:, pair * 256:pair * 256 + P + 1], MQ[half, pair, tile(t)],
                                          state[half, d, pair, :], start=True, stop=True)
                            last.then_inc(banks[k].filled, 1)
                elif kind == "out":
                    d = step[1]
                    u = use(here, step)
                    w = chunk(l, ("out", d // 4))
                    pe.wait_ge(merged, l * 16 + 16)
                    pe.wait_ge(u.drained, u.before)
                    to_channels(u, w, d % 4, MG)
                elif kind == "h_turn":
                    t, f = step[1:]
                    u = use(here, step)
                    pe.wait_ge(u.drained, u.before)
                    for j in range(4):
                        if t == 0 and f == 0:
                            pe.wait_ge(h_ready, l * (2 * KT) + (KT + j + 1))
                        last = turn(u.t[:, tile(j)], HT[:, f * 4 + j, tile(t)], ident)
                    last.then_inc(u.filled, 1)
                elif kind == "rank":
                    rank(use(here, step), step[1], l * (GROUPS + 1) + 1)

            def rank(u, j, turns):
                pe.wait_ge(ag_ready, turns)
                pe.wait_ge(u.drained, u.before)
                spread(u, [AG[:, t, j:j + 1] for t in range(TT)])

            def group_step(l, g, step):
                kind = step[0]
                if kind == "next_rank":
                    rank(use(here, step), step[1], l * (GROUPS + 1) + g + 2)
                elif kind == "gather":
                    a = step[1]
                    u = use(here, step)
                    pe.wait_ge(picked, l * (GROUPS + 1) + g + 1)
                    turned = [use(here, ("h_turn", t, f)) for t in range(TT) for f in range(2)] if a == 0 else []
                    for semaphore, value in drains(turned, [u]):
                        pe.wait_ge(semaphore, value)
                    for k in range(4):
                        for t in (1, 2) if a < 2 else (0,):
                            last = mm(u.t[:, tile(k)], H2[:, t, tile(a % 2 * 4 + k)], PO[:, t, :],
                                      start=t < 2, stop=t != 1)
                    last.then_inc(u.filled, 1)
                elif kind == "g_turn":
                    u = use(here, step)
                    pe.wait_ge(weighted, l * (GROUPS + 1) + g + 1)
                    pe.wait_ge(u.drained, u.before)
                    for t in range(TT):
                        last = turn(u.t[:, tile(t)], GO[:, t, :], ident)
                    last.then_inc(u.filled, 1)
                elif kind == "up":
                    j, half = step[1:]
                    if j == 0 and half == 0:
                        for semaphore, value in drains([use(here, ("gather", a)) for a in range(4)]):
                            pe.wait_ge(semaphore, value)
                    for k in range(2):
                        u = use(here, step, k)
                        w = expert_chunk(l, g, j * 6 + k * 2 + half)
                        pe.wait_ge(u.drained, u.before)
                        for kt in range(KT):
                            for c in range(2):
                                last = mm(u.t[64 * c:64 * c + 64, 0:256], XE[:, kt, j, :], w[:, kt, c * 256:(c + 1) * 256],
                                          start=kt == 0, stop=kt == KT - 1)
                        last.then_inc(u.filled, 1)
                elif kind == "hid_turn":
                    j = step[1]
                    u = use(here, step)
                    for semaphore, value in drains([use(here, ("up", j, x), 1) for x in range(2)]):
                        pe.wait_ge(semaphore, value)
                    pe.wait_ge(u.drained, u.before)
                    for x in range(4):
                        last = turn(u.t[:, tile(x)], HH[:, x // 2, tile(x % 2)], ident)
                    last.then_inc(u.filled, 1)
                elif kind == "down":
                    j, half = step[1:]
                    u = use(here, step)
                    w = expert_chunk(l, g, j * 6 + 4 + half)
                    hid = use(here, ("hid_turn", j))
                    pe.wait_ge(hid.drained, hid.after)
                    pe.wait_ge(u.drained, u.before)
                    for f in range(KT):
                        row = f // 4 * 4 + f % 2 * 2 + f // 2 % 2
                        for c in range(2):
                            last = mm(u.t[64 * c:64 * c + 64, 0:256], HIDT[:, j % 2, f, :], w[:, row, c * 256:(c + 1) * 256],
                                      start=f == 0, stop=f == KT - 1)
                    last.then_inc(u.filled, 1)
                elif kind == "scatter":
                    d = step[1]
                    u = use(here, step)
                    if d == 0:
                        for half in range(2):
                            y = use(here, ("down", GE - 1, half))
                            pe.wait_ge(y.drained, y.after)
                        x = use(here, ("g_turn",))
                        pe.wait_ge(x.drained, x.after)
                    pe.wait_ge(u.drained, u.before)
                    mm(u.t[:, 0:P], YEC[:, tile(d)], GT[:, 0, :], start=True, stop=True)
                    mm(u.t[:, P:N], YES[:, tile(d)], GT[:, 1:3, :], start=True, stop=True).then_inc(u.filled, 1)

            with pe.Fori(0, DEPTH) as l:
                here.layer, here.part = l, "layer"
                for step in STEPS:
                    mixer_step(l, step)
                with pe.Fori(0, GROUPS) as g:
                    here.group, here.part = g, "group"
                    for step in GROUP_STEPS:
                        group_step(l, g, step)
            here.part = "end"
            norm(DEPTH, 0, 2)

        @block.scalar
        def _(act):
            here = Place()
            fn = nc.scalar.activation
            fence = nc.scalar.drain

            def copy(out, in_, scale=1.0):
                return fn(out, in_, ACT.Copy, scale=scale)

            def norm(l, i, name, shift):
                for kt in range(KT):
                    if name != 1 and kt == 0:
                        act.wait_ge(layer_done, l * GROUPS + 1)
                    if name == 1:
                        x = use(here, ("out", kt))
                        act.wait_ge(x.drained, x.after)
                    fn(HT[:, kt, :], XT[:, kt, :], ACT.Square).then_inc(squares, 1)
                u = use(here, ("norm", name))
                act.wait_ge(u.filled, u.after)
                fn(RS[:, :], u.t[:, 0:N], ACT.Ln, bias=const("eps"), scale=1.0 / D).then_inc(u.drained, 1)
                fence()
                fn(RS[:, :], RS[:, :], ACT.Exp, scale=-0.5).then_inc(rstd_ready, 1)
                if shift is None:
                    return
                for kt in range(KT):
                    for v, a, b in SEGS:
                        act.wait_ge(scaled, l * (4 * KT) + (i * 2 * KT + kt * 2 + v + 1))
                        last = fn(HT[:, kt, a:b], HT[:, kt, a:b], ACT.Identity, bias=MOD[:, shift, kt, v:v + 1])
                    last.then_inc(h_ready, 1)

            def tile_free(l, n, t):
                i = n * TT + t
                if i >= 2:
                    x = use(here, ("y_turn", (i - 2) // TT, (i - 2) % TT))
                    act.wait_ge(x.filled, x.after)

            def mixer_step(l, step):
                kind = step[0]
                if kind == "norm":
                    norm(l, step[1], step[1], 0 if step[1] == 0 else 3)
                elif kind == "q":
                    u = use(here, step)
                    if step[1] == 0:
                        act.wait_ge(arena_free, l + 1)
                    act.wait_ge(u.filled, u.after)
                    copy(QT[:, step[1], :], u.t[:, 0:N], 0.125).then_inc(u.drained, 1)
                elif kind == "k":
                    u = use(here, step)
                    act.wait_ge(u.filled, u.after)
                    copy(KTT[:, step[1], 0:P], u.t[:, 0:P])
                    copy(KTT[:, step[1], 2 * P:4 * P], u.t[:, P:N]).then_inc(u.drained, 1)
                elif kind == "v":
                    u = use(here, step)
                    act.wait_ge(u.filled, u.after)
                    copy(V[:, step[1], :], u.t[:, :]).then_inc(u.drained, 1)
                    if step[1] == 0:
                        act.wait_ge(lam_sums, l + 1)
                        fn(LAM[:, 2:4], LAM[:, 0:2], ACT.Exp).then_inc(lam_exps, 1)
                elif kind == "score":
                    i = step[1]
                    nk = N if i // HEADS else P
                    for m in range(2):
                        u = use(here, step, m)
                        act.wait_ge(maxes, l * (2 * TT * HEADS) + (2 * i + m + 1))
                        fn(PR[:, i % 2, m, 0:nk], u.t[:, 0:nk], ACT.Exp, bias=NMX[:, i % 2, m:m + 1],
                           accum_out=SMX[:, i % 2, m:m + 1]).then_inc(u.drained, 1)
                elif kind == "turn":
                    i = step[1]
                    u = use(here, step)
                    nk = N if i // HEADS else P
                    act.wait_ge(u.filled, u.after)
                    copy(PT[:, i % 2, 0:nk], u.t[:, 0:nk]).then_inc(u.drained, 1)
                elif kind == "att_y":
                    t = step[1]
                    u = use(here, ("value", t * HEADS))
                    tile_free(l, 0, t)
                    act.wait_ge(u.filled, u.after)
                    for h in range(HEADS):
                        last = fn(YTILE[:, t % 2, tile(h)], u.t[:, tile(h)], ACT.Square, scale=P ** -0.5,
                                  accum_out=ST4[:, 0, h:h + 1])
                    last.then_inc(y_squares, 1)
                elif kind == "y_turn":
                    n, t = step[1:]
                    if n and t == 0:
                        for d in (KT - 2, KT - 1):
                            x = use(here, ("merge", n - 1, d))
                            act.wait_ge(x.filled, x.after)
                    u = use(here, step)
                    act.wait_ge(u.filled, u.after)
                    copy(YT[:, :, tile(t)], u.t[:, :].rearrange("p (j c) -> p j c", j=4)).then_inc(u.drained, 1)
                elif kind == "gate":
                    n, d = step[1:]
                    u = use(here, step)
                    if n:
                        x = use(here, ("merge", n - 1, d))
                        act.wait_ge(x.drained, x.after)
                    act.wait_ge(u.filled, u.after)
                    if n == 0 and d == 0:
                        act.wait_ge(cols_in, l * 16 + 16)
                    fn(GB[:, d, :], u.t[:, 0:N], ACT.Identity, bias=col("b_gate")[:, n * KT + d:n * KT + d + 1]
                       ).then_inc(u.drained, 1)
                elif kind == "merge":
                    d = step[2]
                    if d == 0:
                        fence()
                    fn(GB[:, d, :], GB[:, d, :], ACT.Sigmoid).then_inc(gate_sigmoid, 1)
                elif kind == "z":
                    u = use(here, step)
                    act.wait_ge(u.filled, u.after)
                    copy(Z[:, step[1], :], u.t[:, :]).then_inc(u.drained, 1)
                elif kind == "z_sig":
                    fence()
                    for t in range(TT):
                        fn(EB[:, t // 2, t % 2, :], Z[:, t, :], ACT.Sigmoid).then_inc(z_sigmoid, 1)
                elif kind == "mo_sig":
                    fence()
                    for t in range(TT):
                        last = fn(MO[:, t, :], MO[:, t, :], ACT.Sigmoid)
                    last.then_inc(o_sigmoid, 1)
                elif kind == "x":
                    j = step[1]
                    u = use(here, step)
                    act.wait_ge(u.filled, u.after)
                    copy(XB[:, j, 1:P + 1], u.t[:, 0:P])
                    copy(XB[:, j, P + 2:XW - 1], u.t[:, P:N]).then_inc(u.drained, 1)
                elif kind in ("dt", "if", "router"):
                    u = use(here, step)
                    act.wait_ge(u.filled, u.after)
                    copy(YT[:, 0, :], u.t[:, 0:N]).then_inc(u.drained, 1)
                elif kind == "dt_fold":
                    act.wait_ge(rows_in, l * 16 + 16)
                    fn(EXPA[:, :], row("a_log"), ACT.Exp).then_inc(a_exp, 1)
                    act.wait_ge(dt_abs, l + 1)
                    fn(DTV[:, 1, :], DTV[:, 1, :], ACT.Exp, scale=-1.0)
                    fence()
                    fn(DTV[:, 1, :], DTV[:, 1, :], ACT.Ln, bias=1.0).then_inc(dt_ln, 1)
                elif kind == "conv_out":
                    j = step[1]
                    act.wait_ge(conved, l * 6 + (j + 1))
                    fn(XB[:, j, 0:XW - 2], CX[:, j, 0:XW - 2], ACT.Sigmoid).then_inc(conv_sigmoid, 1)
                elif kind == "acum":
                    act.wait_ge(ac_ready, l + 1)
                    fn(EX3[:, :, :], DT3[:, :, :], ACT.Exp).then_inc(ac_exp, 1)
                elif kind == "xs_turn":
                    t = step[1]
                    u = use(here, step)
                    act.wait_ge(u.filled, u.after)
                    copy(XS[:, t, :], u.t[:, :]).then_inc(u.drained, 1)
                elif kind == "b_turn":
                    t = step[1]
                    u = use(here, step)
                    act.wait_ge(u.filled, u.after)
                    copy(BTK[:, t, :], u.t[:, 0:P])
                    copy(CB[:, t, :], u.t[:, P:N]).then_inc(u.drained, 1)
                elif kind == "decay":
                    t, g = step[1:]
                    for d in range(2):
                        u = use(here, step, d)
                        act.wait_ge(u.drained, u.after)
                        fn(EB[:, g, d, :], EB[:, g, d, :], ACT.Exp).then_inc(e_exp, 1)
                elif kind in ("mb_y", "ml_y"):
                    t = step[1]
                    n, parts = (1, 1) if kind == "mb_y" else (2, HEADS)
                    i = n * TT + t
                    tile_free(l, n, t)
                    act.wait_ge(y_sum, l * 6 + (i - TT + 1))
                    w = 512 // parts
                    for h in range(parts):
                        last = fn(YTILE[:, i % 2, h * w:(h + 1) * w], TMP[:, h * w:(h + 1) * w], ACT.Square,
                                  scale=w ** -0.5, accum_out=ST4[:, 0, h:h + 1])
                    last.then_inc(y_squares, 1)
                elif kind == "mq":
                    j = step[1]
                    u = use(here, step)
                    if j == 0:
                        act.wait_ge(k_out, l * 16 + 16)
                        act.wait_ge(v_out, l * 16 + 16)
                    act.wait_ge(u.filled, u.after)
                    if j < 2:
                        copy(MQ[:, j, :], u.t[:, 0:N]).then_inc(u.drained, 1)
                    else:
                        copy(MK[:, j - 2, :], u.t[:, 0:N], 0.125).then_inc(u.drained, 1)
                elif kind == "mv":
                    u = use(here, step)
                    act.wait_ge(u.filled, u.after)
                    copy(MV[:, step[1], :, P:P + 1], ones[:, 0:HEADS].unsqueeze(2))
                    copy(MV[:, step[1], :, 0:P], u.t[:, :].rearrange("p (h c) -> p h c", h=HEADS)).then_inc(u.drained, 1)
                elif kind == "mo":
                    u = use(here, step)
                    act.wait_ge(u.filled, u.after)
                    copy(MO[:, step[1], :], u.t[:, :]).then_inc(u.drained, 1)
                elif kind == "if_fold":
                    act.wait_ge(lf_abs, l + 1)
                    fn(LAB, LAB, ACT.Exp, scale=-1.0)
                    fence()
                    fn(LAB, LAB, ACT.Ln, bias=1.0).then_inc(lf_ln, 1)
                elif kind == "k_turn":
                    t = step[1]
                    u = use(here, step)
                    act.wait_ge(u.filled, u.after)
                    copy(MKTOK[:, t, :], u.t[:, 0:2 * P]).then_inc(u.drained, 1)
                elif kind == "stab":
                    act.wait_ge(stab_ready, l + 1)
                    fn(MEXP[:, :, :], MARG[:, :, :], ACT.Exp).then_inc(stab_exp, 1)
                elif kind == "qk":
                    t = step[1]
                    u = use(here, step)
                    act.wait_ge(u.filled, u.after)
                    if t:
                        act.wait_ge(m_ready, l * 18 + (12 + 2 * t))
                    copy(QK, u.t[:, :]).then_inc(u.drained, 1)
                elif kind == "erow":
                    t, d = step[1:]
                    u = use(here, step)
                    act.wait_ge(u.drained, u.after)
                    fn(EB[:, t % 2, d, :], EB[:, t % 2, d, :], ACT.Exp, scale=-1.0).then_inc(e_exp, 1)
                elif kind == "h_turn":
                    t, f = step[1:]
                    u = use(here, step)
                    if t == 0 and f == 0:
                        act.wait_ge(ssm_out, l * 16 + 16)
                    act.wait_ge(u.filled, u.after)
                    copy(H2[:, t, f * 512:(f + 1) * 512], u.t[:, :]).then_inc(u.drained, 1)
                elif kind == "router_fold":
                    u = use(here, step)
                    act.wait_ge(u.drained, u.after)
                    fn(AFF[:, :, 0:EXPERTS], AFF[:, :, 0:EXPERTS], ACT.Exp).then_inc(aff_exp, 1)

            def group_step(l, g, step):
                kind = step[0]
                if kind == "gather":
                    a = step[1]
                    u = use(here, step)
                    act.wait_ge(u.filled, u.after)
                    first, k = (0 if a < 2 else CAP_S), a % 2 * 4
                    copy(XE[:, k:k + 4, :, first:first + CAP_S].rearrange("p k e c -> p (k e) c"),
                         u.t[:, :].rearrange("p (x c) -> p x c", c=CAP_S)).then_inc(u.drained, 1)
                elif kind == "g_turn":
                    u = use(here, step)
                    act.wait_ge(u.filled, u.after)
                    copy(GT[:, :, :], u.t[:, 0:N].rearrange("p (t c) -> p t c", t=TT)).then_inc(u.drained, 1)
                elif kind == "up":
                    j, half = step[1:]
                    u = use(here, step, 0)
                    act.wait_ge(u.filled, u.after)
                    fn(SGE[:, half, :], u.t[:, 0:256], ACT.Sigmoid).then_inc(hid_sigmoid, 1)
                elif kind == "hid_turn":
                    u = use(here, step)
                    act.wait_ge(u.filled, u.after)
                    copy(HIDT[:, step[1] % 2, :, :], u.t[:, :].rearrange("p (f c) -> p f c", c=SLOTS)).then_inc(u.drained, 1)
                elif kind == "down":
                    j, half = step[1:]
                    u = use(here, step)
                    act.wait_ge(u.filled, u.after)
                    rows = slice(32 * j, 32 * j + 32)
                    for c in range(2):
                        at = slice(half * 512 + c * 256, half * 512 + c * 256 + 256)
                        copy(YES[rows, at], u.t[64 * c:64 * c + 32, 0:256])
                        last = copy(YEC[rows, at], u.t[64 * c + 32:64 * c + 64, 0:256])
                    last.then_inc(u.drained, 1)

            act.dma_start(CVEC[:, :, :], A["c_t"]).then_inc(c_in, 16)
            act.dma_start(CT[:, :], A["constants"]).then_inc(consts_in, 16)
            act.wait_ge(c_in, 16)
            fn(LAM[:, 0:2 * KT].rearrange("p (k v) -> p k v", v=2), CVEC[:, :, :], ACT.Sigmoid).then_inc(c_sigmoid, 1)
            with act.Fori(0, DEPTH) as l:
                here.layer, here.part = l, "layer"
                act.wait_ge(consts_in, 16)
                act.wait_ge(x_in, 16)
                for step in LATE_STEPS:
                    mixer_step(l, step)
                    if step[0] in ACT_STEPS:
                        fence()
                with act.Fori(0, GROUPS) as g:
                    here.group, here.part = g, "group"
                    for step in GROUP_STEPS:
                        group_step(l, g, step)
                        if step[0] in ACT_STEPS:
                            fence()
            here.part = "end"
            norm(DEPTH, 0, 2, None)

        @block.vector
        def _(dve):
            here = Place()
            ve = nc.vector
            tt, ts, stt = ve.tensor_tensor, ve.tensor_scalar, ve.scalar_tensor_tensor
            fence = ve.drain

            def over(ap, n):
                return ap.unsqueeze(2).to_broadcast([ap.shape[0], ap.shape[1], n])

            def norm(l, i, name, scale):
                dve.wait_ge(rstd_ready, l * 2 + (i + 1))
                for kt in range(KT):
                    if scale is None:
                        stt(HT[:, kt, :], XT[:, kt, :], col("final")[:, kt:kt + 1], RS[:, :], ALU.mult,
                            ALU.mult).then_inc(y_final, 1)
                        continue
                    for v, a, b in SEGS:
                        stt(HT[:, kt, a:b], XT[:, kt, a:b], AMOD[:, scale, kt, v:v + 1], RS[:, a:b], ALU.mult,
                            ALU.mult).then_inc(scaled, 1)

            def rotate(x, rot):
                cos = const("cos").unsqueeze(1).to_broadcast([P, HEADS, NS])
                sin = const("sin").unsqueeze(1).to_broadcast([P, HEADS, NS])
                ve.stream_shuffle(rot, x, [(k + 16) % 32 for k in range(32)])
                fence()
                tt(x, x, cos, ALU.mult)
                tt(rot, rot, sin, ALU.mult)
                fence()
                return tt(x, x, rot, ALU.add)

            def mixer_step(l, step):
                kind = step[0]
                if kind == "ada":
                    c = step[1]
                    u = use(here, step)
                    dve.wait_ge(u.filled, u.after)
                    ve.tensor_copy(AD[:, c % 2, :], u.t[:, 0:P]).then_inc(u.drained, 1)
                elif kind == "ada_turn":
                    c = step[1]
                    u = use(here, step)
                    if c == 0:
                        dve.wait_ge(cols_in, l * 16 + 16)
                    dve.wait_ge(u.filled, u.after)
                    half = c % 2 * 4
                    tt(MOD[:, c // 2, half:half + 4, :], u.t[:, 0:P].rearrange("p (j v) -> p j v", v=32)[:, :, 0:2],
                       over(col("ada_b")[:, c * 4:c * 4 + 4], 2), ALU.add).then_inc(u.drained, 1)
                    if c in (3, 9):
                        i = c // 6
                        fence()
                        stt(AMOD[:, i, :, :], MOD[:, c // 2, :, :], 1.0, over(col("n2" if i else "n1"), 2), ALU.add, ALU.mult)
                        fence()
                elif kind == "norm":
                    norm(l, step[1], step[1], step[1])
                elif kind == "rope":
                    for name in ("q", "k"):
                        for h in (HEADS - 2, HEADS - 1):
                            x = use(here, (name, h))
                            dve.wait_ge(x.drained, x.after)
                    dve.wait_ge(rows_in, l * 16 + 16)
                    lam = row("lam").rearrange("p (a b) -> p a b", a=4)
                    tt(TMP[:, 0:128].rearrange("p (a b) -> p a b", a=2), lam[:, 0:4:2, :], lam[:, 1:4:2, :], ALU.mult)
                    fence()
                    ve.tensor_reduce(LAM[:, 0:2], TMP[:, 0:128].rearrange("p (a b) -> p a b", a=2), AX.X,
                                     ALU.add).then_inc(lam_sums, 1)
                    ts(row("subln"), row("subln"), row("lam_rest"), None, ALU.mult)
                    rotate(QT[:, :, P:N], ROT)
                    fence()
                    rotate(KTT[:, :, 2 * P:4 * P], ROT).then_inc(rope_done, 1)
                elif kind == "v" and step[1] == TT - 1:
                    dve.wait_ge(lam_exps, l + 1)
                    tt(LAM[:, 4:5], LAM[:, 3:4], LAM[:, 2:3], ALU.subtract)
                    fence()
                    ts(LAM[:, 5:6], LAM[:, 4:5], row("lam_init"), None, ALU.subtract)
                elif kind == "score":
                    i = step[1]
                    nk = N if i // HEADS else P
                    for m in range(2):
                        u = use(here, step, m)
                        dve.wait_ge(u.filled, u.after)
                        ve.tensor_reduce(NMX[:, i % 2, m:m + 1], u.t[:, 0:nk], AX.X, ALU.max,
                                         negate=True).then_inc(maxes, 1)
                elif kind == "turn":
                    i = step[1]
                    nk = N if i // HEADS else P
                    for m in range(2):
                        s = use(here, ("score", i), m)
                        dve.wait_ge(s.drained, s.after)
                    ve.reciprocal(RCP[:, i % 2, :], SMX[:, i % 2, :])
                    fence()
                    ts(RCP[:, i % 2, 1:2], RCP[:, i % 2, 1:2], LAM[:, 5:6], None, ALU.mult)
                    ts(PR[:, i % 2, 0, 0:nk], PR[:, i % 2, 0, 0:nk], RCP[:, i % 2, 0:1], None, ALU.mult)
                    fence()
                    stt(PR[:, i % 2, 0, 0:nk], PR[:, i % 2, 1, 0:nk], RCP[:, i % 2, 1:2], PR[:, i % 2, 0, 0:nk],
                        ALU.mult, ALU.add).then_inc(probs_ready, 1)
                elif kind == "att_y":
                    t = step[1]
                    u = use(here, ("value", t * HEADS))
                    dve.wait_ge(y_rstd, l * 9 + (t + 1))
                    for h in range(HEADS):
                        last = stt(YTILE[:, t % 2, tile(h)], u.t[:, tile(h)], ST4[:, 0, h:h + 1], row("subln"),
                                   ALU.mult, ALU.mult)
                    last.then_inc(u.drained, 1)
                elif kind == "merge":
                    n, d = step[1:]
                    u = use(here, step)
                    dve.wait_ge(gate_sigmoid, l * (3 * KT) + (n * KT + d + 1))
                    dve.wait_ge(u.filled, u.after)
                    if n == 0:
                        tt(MG[:, d, :], GB[:, d, :], u.t[:, 0:N], ALU.mult).then_inc(u.drained, 1)
                    else:
                        tt(TMP[:, 0:N], GB[:, d, :], u.t[:, 0:N], ALU.mult).then_inc(u.drained, 1)
                        fence()
                        tt(MG[:, d, :], MG[:, d, :], TMP[:, 0:N], ALU.add).then_inc(merged, 1)
                elif kind == "z_sig":
                    for t in range(TT):
                        dve.wait_ge(z_sigmoid, l * TT + (t + 1))
                        tt(Z[:, t, :], Z[:, t, :], EB[:, t // 2, t % 2, :], ALU.mult)
                elif kind == "dt_fold":
                    u = use(here, step)
                    dve.wait_ge(u.filled, u.after)
                    tt(DTV[:, 0, :].rearrange("p (t c) -> p t c", t=TT), u.t[:, 0:48].rearrange("p (t c) -> p t c", t=TT),
                       row("dt_b").unsqueeze(1).to_broadcast([P, TT, 16]), ALU.add).then_inc(u.drained, 1)
                    fence()
                    stt(DTV[:, 1, :], DTV[:, 0, :], -1.0, DTV[:, 0, :], ALU.mult, ALU.max).then_inc(dt_abs, 1)
                elif kind == "conv":
                    j = step[1]
                    w = col("conv_w").rearrange("p (k j) -> p k j", k=3)
                    n = XW - 2
                    if j == 0:
                        dve.wait_ge(dt_ln, l + 1)
                        stt(DTV[:, 2, :], DTV[:, 0, :], 0.0, DTV[:, 1, :], ALU.max, ALU.add)
                        fence()
                        dve.wait_ge(a_exp, l + 1)
                        stt(DTV[:, 3, :].rearrange("p (t c) -> p t c", t=TT), DTV[:, 2, :].rearrange("p (t c) -> p t c", t=TT),
                            -1.0, EXPA.unsqueeze(1).to_broadcast([P, TT, 16]), ALU.mult, ALU.mult).then_inc(dta_ready, 1)
                        for x in (4, 5):
                            v = use(here, ("x", x))
                            dve.wait_ge(v.drained, v.after)
                        for c in (0, P + 1, XW - 1):
                            ve.memset(XB[:, :, c:c + 1], 0.0)
                        fence()
                    ts(CX[:, j, 0:n], XB[:, j, 1:1 + n], w[:, 1, j:j + 1], col("conv_b")[:, j:j + 1], ALU.mult, ALU.add)
                    fence()
                    stt(CX[:, j, 0:n], XB[:, j, 0:n], w[:, 0, j:j + 1], CX[:, j, 0:n], ALU.mult, ALU.add)
                    fence()
                    stt(CX[:, j, 0:n], XB[:, j, 2:2 + n], w[:, 2, j:j + 1], CX[:, j, 0:n], ALU.mult,
                        ALU.add).then_inc(conved, 1)
                elif kind == "conv_out":
                    j, n = step[1], XW - 2
                    dve.wait_ge(conv_sigmoid, l * 6 + (j + 1))
                    tt(CX[:, j, 0:n], CX[:, j, 0:n], XB[:, j, 0:n], ALU.mult).then_inc(conv_done, 1)
                elif kind == "acum":
                    u = use(here, step)
                    dve.wait_ge(u.filled, u.after)
                    ve.tensor_copy(DT3[:, 0, :], u.t[:, 0:48])
                    ve.tensor_copy(DT3[:, 2, :], u.t[:, 48:96]).then_inc(u.drained, 1)
                    fence()
                    tt(DT3[:, 1, :], DT3[:, 2, :], DT3[:, 0, :], ALU.subtract).then_inc(ac_ready, 1)
                    dve.wait_ge(ac_exp, l + 1)
                    tt(DTV[:, 1, :], DTV[:, 2, :], EX3[:, 1, :], ALU.mult)
                    fence()
                elif kind == "state":
                    i = step[1]
                    t, d = STATES[i]
                    x = use(here, ("xs_turn", t))
                    dve.wait_ge(x.drained, x.after)
                    c = t * 16 + d * 8
                    tt(XWT.rearrange("p (h c) -> p h c", h=8), XS[:, t, :].rearrange("p (h c) -> p h c", h=8),
                       over(DTV[:, 1, c:c + 8], 64), ALU.mult).then_inc(xw_ready, 1)
                    u = use(here, step)
                    if i >= 2:
                        dve.wait_ge(ssm_out, l * 16 + 16)
                        dve.wait_ge(ssm_in, l * 16 + 16)
                        for g in range(2):
                            half = slice(64 * g, 64 * g + 64)
                            tt(HC[half, d, :].rearrange("p (h c) -> p h c", h=4),
                               HS[half, d, :].rearrange("p (h c) -> p h c", h=4),
                               over(EX3[half, 2, c + 4 * g:c + 4 * g + 4], 64), ALU.mult)
                        fence()
                        dve.wait_ge(u.filled, u.after)
                        tt(HC[:, d, :], HC[:, d, :], u.t[:, 0:256], ALU.add).then_inc(u.drained, 1)
                    else:
                        dve.wait_ge(u.filled, u.after)
                        ve.tensor_copy(HC[:, d, :], u.t[:, 0:256]).then_inc(u.drained, 1)
                elif kind == "xd":
                    t = step[1]
                    for d in range(2):
                        last = tt(XD[:, d, :].rearrange("p (h c) -> p h c", h=8), XS[:, t, :].rearrange("p (h c) -> p h c", h=8),
                                  over(DTV[:, 2, t * 16 + d * 8:t * 16 + d * 8 + 8], 64), ALU.mult)
                    last.then_inc(xd_ready, 1)
                elif kind == "decay":
                    t, g = step[1:]
                    for d in range(2):
                        u = use(here, step, d)
                        dve.wait_ge(u.filled, u.after)
                        for h in range(4):
                            c = t * 16 + d * 8 + g * 4 + h
                            last = stt(EB[:, g, d, tile(h)], u.t[:, tile(h)], DT3[:, 0, c:c + 1], NEGT[d],
                                       ALU.subtract, ALU.add)
                        last.then_inc(u.drained, 1)
                elif kind == "diag":
                    t, g = step[1:]
                    for d in range(2):
                        dve.wait_ge(e_exp, l * 18 + ((t * 2 + g) * 2 + d + 1))
                        e = EB[:, g, d, :].rearrange("p (h c) -> p h c", h=4)
                        tt(e, e, CB[:, t, tile(g)].unsqueeze(1).to_broadcast([P, 4, P]), ALU.mult).then_inc(m_ready, 1)
                elif kind == "mb_y":
                    t = step[1]
                    u = use(here, ("diag", t, 0))
                    tt(TMP[:, :].rearrange("p (h c) -> p h c", h=8), XS[:, t, :].rearrange("p (h c) -> p h c", h=8),
                       over(row("mb_d"), 64), ALU.mult)
                    fence()
                    dve.wait_ge(u.filled, u.after)
                    tt(TMP[:, :], TMP[:, :], u.t[:, :], ALU.add).then_inc(u.drained, 1)
                    for d in range(2 if t else 0):
                        o = use(here, ("off", t, d))
                        dve.wait_ge(o.filled, o.after)
                        tt(XWT.rearrange("p (h c) -> p h c", h=8), o.t[:, :].rearrange("p (h c) -> p h c", h=8),
                           over(EX3[:, 0, t * 16 + d * 8:t * 16 + d * 8 + 8], 64), ALU.mult).then_inc(o.drained, 1)
                        fence()
                        tt(TMP[:, :], TMP[:, :], XWT, ALU.add)
                        fence()
                    fence()
                    tt(TMP[:, :], TMP[:, :], Z[:, t, :], ALU.mult).then_inc(y_sum, 1)
                elif kind == "mb_gain":
                    t = step[1]
                    dve.wait_ge(y_rstd, l * 9 + (TT + t + 1))
                    stt(YTILE[:, (TT + t) % 2, :], TMP[:, :], ST4[:, 0, 0:1], row("mb_g"), ALU.mult,
                        ALU.mult).then_inc(y_ready, 1)
                    fence()
                elif kind == "if_fold":
                    u = use(here, step)
                    dve.wait_ge(u.filled, u.after)
                    tt(PRE.rearrange("p (t c) -> p t c", t=TT), u.t[:, 0:48].rearrange("p (t c) -> p t c", t=TT),
                       row("gate_b").unsqueeze(1).to_broadcast([P, TT, 16]), ALU.add).then_inc(u.drained, 1)
                    fence()
                    f = PRE.rearrange("p (x k h) -> p k x h", k=2, h=4)[:, 1, :, :]
                    stt(LAB.rearrange("p (x h) -> p x h", h=4), f, -1.0, f, ALU.mult, ALU.max).then_inc(lf_abs, 1)
                elif kind == "bcum":
                    f = PRE.rearrange("p (x k h) -> p k x h", k=2, h=4)[:, 1, :, :]
                    i_ = PRE.rearrange("p (x k h) -> p k x h", k=2, h=4)[:, 0, :, :]
                    dve.wait_ge(lf_ln, l + 1)
                    stt(LFF.rearrange("p (x h) -> p x h", h=4), f, 0.0, LAB.rearrange("p (x h) -> p x h", h=4), ALU.min,
                        ALU.subtract).then_inc(lf_ready, 1)
                    u = use(here, step)
                    dve.wait_ge(u.filled, u.after)
                    ve.tensor_copy(BC, u.t[:, 0:24])
                    ve.tensor_copy(TB, u.t[:, 24:48]).then_inc(u.drained, 1)
                    fence()
                    tt(UU.rearrange("p (x h) -> p x h", h=4), i_, BC.rearrange("p (x h) -> p x h", h=4),
                       ALU.subtract).then_inc(u_ready, 1)
                elif kind == "urow":
                    t, d = step[1:]
                    u = use(here, step)
                    c = t * 8 + d * 4
                    dve.wait_ge(u.filled, u.after)
                    rows = u.t[:, :].rearrange("p (h c) -> p h c", h=4)
                    ve.tensor_reduce(UM[:, c:c + 4], rows, AX.X, ALU.max)
                    tmp = TMP[:, :].rearrange("p (h c) -> p h c", h=4)
                    fence()
                    tt(tmp, rows, NEGT[1 - d].unsqueeze(1).to_broadcast([P, 4, P]), ALU.add).then_inc(u.drained, 1)
                    fence()
                    ve.tensor_reduce(PM[:, c:c + 4], tmp, AX.X, ALU.max)
                elif kind == "stab":
                    m0 = row("m0")
                    ve.memset(MS[:, 0:8], 0.0)
                    ve.tensor_copy(MS[:, 8:12], m0[:, 0:4])
                    ve.tensor_copy(MS[:, 20:24], m0[:, 4:8])
                    fence()
                    tt(MXX[:, 8:12], MS[:, 8:12], UM[:, 8:12], ALU.max)
                    tt(MXX[:, 20:24], MS[:, 20:24], UM[:, 20:24], ALU.max)
                    fence()
                    tt(MS[:, 16:20], TB[:, 8:12], MXX[:, 8:12], ALU.add)
                    tt(MS[:, 12:16], TB[:, 20:24], MXX[:, 20:24], ALU.add)
                    fence()
                    tt(MXX, MS, UM, ALU.max)
                    tt(NRR, MS, PM, ALU.max)
                    fence()
                    tt(MARG[:, 0, :], MS, NRR, ALU.subtract)
                    tt(MARG[:, 1, :], MS, MXX, ALU.subtract)
                    tt(MARG[:, 2, :], UU, MXX, ALU.subtract)
                    stt(MARG[:, 3, :], BC, -1.0, NRR, ALU.mult, ALU.subtract)
                    tt(MNEW, TB, MXX, ALU.add).then_inc(stab_ready, 1)
                    dve.wait_ge(stab_exp, l + 1)
                elif kind == "cstate":
                    i = step[1]
                    t, d = STATES[i]
                    c = t * 8 + d * 4
                    x = use(here, ("k_turn", t))
                    dve.wait_ge(x.drained, x.after)
                    tt(KW.rearrange("p (h c) -> p h c", h=4), MKTOK[:, t, :].rearrange("p (h c) -> p h c", h=4),
                       over(MEXP[:, 2, c:c + 4], 64), ALU.mult).then_inc(kw_ready, 1)
                    u = use(here, step)
                    new = u.t[:, 0:260].rearrange("p (a b) -> p a b", a=2)[:, :, 0:P + 1]
                    if i < 2:
                        dve.wait_ge(u.filled, u.after)
                        ve.tensor_copy(CC[:, d, :, :], new).then_inc(u.drained, 1)
                    else:
                        dve.wait_ge(c_out, l * 16 + 16)
                        dve.wait_ge(c0_in, l * 16 + 16)
                        dve.wait_ge(u.filled, u.after)
                        for h in range(HEADS):
                            half = slice(64 * (h % 2), 64 * (h % 2) + 64)
                            last = stt(CC[half, d, h // 2, :], CS[half, d, h // 2, :], MEXP[half, 1, c + h:c + h + 1],
                                       new[half, h // 2, :], ALU.mult, ALU.add)
                        last.then_inc(u.drained, 1)
                elif kind == "erow":
                    t, d = step[1:]
                    u = use(here, step)
                    dve.wait_ge(u.filled, u.after)
                    for h in range(4):
                        c = t * 8 + d * 4 + h
                        last = stt(EB[:, t % 2, d, tile(h)], u.t[:, tile(h)], UU[:, c:c + 1], NEGT[d],
                                   ALU.subtract, ALU.subtract)
                    last.then_inc(u.drained, 1)
                    if d == 1:
                        q = use(here, ("qk", t))
                        dve.wait_ge(q.drained, q.after)
                        for x in range(2):
                            dve.wait_ge(e_exp, l * 18 + (12 + t * 2 + x + 1))
                            tt(EB[:, t % 2, x, :], EB[:, t % 2, x, :], QK, ALU.mult).then_inc(m_ready, 1)
                elif kind == "num":
                    t, d = step[1:]
                    c = t * 8 + d * 4
                    ha = HA.rearrange("p (h c) -> p h c", h=4)
                    if t:
                        for k in range(2):
                            u = use(here, step, 2 + k)
                            dve.wait_ge(u.filled, u.after)
                            x = u.t[:, :].rearrange("p (a c) -> p a c", a=2)[:, :, 0:P + 1]
                            tt(ha[:, k:4:2, 0:P + 1], x, over(MEXP[:, 0, c + k:c + 4:2], P + 1), ALU.mult).then_inc(u.drained, 1)
                        fence()
                    for k in range(2):
                        u = use(here, step, k)
                        dve.wait_ge(u.filled, u.after)
                        x = u.t[:, :].rearrange("p (a c) -> p a c", a=2)[:, :, 0:P + 1]
                        if t:
                            tt(ha[:, 2 * k:2 * k + 2, 0:P + 1], ha[:, 2 * k:2 * k + 2, 0:P + 1], x, ALU.add).then_inc(u.drained, 1)
                        else:
                            ve.tensor_copy(ha[:, 2 * k:2 * k + 2, 0:P + 1], x).then_inc(u.drained, 1)
                    fence()
                    den = ha[:, :, P]
                    stt(DEN[:, 4:8], den, -1.0, den, ALU.mult, ALU.max)
                    fence()
                    tt(DEN[:, 4:8], DEN[:, 4:8], MEXP[:, 3, c:c + 4], ALU.max)
                    fence()
                    ve.reciprocal(DEN[:, 0:4], DEN[:, 4:8])
                    fence()
                    tmp = TMP[:, :].rearrange("p (h c) -> p h c", h=4)
                    if d == 0:
                        tt(tmp, ha[:, :, 0:P], over(DEN[:, 0:4], P), ALU.mult)
                    else:
                        tt(ha[:, :, 0:P], ha[:, :, 0:P], over(DEN[:, 0:4], P), ALU.mult)
                        fence()
                        tt(tmp, tmp, ha[:, :, 0:P], ALU.add).then_inc(y_sum, 1)
                    fence()
                elif kind == "ml_gain":
                    t = step[1]
                    dve.wait_ge(y_rstd, l * 9 + (2 * TT + t + 1))
                    if t == 0:
                        dve.wait_ge(o_sigmoid, l + 1)
                    for h in range(HEADS):
                        stt(TMP[:, tile(h)], TMP[:, tile(h)], ST4[:, 0, h:h + 1], row("ml_g")[:, tile(h)], ALU.mult, ALU.mult)
                    fence()
                    tt(YTILE[:, (2 * TT + t) % 2, :], TMP[:, :], MO[:, t, :], ALU.mult).then_inc(y_ready, 1)
                    fence()
                elif kind == "out":
                    d = step[1]
                    u = use(here, step)
                    dve.wait_ge(u.filled, u.after)
                    for v, a, b in SEGS:
                        last = stt(XT[:, d, a:b], u.t[:, a:b], MOD[:, 2, d, v:v + 1], XT[:, d, a:b], ALU.mult, ALU.add)
                    last.then_inc(u.drained, 1)
                elif kind == "rank":
                    rank(use(here, step), step[1], 0)
                elif kind == "pick":
                    pick()
                elif kind == "router_fold":
                    u = use(here, step)
                    dve.wait_ge(u.filled, u.after)
                    logits = u.t[:, 0:TT * EXPERTS].rearrange("p (t e) -> p t e", t=TT)
                    ve.tensor_reduce(R3[:, 0:3], logits, AX.X, ALU.max)
                    fence()
                    tt(AFF[:, :, 0:EXPERTS], logits, over(R3[:, 0:3], EXPERTS), ALU.subtract).then_inc(u.drained, 1)
                    ve.memset(AFF[:, :, EXPERTS:EXPERTS + GE], 0.0)
                    dve.wait_ge(aff_exp, l + 1)
                    ve.tensor_reduce(R3[:, 3:6], AFF[:, :, 0:EXPERTS], AX.X, ALU.add)
                    fence()
                    ve.reciprocal(R3[:, 0:3], R3[:, 3:6])
                    fence()
                    tt(AFF[:, :, 0:EXPERTS], AFF[:, :, 0:EXPERTS], over(R3[:, 0:3], EXPERTS), ALU.mult)
                    fence()

            def rank(u, j, group):
                if j == 0:
                    at = slice(0, GE) if isinstance(group, int) else bass.ds(group * GE, GE)
                    ve.tensor_copy(AG[:, :, :], AFF[:, :, at]).then_inc(ag_ready, 1)
                    fence()
                dve.wait_ge(u.filled, u.after)
                scratch = YTILE.rearrange("p a b -> p (a b)")
                tiles = []
                for t in range(TT):
                    a, b = (P, N) if t else (0, P)
                    first = before_at + {0: 1, 1: 1, 2: 0}[t] * P
                    at = {0: 0, 1: P, 2: N}[t]
                    tiles.append((u.t[:, a:b], AG[:, t, j:j + 1], CT[:, first:first + b - a], RK[:, t * GE + j:t * GE + j + 1],
                                  scratch[:, at:at + b - a]))
                for rows, own, mask, rank, tmp in tiles:
                    stt(tmp, rows, own, mask, ALU.is_equal, ALU.mult)
                fence()
                for rows, own, mask, rank, tmp in tiles:
                    last = stt(tmp, rows, own, tmp, ALU.is_gt, ALU.add, accum_out=rank)
                last.then_inc(u.drained, 1)

            def pick():
                def places(x, t, n):
                    return x[:, t:t + n, :].rearrange("p t (e c) -> p t e c", c=CAP_S)

                def per_expert(x, t, n):
                    return x[:, t:t + n, :].unsqueeze(3).to_broadcast([P, n, GE, CAP_S])

                ranks = RK.rearrange("p (t e) -> p t e", e=GE)
                parts = ((1, 2, const("slot_s")), (0, 1, const("slot_c")))
                for t, n, slots in parts:
                    slots = slots.unsqueeze(1).unsqueeze(1).to_broadcast([P, n, GE, CAP_S])
                    last = tt(places(PO, t, n), slots, per_expert(ranks, t, n), ALU.is_equal)
                last.then_inc(picked, 1)
                fence()
                for t, n, _ in parts:
                    last = tt(places(GO, t, n), places(PO, t, n), per_expert(AG, t, n), ALU.mult)
                last.then_inc(weighted, 1)

            def group_step(l, g, step):
                kind = step[0]
                if kind == "next_rank":
                    rank(use(here, step), step[1], g + 1)
                elif kind == "next_pick":
                    for x in [use(here, ("gather", a)) for a in (2, 3)] + [use(here, ("g_turn",))]:
                        dve.wait_ge(x.filled, x.after)
                    pick()
                elif kind == "up":
                    j, half = step[1:]
                    gate, up = use(here, step, 0), use(here, step, 1)
                    dve.wait_ge(hid_sigmoid, l * (GROUPS * GE * 2) + g * (GE * 2) + (j * 2 + half + 1))
                    tt(SGE[:, half, :], SGE[:, half, :], gate.t[:, 0:256], ALU.mult).then_inc(gate.drained, 1)
                    fence()
                    dve.wait_ge(up.filled, up.after)
                    tt(HH[:, half, :], SGE[:, half, :], up.t[:, 0:256], ALU.mult).then_inc(up.drained, 1)
                elif kind == "scatter":
                    d = step[1]
                    u = use(here, step)
                    dve.wait_ge(u.filled, u.after)
                    for v, a, b in SEGS:
                        last = stt(XT[:, d, a:b], u.t[:, a:b], MOD[:, 5, d, v:v + 1], XT[:, d, a:b], ALU.mult, ALU.add)
                    last.then_inc(u.drained, 1)
                    if d == KT - 1:
                        fence()
                        ve.tensor_copy(R3[:, 0:1], R3[:, 0:1]).then_inc(layer_done, 1)

            ve.memset(CSIG[:, :, :], 0.0)
            fence()
            dve.wait_ge(c_sigmoid, 1)
            tt(CSIG[:, :, 0:2], LAM[:, 0:2 * KT].rearrange("p (k v) -> p k v", v=2), CVEC[:, :, :], ALU.mult).then_inc(c_ready, 1)
            with dve.Fori(0, DEPTH) as l:
                here.layer, here.part = l, "layer"
                for step in LATE_STEPS:
                    mixer_step(l, step)
                    if step[0] in DVE_STEPS:
                        fence()
                with dve.Fori(0, GROUPS) as g:
                    here.group, here.part = g, "group"
                    for step in GROUP_STEPS:
                        group_step(l, g, step)
                        if step[0] in DVE_STEPS:
                            fence()
            here.part = "end"
            norm(DEPTH, 0, 2, None)


_WEIGHTS = ["ada_w", "w_in", "w_branch", "w_mgate", "w_out", "ex_w_gate", "ex_w_up", "ex_w_down"]
_OUTS = {
    "k_out": (DEPTH, P, HEADS, P), "v_out": (DEPTH, P, 512), "ssm_out": (DEPTH, 2, P, 256),
    "c_out": (DEPTH, P, 2, 2, P + 1), "m_out": (DEPTH, 8), "y_out": (P, KT, N),
}


def _columns(a, parts):
    return np.ascontiguousarray(a.reshape(parts, P).T)


def kernel(**inputs):
    import numpy as _np
    import concourse.bacc as _bacc
    from concourse.bass_utils import run_bass_kernel_spmd as _run

    a = {k: _np.asarray(v) for k, v in inputs.items()}
    arrays = {k: _np.ascontiguousarray(a[k]) for k in _WEIGHTS}
    arrays["constants"] = CONSTANTS
    x = _np.concatenate([a["x_prompt"][0], a["x_sample"][0]], axis=0)
    arrays["x_t"] = _np.ascontiguousarray(x.reshape(N, KT, P).transpose(2, 1, 0))
    arrays["c_t"] = _np.stack([_columns(a["c_ctx"], KT), _columns(a["c"][0], KT)], axis=2)
    rows, cols = [], []
    for l in range(DEPTH):
        lam_init = 0.8 - 0.6 * math.exp(-0.3 * l)
        rows.append(_np.concatenate([
            a["mb_dt_bias"][l].reshape(-1), a["mb_a_log"][l].reshape(-1), a["mb_d"][l], a["ml_gate_b"][l].reshape(-1),
            a["state_mlstm_m"][0, l].reshape(-1), a["da_lambda"][l].reshape(-1), a["da_subln_g"][l],
            a["mb_norm_g"][l], a["ml_norm_g"][l].reshape(-1),
            _np.array([lam_init, 1.0 - lam_init], _np.float32)]))
        cols.append(_np.concatenate([
            _columns(a["ada_b"][l], 48), _columns(a["norm1_g"][l], KT), _columns(a["norm2_g"][l], KT),
            _columns(a["b_mgate"][l], 24), _columns(a["mb_conv_w"][l].reshape(-1), 18), _columns(a["mb_conv_b"][l], 6),
            a["router_w"][l].reshape(KT, P, EXPERTS).transpose(1, 0, 2).reshape(P, KT * EXPERTS),
            _columns(a["final_g"], KT)], axis=1))
    arrays["rows"], arrays["cols"] = _np.stack(rows), _np.stack(cols)
    arrays["cache_k_t"] = _np.ascontiguousarray(
        a["cache_k"][0].reshape(DEPTH, P, HEADS, 2 * 64).transpose(0, 3, 2, 1))
    arrays["cache_v"] = _np.ascontiguousarray(a["cache_v"][0].reshape(DEPTH, P, 512))
    arrays["ssm_t"] = _np.ascontiguousarray(
        a["state_ssm"][0].reshape(DEPTH, 2, 2, 4, 64, 64).transpose(0, 1, 2, 5, 3, 4).reshape(DEPTH, 2, P, 256))
    cn = _np.concatenate([a["state_mlstm_c"][0], a["state_mlstm_n"][0][..., None]], axis=-1)
    arrays["c_t0"] = _np.ascontiguousarray(
        cn.reshape(DEPTH, 2, 2, 2, 64, P + 1).transpose(0, 3, 4, 1, 2, 5).reshape(DEPTH, P, 2, 2, P + 1))

    nc = _bacc.Bacc("TRN2", target_bir_lowering=False, num_devices=1)
    aps = {k: nc.dram_tensor(k, v.shape, F, kind="ExternalInput").ap() for k, v in arrays.items()}
    aps.update({k: nc.dram_tensor(k, s, F, kind="ExternalOutput").ap() for k, s in _OUTS.items()})
    build(nc, aps)
    r = _run(nc, [arrays], core_ids=[0]).results[0]

    y = r["y_out"].transpose(2, 1, 0).reshape(N, D)
    k = r["k_out"].transpose(0, 3, 2, 1).reshape(1, DEPTH, P, HEADS, 2, 64)
    v = r["v_out"].reshape(1, DEPTH, P, HEADS, 2 * 64)
    ssm = r["ssm_out"].reshape(DEPTH, 2, 2, 64, 4, 64).transpose(0, 1, 2, 4, 5, 3).reshape(1, DEPTH, 2, 8, 64, 64)
    c = r["c_out"].reshape(DEPTH, 2, 64, 2, 2, P + 1).transpose(0, 3, 4, 1, 2, 5).reshape(1, DEPTH, 2, HEADS, 64, P + 1)
    m = r["m_out"].reshape(1, DEPTH, 2, HEADS)
    return (y[None, :P], y[None, P:], k, v, ssm, c[..., :P], c[..., P], m)
```
